# Optimizing a Trainium2 kernel written in Bass

```python
import math
import jax, jax.numpy as jnp
from jax import lax
import numpy as np

D_MODEL = 2048
BATCH = 1
SEQ = 256
DEPTH = 2

HEAD_DIM = 128
Q_BLOCK = 128
NORM_EPS = 1e-6
FOX_HEADS = 8
FOX_W = FOX_HEADS * HEAD_DIM
DIFF_HEADS = 4
DIFF_V_DIM = 2 * HEAD_DIM
DIFF_QK_W = DIFF_HEADS * 2 * HEAD_DIM
DIFF_V_W = DIFF_HEADS * DIFF_V_DIM
MLA_HEADS = 8
MLA_Q_RANK = 512
MLA_KV_RANK = 512
MLA_NOPE = 128
MLA_ROPE = 64
MLA_V = 128
ROPE_THETA = 10000.0
MOBA_HEADS = 8
MOBA_W = MOBA_HEADS * HEAD_DIM
MOBA_BLOCK = 256
MOBA_TOPK = 3
MOBA_Q_CHUNK = 16
MEM_LEN = 256
XATTN_HEADS = 4
XATTN_DIM = 128
XATTN_W = XATTN_HEADS * XATTN_DIM
FFN_DIM = 4 * D_MODEL
AB_IN = 3 * FOX_W + FOX_HEADS + 2 * DIFF_QK_W + DIFF_V_W
AB_OUT = FOX_W + DIFF_V_W
CD_IN = MLA_Q_RANK + MLA_KV_RANK + MLA_ROPE + 3 * MOBA_W
CD_OUT = MLA_HEADS * MLA_V + MOBA_W
N_EVEN = (DEPTH + 1) // 2
N_ODD = DEPTH // 2

kernel_name = 'hybrid_fox_diff_mla_moba_trunk'

def rmsnorm(x, g):
    xf = x.astype(jnp.float32)
    y = xf * lax.rsqrt(jnp.mean(xf * xf, axis=-1, keepdims=True) + NORM_EPS)
    return (y * g.astype(jnp.float32)).astype(x.dtype)

def split_heads(t, n_heads):
    b, s, _ = t.shape
    return t.reshape(b, s, n_heads, -1).transpose(0, 2, 1, 3)

def merge_heads(t):
    b, h, s, d = t.shape
    return t.transpose(0, 2, 1, 3).reshape(b, s, h * d)

def alibi_slopes(n):
    return jnp.asarray([2.0 ** (-8.0 * (i + 1) / n) for i in range(n)], dtype=jnp.float32)

def alibi_bias(slopes):
    def fn(q0, q1):
        dist = jnp.abs(jnp.arange(q0, q1)[:, None] - jnp.arange(q1)[None, :]).astype(jnp.float32)
        return -slopes[None, :, None, None] * dist[None, None]
    return fn

def blocked_causal_attention(q, k, v, scale, bias_fn=None):
    s = q.shape[2]
    neg = jnp.finfo(jnp.float32).min
    outs = []
    for i in range(s // Q_BLOCK):
        q0, q1 = i * Q_BLOCK, (i + 1) * Q_BLOCK
        logits = jnp.einsum('bhqd,bhkd->bhqk', q[:, :, q0:q1], k[:, :, :q1]).astype(jnp.float32) * scale
        if bias_fn is not None:
            logits = logits + bias_fn(q0, q1)
        causal = jnp.arange(q1)[None, :] <= jnp.arange(q0, q1)[:, None]
        p = jax.nn.softmax(jnp.where(causal, logits, neg), axis=-1).astype(v.dtype)
        outs.append(jnp.einsum('bhqk,bhkd->bhqd', p, v[:, :, :q1]))
    return jnp.concatenate(outs, axis=2)

def rope_tables(s):
    inv = ROPE_THETA ** (-jnp.arange(0, MLA_ROPE, 2, dtype=jnp.float32) / MLA_ROPE)
    ang = jnp.arange(s, dtype=jnp.float32)[:, None] * inv[None, :]
    return jnp.cos(ang), jnp.sin(ang)

def apply_rope(t, cos, sin):
    half = t.shape[-1] // 2
    t1, t2 = t[..., :half], t[..., half:]
    c, s_ = cos.astype(t.dtype), sin.astype(t.dtype)
    return jnp.concatenate([t1 * c - t2 * s_, t2 * c + t1 * s_], axis=-1)

def moba_attention(q, k, v, slopes):
    b, h, s, dh = q.shape
    nblk = -(-s // MOBA_BLOCK)
    pad = nblk * MOBA_BLOCK - s
    kp = jnp.pad(k, ((0, 0), (0, 0), (0, pad), (0, 0))).reshape(b, h, nblk, MOBA_BLOCK, dh)
    vp = jnp.pad(v, ((0, 0), (0, 0), (0, pad), (0, 0))).reshape(b, h, nblk, MOBA_BLOCK, dh)
    kmean = jnp.mean(kp.astype(jnp.float32), axis=3)
    gate = jnp.einsum('bhsd,bhnd->bhsn', q.astype(jnp.float32), kmean)
    tpos = jnp.arange(s)
    own = tpos // MOBA_BLOCK
    past = jnp.arange(nblk)[None, :] < own[:, None]
    gate = jnp.where(past[None, None], gate, -jnp.inf)
    k_sel = min(MOBA_TOPK, nblk)
    top_val, top_idx = lax.top_k(gate, k_sel)
    own_b = jnp.broadcast_to(own[None, None, :, None], (b, h, s, 1)).astype(top_idx.dtype)
    idx = jnp.concatenate([top_idx, own_b], axis=-1)
    valid = jnp.concatenate([jnp.isfinite(top_val), jnp.ones((b, h, s, 1), dtype=bool)], axis=-1)
    nc = s // MOBA_Q_CHUNK

    def chunk_view(t):
        return jnp.moveaxis(t.reshape(b, h, nc, MOBA_Q_CHUNK, *t.shape[3:]), 2, 0)

    bi = jnp.arange(b)[:, None, None, None]
    hi = jnp.arange(h)[None, :, None, None]
    slopes_b = slopes[None, :, None, None, None]
    scale = dh ** -0.5
    neg = jnp.finfo(jnp.float32).min

    def one_chunk(args):
        qc, ic, vc, pc = args
        kg = kp[bi, hi, ic]
        vg = vp[bi, hi, ic]
        kpos = ic[..., None] * MOBA_BLOCK + jnp.arange(MOBA_BLOCK)
        qpos = pc[None, None, :, None, None]
        dist = jnp.abs(qpos - kpos).astype(jnp.float32)
        logits = jnp.einsum('bhcd,bhcjpd->bhcjp', qc, kg).astype(jnp.float32) * scale - slopes_b * dist
        mask = vc[..., None] & (kpos <= qpos)
        logits = jnp.where(mask, logits, neg)
        shp = logits.shape
        p = jax.nn.softmax(logits.reshape(shp[0], shp[1], shp[2], -1), axis=-1).reshape(shp).astype(vg.dtype)
        return jnp.einsum('bhcjp,bhcjpd->bhcd', p, vg)

    out = lax.map(one_chunk, (chunk_view(q), chunk_view(idx), chunk_view(valid), tpos.reshape(nc, MOBA_Q_CHUNK)))
    return jnp.moveaxis(out, 0, 2).reshape(b, h, s, dh)

def mixer_fox_diff(u, w_in, w_out, b_f, lam, subln, layer_idx):
    b, s, _ = u.shape
    sizes = [FOX_W, FOX_W, FOX_W, FOX_HEADS, DIFF_QK_W, DIFF_QK_W, DIFF_V_W]
    fq, fk, fv, fg, dq, dk, dv = jnp.split(u @ w_in, np.cumsum(sizes)[:-1].tolist(), axis=-1)
    logf = jax.nn.log_sigmoid(fg.astype(jnp.float32) + b_f.astype(jnp.float32))
    cum = jnp.cumsum(logf, axis=1).transpose(0, 2, 1)
    fox_bias = lambda q0, q1: cum[:, :, q0:q1, None] - cum[:, :, None, :q1]
    a = blocked_causal_attention(split_heads(fq, FOX_HEADS), split_heads(fk, FOX_HEADS),
                                 split_heads(fv, FOX_HEADS), HEAD_DIM ** -0.5, fox_bias)
    qd = dq.reshape(b, s, DIFF_HEADS, 2, HEAD_DIM).transpose(0, 3, 2, 1, 4).reshape(b, 2 * DIFF_HEADS, s, HEAD_DIM)
    kd = dk.reshape(b, s, DIFF_HEADS, 2, HEAD_DIM).transpose(0, 3, 2, 1, 4).reshape(b, 2 * DIFF_HEADS, s, HEAD_DIM)
    vd = split_heads(dv, DIFF_HEADS)
    od = blocked_causal_attention(qd, kd, jnp.concatenate([vd, vd], axis=1), HEAD_DIM ** -0.5,
                                  alibi_bias(jnp.tile(alibi_slopes(DIFF_HEADS), 2)))
    od = od.reshape(b, 2, DIFF_HEADS, s, DIFF_V_DIM)
    lam_init = 0.8 - 0.6 * math.exp(-0.3 * layer_idx)
    lf = lam.astype(jnp.float32)
    lam_full = jnp.exp(jnp.sum(lf[0] * lf[1])) - jnp.exp(jnp.sum(lf[2] * lf[3])) + lam_init
    d = od[:, 0] - lam_full.astype(od.dtype) * od[:, 1]
    d = rmsnorm(d, subln) * (1.0 - lam_init)
    return jnp.concatenate([merge_heads(a), merge_heads(d)], axis=-1) @ w_out

def mixer_mla_moba(u, w_in, w_out, q_norm, kv_norm, w_uq, w_ukv, cos, sin):
    b, s, _ = u.shape
    sizes = [MLA_Q_RANK, MLA_KV_RANK, MLA_ROPE, MOBA_W, MOBA_W, MOBA_W]
    cq, ckv, kpe, mq, mk, mv = jnp.split(u @ w_in, np.cumsum(sizes)[:-1].tolist(), axis=-1)
    q = (rmsnorm(cq, q_norm) @ w_uq).reshape(b, s, MLA_HEADS, MLA_NOPE + MLA_ROPE).transpose(0, 2, 1, 3)
    kv = (rmsnorm(ckv, kv_norm) @ w_ukv).reshape(b, s, MLA_HEADS, MLA_NOPE + MLA_V).transpose(0, 2, 1, 3)
    q_pe = apply_rope(q[..., MLA_NOPE:], cos, sin)
    k_pe = apply_rope(kpe[:, None], cos, sin)
    qf = jnp.concatenate([q[..., :MLA_NOPE], q_pe], axis=-1)
    kf = jnp.concatenate([kv[..., :MLA_NOPE], jnp.broadcast_to(k_pe, (b, MLA_HEADS, s, MLA_ROPE))], axis=-1)
    c = blocked_causal_attention(qf, kf, kv[..., MLA_NOPE:], (MLA_NOPE + MLA_ROPE) ** -0.5)
    dout = moba_attention(split_heads(mq, MOBA_HEADS), split_heads(mk, MOBA_HEADS),
                          split_heads(mv, MOBA_HEADS), alibi_slopes(MOBA_HEADS))
    return jnp.concatenate([merge_heads(c), merge_heads(dout)], axis=-1) @ w_out

def memory_attention(u, wq, wo, mem_k, mem_v):
    q = split_heads(u @ wq, XATTN_HEADS)
    logits = jnp.einsum('bhsd,bhmd->bhsm', q, mem_k).astype(jnp.float32) * XATTN_DIM ** -0.5
    p = jax.nn.softmax(logits, axis=-1).astype(mem_v.dtype)
    return merge_heads(jnp.einsum('bhsm,bhmd->bhsd', p, mem_v)) @ wo

def squared_relu_mlp(u, w1, w2):
    return jnp.square(jax.nn.relu(u @ w1)) @ w2

def setup_inputs(seed: int = 0) -> dict:
    key = jax.random.key(seed)
    ks = jax.random.split(key, 20)
    nrm = lambda k, shp, sc: jax.random.normal(k, shp, jnp.float32) * sc
    gain = lambda k, shp: 1.0 + 0.02 * jax.random.normal(k, shp, jnp.float32)
    return {
        'x': nrm(ks[0], (BATCH, SEQ, D_MODEL), 1.0),
        'mem': nrm(ks[1], (BATCH, MEM_LEN, D_MODEL), 1.0),
        'mem_norm': gain(ks[2], (D_MODEL,)),
        'mem_wkv': nrm(ks[3], (D_MODEL, 2 * XATTN_W), D_MODEL ** -0.5),
        'norms': gain(ks[4], (DEPTH, 6, D_MODEL)),
        'xattn_wq': nrm(ks[5], (DEPTH, D_MODEL, XATTN_W), D_MODEL ** -0.5),
        'xattn_wo': nrm(ks[6], (DEPTH, XATTN_W, D_MODEL), XATTN_W ** -0.5),
        'ffn_w1': nrm(ks[7], (DEPTH, D_MODEL, FFN_DIM), D_MODEL ** -0.5),
        'ffn_w2': nrm(ks[8], (DEPTH, FFN_DIM, D_MODEL), FFN_DIM ** -0.5),
        'ab_w_in': nrm(ks[9], (N_EVEN, D_MODEL, AB_IN), D_MODEL ** -0.5),
        'ab_w_out': nrm(ks[10], (N_EVEN, AB_OUT, D_MODEL), AB_OUT ** -0.5),
        'fox_b_f': 2.0 + 0.1 * jax.random.normal(ks[11], (N_EVEN, FOX_HEADS), jnp.float32),
        'diff_lambda': nrm(ks[12], (N_EVEN, 4, HEAD_DIM), 0.1),
        'diff_subln': gain(ks[13], (N_EVEN, DIFF_V_DIM)),
        'cd_w_in': nrm(ks[14], (N_ODD, D_MODEL, CD_IN), D_MODEL ** -0.5),
        'cd_w_out': nrm(ks[15], (N_ODD, CD_OUT, D_MODEL), CD_OUT ** -0.5),
        'mla_q_norm': gain(ks[16], (N_ODD, MLA_Q_RANK)),
        'mla_kv_norm': gain(ks[17], (N_ODD, MLA_KV_RANK)),
        'mla_w_uq': nrm(ks[18], (N_ODD, MLA_Q_RANK, MLA_HEADS * (MLA_NOPE + MLA_ROPE)), MLA_Q_RANK ** -0.5),
        'mla_w_ukv': nrm(ks[19], (N_ODD, MLA_KV_RANK, MLA_HEADS * (MLA_NOPE + MLA_V)), MLA_KV_RANK ** -0.5),
    }

def reference(x, mem, mem_norm, mem_wkv, norms, xattn_wq, xattn_wo, ffn_w1, ffn_w2,
              ab_w_in, ab_w_out, fox_b_f, diff_lambda, diff_subln,
              cd_w_in, cd_w_out, mla_q_norm, mla_kv_norm, mla_w_uq, mla_w_ukv):
    s = x.shape[1]
    cos, sin = rope_tables(s)
    mkv = rmsnorm(mem, mem_norm) @ mem_wkv
    mem_k = split_heads(mkv[..., :XATTN_W], XATTN_HEADS)
    mem_v = split_heads(mkv[..., XATTN_W:], XATTN_HEADS)
    h = x
    for i in range(DEPTH):
        n = norms[i]
        j = i // 2
        u = rmsnorm(h, n[0])
        if i % 2 == 0:
            u = mixer_fox_diff(u, ab_w_in[j], ab_w_out[j], fox_b_f[j], diff_lambda[j], diff_subln[j], i)
        else:
            u = mixer_mla_moba(u, cd_w_in[j], cd_w_out[j], mla_q_norm[j], mla_kv_norm[j],
                               mla_w_uq[j], mla_w_ukv[j], cos, sin)
        h = h + rmsnorm(u, n[1])
        h = h + rmsnorm(memory_attention(rmsnorm(h, n[2]), xattn_wq[i], xattn_wo[i], mem_k, mem_v), n[3])
        h = h + rmsnorm(squared_relu_mlp(rmsnorm(h, n[4]), ffn_w1[i], ffn_w2[i]), n[5])
    return h


_drawn_inputs = setup_inputs


def setup_inputs(seed=0):
    import zlib

    import numpy as np

    out = dict(_drawn_inputs(seed))
    spreads = {}
    factors = {'fox_b_f': 27.16, 'diff_subln': 4.027, 'mla_q_norm': 8.0, 'mla_kv_norm': 8.0}
    for name, (base, spread) in spreads.items():
        noise = np.random.default_rng([zlib.crc32(name.encode()), seed]).standard_normal(out[name].shape)
        drawn = base * np.exp(spread * noise) if base else spread * noise
        out[name] = __import__('jax').numpy.asarray(drawn.astype(out[name].dtype))
    for name, factor in factors.items():
        out[name] = (out[name] * factor).astype(out[name].dtype)
    return out
```

```python
from contextlib import ExitStack
import math

import numpy as np

import concourse.bass as bass
from concourse import mybir

F32 = mybir.dt.float32
F32R = mybir.dt.float32r
ALU = mybir.AluOpType
ACT = mybir.ActivationFunctionType
AX_X = mybir.AxisListType.X

P = 128
SEQ = 256
HALVES = SEQ // P
D = 2048
CH = D // P
FFN = 4 * D
BLOCKS = FFN // 1024
EPS = 1e-6
HD = 128
FOX_W = 1024
DIFF_HEADS = 4
MLA_ROPE = 64
MLA_QK = HD + MLA_ROPE
MEM_LEN = 256
XW = 512
SCALE = HD ** -0.5
MLA_SCALE = MLA_QK ** -0.5
LAM_INIT = 0.8 - 0.6 * math.exp(0.0)
MASKED = -1e36

RAW = 4
RING = 4
TILE = 1024
LEAD = 3

C_ID, C_TRI, C_ONE, C_DIST, C_MASK, C_COS, C_SIN, C_END = np.cumsum([0, 128, 128, 128, 384, 384, 64, 64]).tolist()

GROUPS = [
    ("mem", 16, 1, 1024),
    ("fg", 16, 8, 8), ("fv", 16, 1, 1024), ("fq", 16, 1, 1024), ("fk", 16, 1, 1024),
    ("dq", 16, 1, 1024), ("dk", 16, 1, 1024), ("dv", 16, 1, 1024),
    ("abo0", 16, 1, 1024), ("abo1", 16, 1, 1024),
    ("xq0", 16, 2, 512), ("xo00", 4, 1, 1024), ("xo01", 4, 1, 1024),
    ("ffn0", None, None, None),
    ("kpe", 16, 8, 64), ("cqkv", 16, 1, 1024), ("mq", 16, 1, 1024),
    ("uq0", 4, 1, 768), ("uq1", 4, 1, 768), ("ukv0", 4, 1, 1024), ("ukv1", 4, 1, 1024),
    ("mk", 16, 1, 1024), ("mv", 16, 1, 1024),
    ("cdo0", 16, 1, 1024), ("cdo1", 16, 1, 1024),
    ("xq1", 16, 2, 512), ("xo10", 4, 1, 1024), ("xo11", 4, 1, 1024),
    ("ffn1", None, None, None),
]
FFN_GROUPS = 3 * BLOCKS
FFN_TILES = BLOCKS * (16 + 2 * 8)


def col_banks(width):
    n = -(-width // 512)
    return [(c * (width // n), width // n) for c in range(n)]


def plan_groups():
    plan, index, tile, act, dve = {}, 0, 0, 0, 0
    for name, chunks, per, width in GROUPS:
        plan[name] = dict(index=index, tile=tile, chunks=chunks, per=per, width=width, act=act, dve=dve)
        if chunks is None:
            index, tile = index + FFN_GROUPS, tile + FFN_TILES
            act, dve = act + 2 * BLOCKS, dve + (2 + 8) * BLOCKS
        else:
            n = len(col_banks(width))
            plan[name].update(tiles=chunks // per, banks=n)
            index, tile, act, dve = index + 1, tile + chunks // per, act + n, dve + n
    return plan


def running(items):
    at, out = 0, {}
    for name, n in items:
        out[name] = at
        at += n
    return out


PLAN = plan_groups()
SPLITS = running([("mem", 8), ("a0", 8), ("o0a", 4), ("o0b", 4), ("x0", 8), ("xo0", 2), ("f0", 8), ("h0", 4 * BLOCKS),
                  ("a1", 8), ("c1", 4), ("o1a", 4), ("o1b", 4), ("x1", 8), ("xo1", 2), ("f1", 8), ("h1", 4 * BLOCKS)])
TURN_BANKS = [("gain", 1), ("mem_k", 2), ("cum", 1), ("fq", 4), ("fk", 4), ("dq", 4), ("dk", 4), ("xq0", 2),
              ("kpe", 1), ("mq", 4), ("kn0", 2), ("kn1", 2), ("qn", 4), ("qpe", 2), ("mk", 4), ("xq1", 2)]
TURNS = running(TURN_BANKS)


def turned_by(name):
    n = dict(TURN_BANKS)[name]
    return (n // 2, n - n // 2)


TURNED_ACT = running([(n, turned_by(n)[0]) for n, _ in TURN_BANKS])
TURNED_DVE = running([(n, turned_by(n)[1]) for n, _ in TURN_BANKS])
UNITS = running([("fox", 8), ("diff", 8), ("x0", 4), ("mla", 8), ("moba", 8), ("x1", 4)])
NORMS = running([(n, 1) for n in ("mem", "a0", "sub", "pa0", "x0", "px0", "f0", "pf0",
                                  "a1", "c1", "pa1", "x1", "px1", "f1", "pf1")])
SCALED_ACT = running([(n, int(n != "sub")) for n in ("mem", "a0", "sub", "x0", "f0", "a1", "c1", "x1", "f1")])
SCALED_DVE = running([(n, 1) for n in ("mem", "a0", "sub", "x0", "f0", "a1", "c1", "x1", "f1")])
GAIN_COL = {"mem": 0, "a0": 16, "x0": 32, "f0": 48, "a1": 64, "x1": 80, "f1": 96, "q": 112, "kv": 116}
POST = {"pa0": (0, 1), "px0": (0, 3), "pf0": (0, 5), "pa1": (1, 1), "px1": (1, 3), "pf1": (1, 5)}
POST_AT = {n: i for i, n in enumerate(POST)}
BEFORE = {"x0": "pa0", "f0": "px0", "a1": "pf0", "x1": "pa1", "f1": "px1"}
SMALL_LOADS = 12
FOX_FIRST, MLA_FIRST = 5, 2
NEXT_GROUP = {"mem": "mem", "a0": "fg", "x0": "xq0", "f0": "ffn0", "a1": "kpe", "x1": "xq1", "f1": "ffn1"}


def norm_bank(name, c):
    return (4 * (PLAN[NEXT_GROUP[name]]["index"] % 2) + c // 2) % 8


def at(i, per, static):
    return static if i is None else i * per + static


class Mlp:
    TILES, SPLITS, ACT, DVE = 64, 8, 4, 20

    def __init__(self, l):
        g = PLAN[f"ffn{l}"]
        self.l, self.g, self.t, self.a, self.v, self.s = l, g["index"], g["tile"], g["act"], g["dve"], SPLITS[f"h{l}"]

    def up(self, b):
        return (self.g + b, self.t + 16 * b) if b < 2 else (self.g + 3 * b - 2, self.t + 32 * b - 16)

    def down(self, b, half):
        if b == 0:
            return self.g + 2 + half, self.t + 32 + 8 * half
        if b == BLOCKS - 1:
            return self.g + 3 * b + 1 + half, self.t + 32 * b + 16 + 8 * half
        return self.g + 3 * b + 2 + half, self.t + 32 * b + 32 + 8 * half

    def hid_dve(self, b):
        return self.v + (0 if b == 0 else 10 * b - 8)

    def y_dve(self, b, half):
        return self.v + (10 * b + 4 if b < BLOCKS - 1 else 10 * b + 2) + 4 * half


def trunk(nc, x, mem, mem_norm, mem_wkv, norms, xattn_wq, xattn_wo, ffn_w1, ffn_w2, ab_w_in, ab_w_out,
          fox_b_f, diff_lambda, diff_subln, cd_w_in, cd_w_out, mla_q_norm, mla_kv_norm, mla_w_uq, mla_w_ukv,
          consts, out):
    AB, CD = ab_w_in[0], cd_w_in[0]
    weights = {
        "mem": (mem_wkv, 0),
        "fq": (AB, 0), "fk": (AB, 1024), "fv": (AB, 2048), "fg": (AB, 3072),
        "dq": (AB, 3080), "dk": (AB, 4104), "dv": (AB, 5128),
        "abo0": (ab_w_out[0], 0), "abo1": (ab_w_out[0], 1024),
        "kpe": (CD, 1024), "cqkv": (CD, 0), "mq": (CD, 1088), "mk": (CD, 2112), "mv": (CD, 3136),
        "uq0": (mla_w_uq[0], 0), "uq1": (mla_w_uq[0], 768), "ukv0": (mla_w_ukv[0], 0), "ukv1": (mla_w_ukv[0], 1024),
        "cdo0": (cd_w_out[0], 0), "cdo1": (cd_w_out[0], 1024),
    }
    for l in range(2):
        weights |= {f"xq{l}": (xattn_wq[l], 0), f"xo{l}0": (xattn_wo[l], 0), f"xo{l}1": (xattn_wo[l], 1024)}

    with ExitStack() as ctx:
        def sb(name, shape, dt=F32, own=ctx):
            return own.enter_context(nc.sbuf_tensor(name, shape, dt))

        def sem(name):
            return ctx.enter_context(nc.semaphore(name))

        PS = ctx.enter_context(nc.psum_tensor("PS", [P, 8, 512], F32))
        resid = sb("resid", [P, HALVES, D])
        x_hi = sb("x_hi", [P, CH, SEQ], F32R)
        x_lo = sb("x_lo", [P, CH, SEQ], F32R)
        rows = sb("rows", [P, HALVES, D])
        raw = sb("raw", [P, RAW, 2 * TILE])
        w_hi = sb("w_hi", [P, RING, TILE], F32R)
        w_lo = sb("w_lo", [P, RING, TILE], F32R)
        const = sb("const", [P, C_END])
        mem_kT = sb("mem_kT", [P, 4, MEM_LEN])
        mem_v = sb("mem_v", [P, HALVES, XW])
        gain_rows = sb("gain_rows", [120, P])
        gain_col = sb("gain_col", [P, 120])
        small = sb("small", [P, 160])
        subln = sb("subln", [P, 2 * HD])
        with ExitStack() as mixer:
            qT_a = sb("qT_a", [P, 8, SEQ], own=mixer)
            kT_a = sb("kT_a", [P, 8, SEQ], own=mixer)
            v_a = sb("v_a", [P, HALVES, 1024], own=mixer)
            qT_b = sb("qT_b", [P, 8, SEQ], own=mixer)
            kT_b = sb("kT_b", [P, 8, SEQ], own=mixer)
            v_b = sb("v_b", [P, HALVES, 1024], own=mixer)
            logit = sb("logit", [P, 2, 512], own=mixer)
            prob = sb("prob", [P, 2, 512], own=mixer)
            qpeT = sb("qpeT", [P, 4, SEQ], own=mixer)
            kpeT = sb("kpeT", [P, SEQ], own=mixer)
        with ExitStack() as low_rank:
            sb("gap_q", [P, 4, 8 * SEQ], own=low_rank)
            c_hi = sb("c_hi", [P, 8, SEQ], F32R, own=low_rank)
            c_lo = sb("c_lo", [P, 8, SEQ], F32R, own=low_rank)
        with ExitStack() as mlp:
            gain_row = sb("gain_row", [P, D], own=mlp)
            y_acc = sb("y_acc", [P, HALVES, D], own=mlp)
            h_hi = [sb(f"h_hi{i}", [P, 8, SEQ], F32R, own=mlp) for i in range(2)]
            h_lo = [sb(f"h_lo{i}", [P, 8, SEQ], F32R, own=mlp) for i in range(2)]
        sb("mixer_region", [P, 6 * 8 * SEQ + 2 * 1024 + 5 * SEQ])

        ident = const[:, C_ID:C_TRI]
        tri = const[:, C_TRI:C_ONE]
        ones = const[:, C_ONE:C_DIST]
        dist = const[:, C_DIST:C_MASK]
        mask = const[:, C_MASK:C_COS]
        cos = const[:, C_COS:C_SIN].rearrange("p (t r) -> p t r", t=2)
        sin = const[:, C_SIN:C_END].rearrange("p (t r) -> p t r", t=2)

        b_f = small[:, 0:8]
        gate_z = small[:, 8:24].rearrange("p (t h) -> p t h", t=2)
        gate_a = small[:, 24:40].rearrange("p (t h) -> p t h", t=2)
        gate_l = small[:, 40:56].rearrange("p (t h) -> p t h", t=2)
        cum = small[:, 56:72].rearrange("p (t h) -> p t h", t=2)
        lam = small[:, 72:77]
        top = small[:, 144:148].rearrange("p (u t) -> p u t", t=2)
        shift = small[:, 82:86].rearrange("p (u t) -> p u t", t=2)
        total = small[:, 86:94].rearrange("p (u t) -> p u t", t=2)
        inverse = small[:, 148:152].rearrange("p (u t) -> p u t", t=2)
        sumsq = small[:, 96:112]
        var = small[:, 112:120]
        rstd = small[:, 120:128]
        newton = small[:, 128:136]
        seed = small[:, 136:144]
        lam_rows = prob[:, 0, :]
        cumT = prob[0:8, 1, 0:SEQ]
        key_cum = v_b[:, :, :].rearrange("p t (h k) -> p (t h) k", k=SEQ)

        x_loaded, mem_loaded, const_loaded, small_loaded = map(sem, ("x_loaded", "mem_loaded", "const_loaded", "small_loaded"))
        raw_loaded = [sem(f"raw_loaded{s}") for s in range(RAW)]
        gain_loaded = sem("gain_loaded")
        hi_ready, lo_ready, tile_used = map(sem, ("hi_ready", "lo_ready", "tile_used"))
        evac_act, evac_dve = sem("evac_act"), sem("evac_dve")
        turn_done, turned_act, turned_dve = map(sem, ("turn_done", "turned_act", "turned_dve"))
        xturn_done, split_hi, split_lo = map(sem, ("xturn_done", "split_hi", "split_lo"))
        squares_act, squares_dve, var_ready, seed_ready, rstd_ready = map(
            sem, ("squares_act", "squares_dve", "var_ready", "seed_ready", "rstd_ready"))
        scaled_act, scaled_dve = sem("scaled_act"), sem("scaled_dve")
        resid_ready = sem("resid_ready")
        s_done, soft_ready, p_ready, pt_done, pt_ready, o_done, o_ready = map(
            sem, ("s_done", "soft_ready", "p_ready", "pt_done", "pt_ready", "o_done", "o_ready"))
        act_chain, dve_chain = sem("act_chain"), sem("dve_chain")
        gate_pe, gate_act, gate_dve = map(sem, ("gate_pe", "gate_act", "gate_dve"))
        key_cum_act, relu_act, relu_dve, lam_exp = map(sem, ("key_cum_act", "relu_act", "relu_dve", "lam_exp"))
        y_zero, sub_done, rope_ready, lam_ready, out_stored = map(sem, ("y_zero", "sub_done", "rope_ready", "lam_ready", "out_stored"))

        def bank(index, c, t):
            return 4 * (index % 2) + 2 * c + t

        def side_of(name):
            return 4 * ((PLAN[name]["index"] + 1) % 2)

        def finished(eng, name):
            eng.wait_ge(tile_used, PLAN[name]["tile"] + PLAN[name]["tiles"])

        def evacuated(eng, name):
            g = PLAN[name]
            eng.wait_ge(evac_act, g["act"] + g["banks"])
            eng.wait_ge(evac_dve, g["dve"] + g["banks"])

        def turns_evacuated(eng, name):
            eng.wait_ge(turned_act, TURNED_ACT[name] + turned_by(name)[0])
            eng.wait_ge(turned_dve, TURNED_DVE[name] + turned_by(name)[1])

        def split(eng, name, banks):
            eng.wait_ge(split_hi, SPLITS[name] + banks)
            eng.wait_ge(split_lo, SPLITS[name] + banks)

        def wait_then(wait, side):
            wait()
            yield from side

        class Unit:
            def __init__(self, family, n):
                self.u = UNITS[family] + n
                self.family, self.n = family, n
                self.causal = family not in ("x0", "x1")
                self.scale = MLA_SCALE if family == "mla" else SCALE
                j = n
                if family in ("fox", "mla"):
                    self.q, self.k = qT_a[:, j, :], kT_a[:, j, :]
                    self.v = v_a[:, :, j * HD:(j + 1) * HD]
                    self.o = rows[:, :, j * HD:(j + 1) * HD]
                elif family == "diff":
                    h = j // 2
                    self.q, self.k = qT_b[:, j, :], kT_b[:, j, :]
                    self.v = v_b[:, :, h * 2 * HD:(h + 1) * 2 * HD]
                    self.o = rows[:, :, FOX_W + h * 2 * HD:FOX_W + (h + 1) * 2 * HD]
                    self.slope = 2.0 ** (-8.0 * (h + 1) / DIFF_HEADS)
                elif family == "moba":
                    self.q, self.k = qT_b[:, j, :], kT_b[:, j, :]
                    self.v = v_b[:, :, j * HD:(j + 1) * HD]
                    self.o = rows[:, :, 1024 + j * HD:1024 + (j + 1) * HD]
                    self.slope = 2.0 ** (-8.0 * (j + 1) / 8)
                else:
                    self.q, self.k = kT_a[:, j, :], mem_kT[:, j, :]
                    self.v = mem_v[:, :, j * HD:(j + 1) * HD]
                    self.o = rows[:, :, j * HD:(j + 1) * HD]
                if family == "mla":
                    r = 64 * (j % 2)
                    self.qpe, self.kpe = qpeT[r:r + 64, j // 2, :], kpeT[r:r + 64, :]
                self.exp_scale = 1.0 if family == "fox" else self.scale
                self.dv = 2 * HD if family == "diff" else HD
                self.parts = [(0, 0, P), (1, P, 2 * P)] if self.causal else [(0, 0, 2 * P), (1, 2 * P, 2 * P)]
                self.cols = sum(p[2] for p in self.parts)

        def units(family, a=0, b=8):
            return [Unit(family, n) for n in range(a, b)]

        block = ctx.enter_context(nc.Block())

        @block.sync
        def _(sp):
            sp.dma_start(rows[:, :, :], mem[0].rearrange("(t p) d -> p t d", p=P)).then_inc(mem_loaded, 16)
            sp.dma_start(const[:, :], consts).then_inc(const_loaded, 16)

            def load(i, dma, source, per, width):
                slot = dma % RAW
                if i is not None or dma >= RAW:
                    sp.wait_ge(hi_ready, at(i, Mlp.TILES, 2 * dma - 2 * RAW + 2))
                    sp.wait_ge(lo_ready, at(i, Mlp.TILES, 2 * dma - 2 * RAW + 2))
                sp.dma_start(raw[:, slot, 0:2 * per * width].rearrange("p (c w) -> p c w", w=width), source)\
                    .then_inc(raw_loaded[slot], 16)

            def load_group(name):
                g = PLAN[name]
                w, col = weights[name]
                height = 2 * g["per"] * P
                for n in range(g["tiles"] // 2):
                    if name == "mem" and n == RAW:
                        sp.dma_start(resid[:, :, :], x[0].rearrange("(t p) d -> p t d", p=P)).then_inc(x_loaded, 16)
                    source = w[n * height:(n + 1) * height, col:col + g["width"]].rearrange("(c p) w -> p c w", p=P)
                    load(None, g["tile"] // 2 + n, source, g["per"], g["width"])

            def load_up(l, i, b, tile):
                for n in range(8):
                    source = ffn_w1[l][2 * n * P:2 * (n + 1) * P, bass.ds(at(i, 2048, b * 1024), 1024)]
                    load(i, tile // 2 + n, source.rearrange("(c p) w -> p c w", p=P), 1, 1024)

            def load_down(l, i, b, tile):
                for half in range(2):
                    for n in range(4):
                        source = ffn_w2[l][bass.ds(at(i, 2048, b * 1024 + 2 * n * P), 2 * P), 1024 * half:1024 * (half + 1)]
                        load(i, tile // 2 + 4 * half + n, source.rearrange("(c p) w -> p c w", p=P), 1, 1024)

            for name, chunks, _, _ in GROUPS:
                if chunks is not None:
                    load_group(name)
                    continue
                l = int(name[3])
                m = Mlp(l)
                load_up(l, None, 0, m.up(0)[1])
                load_up(l, None, 1, m.up(1)[1])
                load_down(l, None, 0, m.down(0, 0)[1])
                with sp.Fori(0, (BLOCKS - 2) // 2) as i:
                    for b in (1, 2):
                        load_up(l, i, b + 1, m.up(b + 1)[1])
                        load_down(l, i, b, m.down(b, 0)[1])
                load_down(l, None, BLOCKS - 1, m.down(BLOCKS - 1, 0)[1])
            sp.wait_ge(resid_ready, 2 * len(POST))
            sp.dma_start(out[0].rearrange("(t p) d -> p t d", p=P), resid[:, :, :]).then_inc(out_stored, 16)
            sp.wait_ge(out_stored, 16)

        @block.gpsimd
        def _(pool):
            loads = [(gain_rows[0:16, :], mem_norm.rearrange("(c p) -> c p", p=P))]
            for n, (l, i) in enumerate([(0, 0), (0, 2), (0, 4), (1, 0), (1, 2), (1, 4)]):
                loads.append((gain_rows[16 + 16 * n:32 + 16 * n, :], norms[l, i].rearrange("(c p) -> c p", p=P)))
            loads.append((gain_rows[112:116, :], mla_q_norm[0].rearrange("(c p) -> c p", p=P)))
            loads.append((gain_rows[116:120, :], mla_kv_norm[0].rearrange("(c p) -> c p", p=P)))
            loads.append((b_f, fox_b_f[0:1, :].to_broadcast([P, 8])))
            loads.append((subln[:, :], diff_subln[0:1, :].to_broadcast([P, 2 * HD])))
            loads.append((lam_rows, diff_lambda.rearrange("a b d -> a (b d)").to_broadcast([P, 4 * HD])))
            assert len(loads) == SMALL_LOADS
            for to, source in loads:
                pool.dma_start(to, source).then_inc(small_loaded, 16)
            for name, (l, i) in POST.items():
                if name[1] == "a":
                    pool.wait_ge(o_done, UNITS["diff" if l == 0 else "moba"] + 8)
                else:
                    pool.wait_ge(resid_ready, 2 * POST_AT[name])
                pool.dma_start(gain_row[:, :], norms[l, i:i + 1, :].to_broadcast([P, D])).then_inc(gain_loaded, 16)

        @block.scalar
        def _(act):
            chain = [0]

            def link(ins):
                chain[0] += 1
                ins.then_inc(act_chain, 1)
                act.wait_ge(act_chain, chain[0])

            def stream(i, tile, count, cols, side=iter(())):
                for k in range(tile, tile + count):
                    if k % 2 == 0:
                        act.wait_ge(raw_loaded[(k // 2) % RAW], at(i, 16 * Mlp.TILES // 2 // RAW, 16 * (k // 2 // RAW + 1)))
                    if i is not None or k >= RING:
                        act.wait_ge(tile_used, at(i, Mlp.TILES, k - RING + 1))
                    nc.scalar.activation(w_hi[:, k % RING, 0:cols], raw[:, (k // 2) % RAW, (k % 2) * cols:(k % 2 + 1) * cols],
                                         ACT.Copy).then_inc(hi_ready, 1)
                    if k - tile >= LEAD:
                        next(side, None)
                for _ in side:
                    pass

            def stream_group(name, side=iter(()), first=0, count=None):
                g = PLAN[name]
                stream(None, g["tile"] + first, count or g["tiles"], g["per"] * g["width"], side)

            def evacuate(name, c, to, view=None):
                g = PLAN[name]
                finished(act, name)
                source = PS[:, bank(g["index"], c, 0), 0:col_banks(g["width"])[c][1]]
                ins = nc.scalar.activation(to, source if view is None else view(source), ACT.Copy)
                return ins.then_inc(evac_act, 1)

            def turned(name, to, side):
                for b in range(turned_by(name)[0]):
                    act.wait_ge(turn_done, TURNS[name] + b + 1)
                    nc.scalar.activation(to[:, 2 * b:2 * b + 2, :].rearrange("p c s -> p (c s)"), PS[:, side + b, :], ACT.Copy)\
                        .then_inc(turned_act, 1)

            def heads(name, to, chunks, where, gain=None):
                if gain is not None:
                    act.wait_ge(turned_dve, TURNED_DVE["gain"] + 1)
                for c in range(0, chunks, 2):
                    act.wait_ge(xturn_done, SPLITS[name] + c // 2 + 1)
                    b = where(c)
                    if gain is None:
                        nc.scalar.activation(to[:, c:c + 2, :].rearrange("p c s -> p (c s)"), PS[:, b, :], ACT.Copy)\
                            .then_inc(split_hi, 1)
                        continue
                    nc.scalar.activation(to[:, c, :], PS[:, b, 0:SEQ], ACT.Copy, scale=gain_col[:, gain + c:gain + c + 1])
                    nc.scalar.activation(to[:, c + 1, :], PS[:, b, SEQ:2 * SEQ], ACT.Copy,
                                         scale=gain_col[:, gain + c + 1:gain + c + 2]).then_inc(split_hi, 1)

            def rstd_seed(name, width=2):
                act.wait_ge(var_ready, NORMS[name] + 1)
                link(nc.scalar.activation(newton[:, 0:width], var[:, 0:width], ACT.Ln))
                nc.scalar.activation(seed[:, 0:width], newton[:, 0:width], ACT.Exp, scale=-0.5).then_inc(seed_ready, 1)

            def prenorm_rows(name, source, scratch):
                nc.scalar.activation(scratch, source, ACT.Square, accum_out=sumsq[:, 0:1]).then_inc(squares_act, 1)
                rstd_seed(name)
                act.wait_ge(rstd_ready, NORMS[name] + 1)
                nc.scalar.activation(rows[:, 0, :], source, ACT.Copy, scale=rstd[:, 0:1]).then_inc(scaled_act, 1)

            def attend(us, side):
                for s in range(len(us) + 2):
                    if 1 <= s <= len(us):
                        a = us[s - 1]
                        act.wait_ge(pt_done, a.u + 1)
                        if a.u >= 2:
                            act.wait_ge(o_done, a.u - 1)
                        nc.scalar.activation(prob[:, a.u % 2, 0:a.cols], PS[:, side + 2, 0:a.cols], ACT.Copy).then_inc(pt_ready, 1)
                    if s < len(us):
                        a = us[s]
                        act.wait_ge(soft_ready, a.u + 1)
                        if not a.causal:
                            act.wait_ge(pt_done, a.u - 1)
                        for t, col, keys in a.parts:
                            source = logit[:, a.u % 2, col:col + keys] if a.causal else PS[:, side + a.u % 2, col:col + keys]
                            ins = nc.scalar.activation(logit[:, a.u % 2, col:col + keys], source, ACT.Exp,
                                                       bias=shift[:, a.u % 2, t:t + 1], scale=a.exp_scale,
                                                       accum_out=total[:, a.u % 4, t:t + 1])
                        ins.then_inc(p_ready, 1)
                    yield

            def postnorm(name, source, evacuations):
                evacuations()
                nc.scalar.activation(x_hi[:, 0:8, :].rearrange("p c s -> p (c s)"), source[:, 0, :], ACT.Square,
                                     accum_out=sumsq[:, 0:1]).then_inc(squares_act, 1)
                rstd_seed(name)

            def prenorm(name):
                act.wait_ge(resid_ready, 2 * POST_AT[BEFORE[name]] + 1)
                prenorm_rows(name, resid[:, 0, :], rows[:, 0, :])
                heads(name, x_hi, 16, lambda c: norm_bank(name, c), GAIN_COL[name])

            def two_column_groups(first, second):
                def side():
                    for c in range(2):
                        evacuate(first, c, rows[:, 0, 512 * c:512 * c + 512])
                        yield
                stream_group(second, side())
                for c in range(2):
                    evacuate(second, c, rows[:, 0, 1024 + 512 * c:1536 + 512 * c])

            def mixer_out(first, second, last_proj, family, o_names, sub):
                for c in range(2):
                    evacuate(last_proj, c, v_b[:, 0, 512 * c:512 * c + 512])
                side = side_of(first)
                heads(o_names[0], x_hi, 8, lambda c: side + c // 2)
                stream_group(first, attend(units(family), side), 0, 8)
                if sub:
                    act.wait_ge(o_ready, UNITS["diff"] + 8)
                    for h in range(DIFF_HEADS):
                        part = rows[:, 0, FOX_W + 256 * h:FOX_W + 256 * (h + 1)]
                        ins = nc.scalar.activation(x_hi[:, 8 + h, :], part, ACT.Square, accum_out=sumsq[:, h:h + 1])
                    ins.then_inc(squares_act, 1)
                    rstd_seed("sub", 8)
                heads(o_names[1], x_hi[:, 8:16, :], 8, lambda c: side + c // 2)
                stream_group(first, first=8, count=8)
                two_column_groups(first, second)

            def cross(l):
                stream_group(f"xq{l}")
                evacuate(f"xq{l}", 0, rows[:, 0, 1024:1536])
                turned(f"xq{l}", kT_a, 4)
                for _ in attend(units(f"x{l}", 0, 4), 0):
                    pass
                heads(f"xo{l}", x_hi, 4, lambda c: c // 2)
                stream_group(f"xo{l}0")
                two_column_groups(f"xo{l}0", f"xo{l}1")

            def mlp(l):
                m = Mlp(l)

                def hidden(i, b):
                    g, tile = m.up(b)
                    act.wait_ge(tile_used, at(i, Mlp.TILES, tile + 16))
                    if i is not None or b > 0:
                        act.wait_ge(xturn_done, at(i, Mlp.SPLITS, m.s + 4 * b))
                    for c in range(2):
                        part = rows[:, 0, 512 * c:512 * c + 512]
                        nc.scalar.activation(part, PS[:, bank(g, c, 0), :], ACT.Relu).then_inc(relu_act, 1)
                    for c in range(2):
                        part = rows[:, 0, 512 * c:512 * c + 512]
                        act.wait_ge(relu_act, at(i, Mlp.ACT, 2 * BLOCKS * l + 2 * b + c + 1))
                        nc.scalar.activation(part, part, ACT.Square).then_inc(evac_act, 1)
                    yield
                    yield
                    for n in range(4):
                        act.wait_ge(xturn_done, at(i, Mlp.SPLITS, m.s + 4 * b + n + 1))
                        nc.scalar.activation(h_hi[b % 2][:, 2 * n:2 * n + 2, :].rearrange("p c s -> p (c s)"),
                                             PS[:, bank(g, 0, 0) + n, :], ACT.Copy).then_inc(split_hi, 1)
                        yield

                def up(i, b, side=iter(())):
                    stream(i, m.up(b)[1], 16, 1024, side)

                def down(i, b, half, side=iter(())):
                    stream(i, m.down(b, half)[1], 8, 1024, side)

                up(None, 0)
                up(None, 1, hidden(None, 0))
                down(None, 0, 0, hidden(None, 1))
                down(None, 0, 1)
                with act.Fori(0, (BLOCKS - 2) // 2) as i:
                    for b in (1, 2):
                        up(i, b + 1)
                        down(i, b, 0, hidden(i, b + 1))
                        down(i, b, 1)
                down(None, BLOCKS - 1, 0)
                down(None, BLOCKS - 1, 1)

            act.wait_ge(mem_loaded, 16)
            prenorm_rows("mem", rows[:, 0, :], qT_a[:, :, :].rearrange("p h s -> p (h s)"))
            heads("mem", x_hi, 16, lambda c: norm_bank("mem", c), GAIN_COL["mem"])

            act.wait_ge(lam_ready, 1)
            nc.scalar.activation(lam[:, 2:4], lam[:, 0:2], ACT.Exp).then_inc(lam_exp, 1)

            def side_first():
                act.wait_ge(x_loaded, 16)
                act.wait_ge(xturn_done, SPLITS["mem"] + 8)
                prenorm_rows("a0", resid[:, 0, :], rows[:, 0, :])
                yield
            stream_group("mem", side_first())
            evacuate("mem", 0, qT_b[:, 0:2, :].rearrange("p h s -> p (h s)"))
            evacuate("mem", 1, mem_v[:, 0, :])
            heads("a0", x_hi, 16, lambda c: norm_bank("a0", c), GAIN_COL["a0"])

            stream_group("fg")

            def side_gate():
                side = side_of("fv")
                evacuate("fg", 0, gate_z[:, 0, :])
                yield
                act.wait_ge(gate_dve, 1)
                link(nc.scalar.activation(gate_a[:, :, :], gate_a[:, :, :], ACT.Exp))
                nc.scalar.activation(gate_a[:, :, :], gate_a[:, :, :], ACT.Ln, bias=1.0).then_inc(gate_act, 1)
                yield
                turned("mem_k", mem_kT, side)
                yield
                yield
                yield
                yield
                act.wait_ge(gate_pe, 2)
                for b in range(2):
                    nc.scalar.activation(key_cum[:, 2 * b:2 * b + 2, :].rearrange("p h k -> p (h k)"), PS[:, side + b, :], ACT.Copy)\
                        .then_inc(key_cum_act, 1)
                yield
            stream_group("fv", side_gate())

            def side_value(name, to):
                for c in range(2):
                    evacuate(name, c, to[:, 0, 512 * c:512 * c + 512])
                yield
            stream_group("fq", side_value("fv", v_a))

            def side_turn(name, to, follow):
                for c in range(2):
                    evacuate(name, c, rows[:, 0, 1024 + 512 * c:1536 + 512 * c])
                yield
                yield
                turned(name, to, side_of(follow))
                yield

            def chained(*sides):
                for side in sides:
                    yield from side

            stream_group("fk", side_turn("fq", qT_a, "fk"))
            stream_group("dq", side_turn("fk", kT_a, "dq"))
            stream_group("dk", chained(side_turn("dq", qT_b, "dk"), attend(units("fox", 0, FOX_FIRST), side_of("dk"))))
            stream_group("dv", chained(side_turn("dk", kT_b, "dv"), attend(units("fox", FOX_FIRST, 8), side_of("dv"))))
            mixer_out("abo0", "abo1", "dv", "diff", ("o0a", "o0b"), True)
            postnorm("pa0", rows, lambda: evacuated(act, "abo1"))

            prenorm("x0")
            cross(0)
            postnorm("px0", rows, lambda: evacuated(act, "xo01"))
            prenorm("f0")
            mlp(0)
            postnorm("pf0", y_acc, lambda: act.wait_ge(evac_dve, PLAN["kpe"]["dve"]))

            prenorm("a1")
            stream_group("kpe")

            def side_kpe():
                evacuate("kpe", 0, rows[:, 0, 1024:1088])
                yield
            stream_group("cqkv", side_kpe())

            def side_low_rank():
                for c in range(2):
                    evacuate("cqkv", c, rows[:, 0, 512 * c:512 * c + 512])
                yield
                act.wait_ge(evac_act, PLAN["cqkv"]["act"] + 2)
                for c in range(2):
                    ins = nc.scalar.activation(logit[:, c, :], rows[:, 0, 512 * c:512 * c + 512], ACT.Square,
                                               accum_out=sumsq[:, c:c + 1])
                ins.then_inc(squares_act, 1)
                rstd_seed("c1", 4)
                act.wait_ge(rstd_ready, NORMS["c1"] + 1)
                for c in range(2):
                    part = rows[:, 0, 512 * c:512 * c + 512]
                    ins = nc.scalar.activation(part, part, ACT.Copy, scale=rstd[:, c:c + 1])
                ins.then_inc(scaled_act, 1)
                yield
                yield
                heads("c1", c_hi, 8, lambda c: side_of("mq") + c // 2, GAIN_COL["q"])
                yield
            stream_group("mq", side_low_rank())
            stream_group("uq0", side_turn("mq", qT_b, "uq0"))

            def side_query(name, first):
                for c in range(2):
                    evacuate(name, c, rows[:, 0, first + 384 * c:first + 384 * (c + 1)])
                yield
            stream_group("uq1", side_query("uq0", 0))
            stream_group("ukv0", side_query("uq1", 768))

            def side_key_value(name, turn, n, follow):
                g = PLAN[name]
                finished(act, name)
                if n:
                    act.wait_ge(turn_done, TURNS["kn0"] + 2)
                for c in range(2):
                    source = PS[:, bank(g["index"], c, 0), :].rearrange("p (h w d) -> p h w d", h=2, w=2)
                    nc.scalar.activation(rows[:, 0, 1536 + 256 * c:1792 + 256 * c].rearrange("p (h d) -> p h d", h=2),
                                         source[:, :, 0, :], ACT.Copy)
                    value = v_a[:, 0, 512 * n + 256 * c:512 * n + 256 * (c + 1)]
                    nc.scalar.activation(value.rearrange("p (h d) -> p h d", h=2), source[:, :, 1, :], ACT.Copy)\
                        .then_inc(evac_act, 1)
                yield
                yield
                turned(turn, kT_a[:, 4 * n:4 * n + 4, :], side_of(follow))
                yield
            stream_group("ukv1", side_key_value("ukv0", "kn0", 0, "ukv1"))

            def side_queries():
                yield
                turned("qn", qT_a, side_of("mk"))
                yield
                yield
                turned("qpe", qpeT, side_of("mk"))
                yield
            stream_group("mk", chained(side_key_value("ukv1", "kn1", 1, "mk"), side_queries(),
                                       attend(units("mla", 0, MLA_FIRST), side_of("mk"))))
            stream_group("mv", chained(side_turn("mk", kT_b, "mv"), attend(units("mla", MLA_FIRST, 8), side_of("mv"))))
            mixer_out("cdo0", "cdo1", "mv", "moba", ("o1a", "o1b"), False)
            postnorm("pa1", rows, lambda: evacuated(act, "cdo1"))
            prenorm("x1")
            cross(1)
            postnorm("px1", rows, lambda: evacuated(act, "xo11"))
            prenorm("f1")
            mlp(1)
            postnorm("pf1", y_acc, lambda: act.wait_ge(evac_dve, Mlp(1).v + 10 * BLOCKS))

        @block.vector
        def _(dve):
            chain = [0]

            def link(ins):
                chain[0] += 1
                ins.then_inc(dve_chain, 1)
                dve.wait_ge(dve_chain, chain[0])

            def stream(i, tile, count, cols, side=iter(())):
                for k in range(tile, tile + count):
                    dve.wait_ge(hi_ready, at(i, Mlp.TILES, k + 1))
                    nc.vector.tensor_tensor(w_lo[:, k % RING, 0:cols], raw[:, (k // 2) % RAW, (k % 2) * cols:(k % 2 + 1) * cols],
                                            w_hi[:, k % RING, 0:cols].bitcast(F32), ALU.subtract).then_inc(lo_ready, 1)
                    if k - tile >= LEAD:
                        next(side, None)
                for _ in side:
                    pass

            def stream_group(name, side=iter(()), first=0, count=None):
                g = PLAN[name]
                stream(None, g["tile"] + first, count or g["tiles"], g["per"] * g["width"], side)

            def evacuate(name, c, to):
                g = PLAN[name]
                finished(dve, name)
                source = PS[:, bank(g["index"], c, 1), 0:col_banks(g["width"])[c][1]]
                return nc.vector.tensor_copy(to, source).then_inc(evac_dve, 1)

            def turned(name, to, side):
                skip, n = turned_by(name)
                for b in range(skip, skip + n):
                    dve.wait_ge(turn_done, TURNS[name] + b + 1)
                    nc.vector.tensor_copy(to[:, 2 * b:2 * b + 2, :].rearrange("p c s -> p (c s)"), PS[:, side + b, :])\
                        .then_inc(turned_dve, 1)

            def rests(name, heads, to, chunks, where, gain=None):
                for c in range(0, chunks, 2):
                    dve.wait_ge(split_hi, SPLITS[name] + c // 2 + 1)
                    b = where(c)
                    if gain is None:
                        nc.vector.tensor_tensor(to[:, c:c + 2, :].rearrange("p c s -> p (c s)"), PS[:, b, :],
                                                heads[:, c:c + 2, :].rearrange("p c s -> p (c s)").bitcast(F32), ALU.subtract)\
                            .then_inc(split_lo, 1)
                        continue
                    nc.vector.scalar_tensor_tensor(out=to[:, c, :], in0=PS[:, b, 0:SEQ], scalar=gain_col[:, gain + c:gain + c + 1],
                                                   in1=heads[:, c, :].bitcast(F32), op0=ALU.mult, op1=ALU.subtract)
                    nc.vector.scalar_tensor_tensor(out=to[:, c + 1, :], in0=PS[:, b, SEQ:2 * SEQ],
                                                   scalar=gain_col[:, gain + c + 1:gain + c + 2],
                                                   in1=heads[:, c + 1, :].bitcast(F32), op0=ALU.mult, op1=ALU.subtract)\
                        .then_inc(split_lo, 1)

            def squares(scratch, source, to):
                return nc.vector.tensor_tensor_reduce(scratch, source, source, 1.0, 0.0, ALU.mult, ALU.add, to)

            def row_rstd(name, width, length):
                dve.wait_ge(squares_act, NORMS[name] + 1)
                v, y, w, r = var[:, 0:width], seed[:, 0:width], newton[:, 0:width], rstd[:, 0:width]
                nc.vector.tensor_scalar(v, sumsq[:, 0:width], 1.0 / length, EPS, ALU.mult, ALU.add).then_inc(var_ready, 1)
                dve.wait_ge(seed_ready, NORMS[name] + 1)
                link(nc.vector.tensor_tensor(w, y, y, ALU.mult))
                link(nc.vector.tensor_tensor(w, w, v, ALU.mult))
                link(nc.vector.tensor_scalar(w, w, -0.5, 1.5, ALU.mult, ALU.add))
                nc.vector.tensor_tensor(r, w, y, ALU.mult).then_inc(rstd_ready, 1)
                dve.wait_ge(rstd_ready, NORMS[name] + 1)

            def prenorm_rows(name, source, scratch):
                link(squares(scratch, source, sumsq[:, 1:2]))
                row_rstd(name, 2, D)
                nc.vector.tensor_scalar(rows[:, 1, :], source, rstd[:, 1:2], None, ALU.mult).then_inc(scaled_dve, 1)

            def attend(us, side):
                for s in range(len(us) + 2):
                    if s < len(us):
                        a = us[s]
                        S, L = PS[:, side + a.u % 2, 0:a.cols], logit[:, a.u % 2, 0:a.cols]
                        dve.wait_ge(s_done, a.u + 1)
                        if a.u >= 2 and a.causal:
                            dve.wait_ge(pt_done, a.u - 1)
                        if a.family == "fox":
                            for t, col, keys in a.parts:
                                ins = nc.vector.scalar_tensor_tensor(
                                    out=logit[:, a.u % 2, col:col + keys], in0=key_cum[:, a.n, 0:keys], scalar=cum[:, t, a.n:a.n + 1],
                                    in1=mask[:, col:col + keys], op0=ALU.subtract, op1=ALU.subtract)
                            link(ins)
                            link(nc.vector.scalar_tensor_tensor(out=L, in0=S, scalar=SCALE, in1=L, op0=ALU.mult, op1=ALU.subtract))
                        elif a.family == "mla":
                            link(nc.vector.tensor_tensor(L, S, mask, ALU.add))
                        elif a.causal:
                            link(nc.vector.scalar_tensor_tensor(out=L, in0=dist, scalar=a.slope / SCALE, in1=S, op0=ALU.mult, op1=ALU.add))
                        source = L if a.causal else S
                        for t, col, keys in a.parts:
                            ins = nc.vector.tensor_reduce(top[:, a.u % 2, t:t + 1], source[:, col:col + keys], AX_X, ALU.max)
                        link(ins)
                        nc.vector.tensor_scalar(shift[:, a.u % 2, :], top[:, a.u % 2, :], -a.exp_scale, None, ALU.mult).then_inc(soft_ready, 1)
                    if s >= 2:
                        a = us[s - 2]
                        dve.wait_ge(o_done, a.u + 1)
                        link(nc.vector.reciprocal(inverse[:, a.u % 2, :], total[:, a.u % 4, :]))
                        minus = a.family == "diff" and a.n % 2
                        if minus:
                            link(nc.vector.tensor_scalar(inverse[:, a.u % 2, :], inverse[:, a.u % 2, :], lam[:, 4:5], None, ALU.mult))
                            dve.wait_ge(o_ready, a.u)
                        for t in range(HALVES):
                            O = PS[:, side + 3, t * a.dv:(t + 1) * a.dv]
                            if minus:
                                ins = nc.vector.scalar_tensor_tensor(out=a.o[:, t, :], in0=O, scalar=inverse[:, a.u % 2, t:t + 1],
                                                                     in1=a.o[:, t, :], op0=ALU.mult, op1=ALU.add)
                            else:
                                ins = nc.vector.tensor_scalar(a.o[:, t, :], O, inverse[:, a.u % 2, t:t + 1], None, ALU.mult)
                        ins.then_inc(o_ready, 1)
                    yield

            def postnorm(name, source, evacuations):
                evacuations()
                link(squares(x_lo[:, 0:8, :].rearrange("p c s -> p (c s)"), source[:, 1, :], sumsq[:, 1:2]))
                row_rstd(name, 2, D)
                dve.wait_ge(gain_loaded, 16 * (POST_AT[name] + 1))
                for t in range(HALVES):
                    link(nc.vector.scalar_tensor_tensor(out=source[:, t, :], in0=source[:, t, :], scalar=rstd[:, t:t + 1],
                                                        in1=gain_row[:, :], op0=ALU.mult, op1=ALU.mult))
                    nc.vector.tensor_tensor(resid[:, t, :], resid[:, t, :], source[:, t, :], ALU.add).then_inc(resid_ready, 1)

            def prenorm(name):
                dve.wait_ge(resid_ready, 2 * POST_AT[BEFORE[name]] + 2)
                prenorm_rows(name, resid[:, 1, :], rows[:, 1, :])
                rests(name, x_hi, x_lo, 16, lambda c: norm_bank(name, c), GAIN_COL[name])

            def two_column_groups(first, second):
                def side():
                    for c in range(2):
                        evacuate(first, c, rows[:, 1, 512 * c:512 * c + 512])
                        yield
                stream_group(second, side())
                for c in range(2):
                    evacuate(second, c, rows[:, 1, 1024 + 512 * c:1536 + 512 * c])

            def mixer_out(first, second, last_proj, family, o_names, sub):
                for c in range(2):
                    evacuate(last_proj, c, v_b[:, 1, 512 * c:512 * c + 512])
                side = side_of(first)
                rests(o_names[0], x_hi, x_lo, 8, lambda c: side + c // 2)
                stream_group(first, attend(units(family), side), 0, 8)
                if sub:
                    dve.wait_ge(o_ready, UNITS["diff"] + 8)
                    for h in range(DIFF_HEADS):
                        ins = squares(x_lo[:, 8 + h, :], rows[:, 1, FOX_W + 256 * h:FOX_W + 256 * (h + 1)], sumsq[:, 4 + h:5 + h])
                    link(ins)
                    row_rstd("sub", 8, 2 * HD)
                    for t in range(HALVES):
                        for h in range(DIFF_HEADS):
                            part = rows[:, t, FOX_W + 256 * h:FOX_W + 256 * (h + 1)]
                            ins = nc.vector.scalar_tensor_tensor(out=part, in0=part, scalar=rstd[:, 4 * t + h:4 * t + h + 1],
                                                                 in1=subln[:, :], op0=ALU.mult, op1=ALU.mult)
                    ins.then_inc(scaled_dve, 1)
                rests(o_names[1], x_hi[:, 8:16, :], x_lo[:, 8:16, :], 8, lambda c: side + c // 2)
                stream_group(first, first=8, count=8)
                two_column_groups(first, second)

            def cross(l):
                stream_group(f"xq{l}")
                evacuate(f"xq{l}", 0, rows[:, 1, 1024:1536])
                turned(f"xq{l}", kT_a, 4)
                for _ in attend(units(f"x{l}", 0, 4), 0):
                    pass
                rests(f"xo{l}", x_hi, x_lo, 4, lambda c: c // 2)
                stream_group(f"xo{l}0")
                two_column_groups(f"xo{l}0", f"xo{l}1")

            def mlp(l):
                m = Mlp(l)
                nc.vector.memset(y_acc[:, :, :], 0.0).then_inc(y_zero, 1)
                dve.wait_ge(y_zero, l + 1)

                def hidden(i, b):
                    g, tile = m.up(b)
                    dve.wait_ge(tile_used, at(i, Mlp.TILES, tile + 16))
                    if i is not None or b > 0:
                        dve.wait_ge(xturn_done, at(i, Mlp.SPLITS, m.s + 4 * b))
                    for c in range(2):
                        part = rows[:, 1, 512 * c:512 * c + 512]
                        nc.vector.tensor_scalar(part, PS[:, bank(g, c, 1), :], 0.0, None, ALU.max).then_inc(relu_dve, 1)
                    for c in range(2):
                        part = rows[:, 1, 512 * c:512 * c + 512]
                        dve.wait_ge(relu_dve, at(i, Mlp.ACT, 2 * BLOCKS * l + 2 * b + c + 1))
                        nc.vector.tensor_tensor(part, part, part, ALU.mult).then_inc(evac_dve, 1)
                    yield
                    yield
                    for n in range(4):
                        dve.wait_ge(split_hi, at(i, Mlp.SPLITS, m.s + 4 * b + n + 1))
                        nc.vector.tensor_tensor(h_lo[b % 2][:, 2 * n:2 * n + 2, :].rearrange("p c s -> p (c s)"),
                                                PS[:, bank(g, 0, 0) + n, :],
                                                h_hi[b % 2][:, 2 * n:2 * n + 2, :].rearrange("p c s -> p (c s)").bitcast(F32),
                                                ALU.subtract).then_inc(split_lo, 1)
                        yield

                def accumulate(i, b, half):
                    g, tile = m.down(b, half)
                    dve.wait_ge(tile_used, at(i, Mlp.TILES, tile + 8))
                    if b:
                        dve.wait_ge(evac_dve, at(i, Mlp.DVE, m.y_dve(b, half)))
                    for c in range(2):
                        for t in range(HALVES):
                            part = y_acc[:, t, 1024 * half + 512 * c:1024 * half + 512 * (c + 1)]
                            nc.vector.tensor_tensor(part, part, PS[:, bank(g, c, t), :], ALU.add).then_inc(evac_dve, 1)
                        yield

                def up(i, b, side=iter(())):
                    stream(i, m.up(b)[1], 16, 1024, side)

                def down(i, b, half, side=iter(())):
                    stream(i, m.down(b, half)[1], 8, 1024, side)

                up(None, 0)
                up(None, 1, hidden(None, 0))
                down(None, 0, 0, hidden(None, 1))
                down(None, 0, 1, accumulate(None, 0, 0))
                with dve.Fori(0, (BLOCKS - 2) // 2) as i:
                    for b in (1, 2):
                        up(i, b + 1, accumulate(i, b - 1, 1))
                        down(i, b, 0, hidden(i, b + 1))
                        down(i, b, 1, accumulate(i, b, 0))
                down(None, BLOCKS - 1, 0, accumulate(None, BLOCKS - 2, 1))
                down(None, BLOCKS - 1, 1, accumulate(None, BLOCKS - 1, 0))
                for _ in accumulate(None, BLOCKS - 1, 1):
                    pass

            dve.wait_ge(small_loaded, 16 * SMALL_LOADS)
            for n in range(2):
                ins = nc.vector.tensor_tensor_reduce(logit[:, 0, n * HD:(n + 1) * HD], lam_rows[:, 2 * n * HD:(2 * n + 1) * HD],
                                                     lam_rows[:, (2 * n + 1) * HD:(2 * n + 2) * HD], 1.0, 0.0, ALU.mult, ALU.add,
                                                     lam[:, n:n + 1])
            ins.then_inc(lam_ready, 1)
            nc.vector.tensor_scalar(subln[:, :], subln[:, :], 1.0 - LAM_INIT, None, ALU.mult)
            dve.wait_ge(turn_done, TURNS["gain"] + 1)
            nc.vector.tensor_copy(gain_col[:, :], PS[:, 7, 0:120]).then_inc(turned_dve, 1)
            dve.wait_ge(turned_dve, TURNED_DVE["gain"] + 1)

            dve.wait_ge(mem_loaded, 16)
            prenorm_rows("mem", rows[:, 1, :], kT_a[:, :, :].rearrange("p h s -> p (h s)"))
            rests("mem", x_hi, x_lo, 16, lambda c: norm_bank("mem", c), GAIN_COL["mem"])
            dve.wait_ge(lam_exp, 1)
            link(nc.vector.tensor_tensor(lam[:, 4:5], lam[:, 3:4], lam[:, 2:3], ALU.subtract))
            link(nc.vector.tensor_scalar(lam[:, 4:5], lam[:, 4:5], -LAM_INIT, None, ALU.add))

            def side_first():
                dve.wait_ge(x_loaded, 16)
                dve.wait_ge(xturn_done, SPLITS["mem"] + 8)
                prenorm_rows("a0", resid[:, 1, :], rows[:, 1, :])
                yield
            stream_group("mem", side_first())
            evacuate("mem", 0, qT_b[:, 2:4, :].rearrange("p h s -> p (h s)"))
            evacuate("mem", 1, mem_v[:, 1, :])
            rests("a0", x_hi, x_lo, 16, lambda c: norm_bank("a0", c), GAIN_COL["a0"])

            stream_group("fg")

            def side_gate():
                side = side_of("fv")
                evacuate("fg", 0, gate_z[:, 1, :])
                yield
                evacuated(dve, "fg")
                for t in range(HALVES):
                    ins = nc.vector.tensor_tensor(gate_z[:, t, :], gate_z[:, t, :], b_f, ALU.add)
                link(ins)
                nc.vector.scalar_tensor_tensor(out=gate_a[:, :, :], in0=gate_z[:, :, :], scalar=-1.0, in1=gate_z[:, :, :],
                                               op0=ALU.mult, op1=ALU.min).then_inc(gate_dve, 1)
                dve.wait_ge(gate_act, 1)
                nc.vector.scalar_tensor_tensor(out=gate_l[:, :, :], in0=gate_z[:, :, :], scalar=0.0, in1=gate_a[:, :, :],
                                               op0=ALU.min, op1=ALU.subtract).then_inc(gate_dve, 1)
                yield
                turned("mem_k", mem_kT, side)
                yield
                dve.wait_ge(gate_pe, 1)
                nc.vector.tensor_copy(cum[:, :, :].rearrange("p t h -> p (t h)"), PS[:, side + 2, 0:16]).then_inc(gate_dve, 1)
                yield
                dve.wait_ge(turn_done, TURNS["cum"] + 1)
                nc.vector.tensor_copy(cumT, PS[0:8, side + 3, 0:SEQ]).then_inc(turned_dve, 1)
                yield
                yield
                dve.wait_ge(gate_pe, 2)
                for b in range(2, 4):
                    nc.vector.tensor_copy(key_cum[:, 2 * b:2 * b + 2, :].rearrange("p h k -> p (h k)"), PS[:, side + b, :])\
                        .then_inc(gate_dve, 1)
                yield
            stream_group("fv", side_gate())

            def side_value(name, to):
                for c in range(2):
                    evacuate(name, c, to[:, 1, 512 * c:512 * c + 512])
                yield
            stream_group("fq", side_value("fv", v_a))

            def side_turn(name, to, follow):
                for c in range(2):
                    evacuate(name, c, rows[:, 1, 1024 + 512 * c:1536 + 512 * c])
                yield
                yield
                turned(name, to, side_of(follow))
                yield

            def chained(*sides):
                for side in sides:
                    yield from side

            stream_group("fk", side_turn("fq", qT_a, "fk"))
            stream_group("dq", side_turn("fk", kT_a, "dq"))
            dve.wait_ge(key_cum_act, 2)
            stream_group("dk", chained(side_turn("dq", qT_b, "dk"), attend(units("fox", 0, FOX_FIRST), side_of("dk"))))
            stream_group("dv", chained(side_turn("dk", kT_b, "dv"), attend(units("fox", FOX_FIRST, 8), side_of("dv"))))
            mixer_out("abo0", "abo1", "dv", "diff", ("o0a", "o0b"), True)
            postnorm("pa0", rows, lambda: evacuated(dve, "abo1"))
            prenorm("x0")
            cross(0)
            postnorm("px0", rows, lambda: evacuated(dve, "xo01"))
            prenorm("f0")
            mlp(0)
            postnorm("pf0", y_acc, lambda: dve.wait_ge(evac_dve, PLAN["kpe"]["dve"]))

            prenorm("a1")
            stream_group("kpe")

            def rotate(source, to, t, heads, done):
                c = cos[:, t:t + 1, :].to_broadcast([P, heads, 32])
                s = sin[:, t:t + 1, :].to_broadcast([P, heads, 32])
                t1, t2 = source[:, :, 0:32], source[:, :, 32:64]
                a = logit[:, 0, 0:32 * heads].rearrange("p (h r) -> p h r", h=heads)
                b = logit[:, 1, 0:32 * heads].rearrange("p (h r) -> p h r", h=heads)
                nc.vector.tensor_tensor(a, t1, c, ALU.mult)
                link(nc.vector.tensor_tensor(b, t2, s, ALU.mult))
                link(nc.vector.tensor_tensor(to[:, :, 0:32], a, b, ALU.subtract))
                nc.vector.tensor_tensor(a, t2, c, ALU.mult)
                link(nc.vector.tensor_tensor(b, t1, s, ALU.mult))
                done(nc.vector.tensor_tensor(to[:, :, 32:64], a, b, ALU.add))

            def side_kpe():
                evacuate("kpe", 0, rows[:, 1, 1024:1088])
                yield
                evacuated(dve, "kpe")
                for t in range(HALVES):
                    source = rows[:, t, 1024:1088].rearrange("p (h r) -> p h r", h=1)
                    to = rows[:, t, 1088:1152].rearrange("p (h r) -> p h r", h=1)
                    rotate(source, to, t, 1, link)
                    ins = nc.vector.tensor_copy(rows[:, t, 1152:1216], rows[:, t, 1088:1152])
                ins.then_inc(rope_ready, 1)
                yield
                yield
                dve.wait_ge(turn_done, TURNS["kpe"] + 1)
                nc.vector.tensor_copy(kpeT[:, :], PS[:, side_of("cqkv"), 0:SEQ]).then_inc(turned_dve, 1)
                yield
            stream_group("cqkv", side_kpe())

            def side_low_rank():
                for c in range(2):
                    evacuate("cqkv", c, rows[:, 1, 512 * c:512 * c + 512])
                yield
                dve.wait_ge(evac_dve, PLAN["cqkv"]["dve"] + 2)
                for c in range(2):
                    ins = squares(prob[:, c, :], rows[:, 1, 512 * c:512 * c + 512], sumsq[:, 2 + c:3 + c])
                link(ins)
                row_rstd("c1", 4, 512)
                for c in range(2):
                    part = rows[:, 1, 512 * c:512 * c + 512]
                    ins = nc.vector.tensor_scalar(part, part, rstd[:, 2 + c:3 + c], None, ALU.mult)
                ins.then_inc(scaled_dve, 1)
                yield
                yield
                rests("c1", c_hi, c_lo, 8, lambda c: side_of("mq") + c // 2, GAIN_COL["q"])
                yield
            stream_group("mq", side_low_rank())
            stream_group("uq0", side_turn("mq", qT_b, "uq0"))

            def side_query(name, first):
                for c in range(2):
                    evacuate(name, c, rows[:, 1, first + 384 * c:first + 384 * (c + 1)])
                yield
            stream_group("uq1", side_query("uq0", 0))
            stream_group("ukv0", side_query("uq1", 768))

            def side_key_value(name, turn, n, follow):
                g = PLAN[name]
                finished(dve, name)
                if n:
                    dve.wait_ge(turn_done, TURNS["kn0"] + 2)
                for c in range(2):
                    source = PS[:, bank(g["index"], c, 1), :].rearrange("p (h w d) -> p h w d", h=2, w=2)
                    nc.vector.tensor_copy(rows[:, 1, 1536 + 256 * c:1792 + 256 * c].rearrange("p (h d) -> p h d", h=2),
                                          source[:, :, 0, :])
                    value = v_a[:, 1, 512 * n + 256 * c:512 * n + 256 * (c + 1)]
                    nc.vector.tensor_copy(value.rearrange("p (h d) -> p h d", h=2), source[:, :, 1, :]).then_inc(evac_dve, 1)
                yield
                yield
                turned(turn, kT_a[:, 4 * n:4 * n + 4, :], side_of(follow))
                yield
            stream_group("ukv1", side_key_value("ukv0", "kn0", 0, "ukv1"))

            def side_queries():
                evacuated(dve, "uq1")
                for t in range(HALVES):
                    source = rows[:, t, 0:8 * MLA_QK].rearrange("p (h w) -> p h w", w=MLA_QK)[:, :, HD:MLA_QK]
                    to = prob[:, t, :].rearrange("p (h r) -> p h r", h=8)
                    rotate(source, to, t, 8, lambda ins: ins.then_inc(rope_ready, 1))
                    dve.wait_ge(rope_ready, 2 + t)
                yield
                turned("qn", qT_a, side_of("mk"))
                yield
                yield
                turned("qpe", qpeT, side_of("mk"))
                yield
            stream_group("mk", chained(side_key_value("ukv1", "kn1", 1, "mk"), side_queries(),
                                       attend(units("mla", 0, MLA_FIRST), side_of("mk"))))
            stream_group("mv", chained(side_turn("mk", kT_b, "mv"), attend(units("mla", MLA_FIRST, 8), side_of("mv"))))
            mixer_out("cdo0", "cdo1", "mv", "moba", ("o1a", "o1b"), False)
            postnorm("pa1", rows, lambda: evacuated(dve, "cdo1"))
            prenorm("x1")
            cross(1)
            postnorm("px1", rows, lambda: evacuated(dve, "xo11"))
            prenorm("f1")
            mlp(1)
            postnorm("pf1", y_acc, lambda: dve.wait_ge(evac_dve, Mlp(1).v + 10 * BLOCKS))

        @block.tensor
        def _(pe):
            def products(i, tile, count, group, per, width, chunks, hi, lo, operand=None, first=0, side=iter(())):
                for k in range(count):
                    pe.wait_ge(hi_ready, at(i, Mlp.TILES, tile + k + 1))
                    pe.wait_ge(lo_ready, at(i, Mlp.TILES, tile + k + 1))
                    slot = (tile + k) % RING
                    for j in range(per):
                        ch = first + k * per + j
                        if operand is not None:
                            operand(ch)
                        start, stop = ch == 0, ch == chunks - 1
                        for t in range(HALVES):
                            xh, xl = hi[:, ch, t * P:(t + 1) * P], lo[:, ch, t * P:(t + 1) * P]
                            for x_part, w_part, a, z in ((xh, w_hi, start, False), (xh, w_lo, False, False), (xl, w_hi, False, stop)):
                                for c, (col, w) in enumerate(col_banks(width)):
                                    mm = nc.tensor.matmul(PS[:, bank(group, c, t), 0:w], x_part,
                                                          w_part[:, slot, j * width + col:j * width + col + w], start=a, stop=z)
                    mm.then_inc(tile_used, 1)
                    next(side, None)
                for _ in side:
                    pass

            def stream_group(name, side=iter(()), operand=None, first=0, count=None, hi=x_hi, lo=x_lo):
                g = PLAN[name]
                products(None, g["tile"] + first, count or g["tiles"], g["index"], g["per"], g["width"], g["chunks"],
                         hi, lo, operand, first * g["per"], side)

            def operand_of(name, base=0):
                def operand(ch):
                    if ch % 2 == 0 and ch >= base:
                        split(pe, name, (ch - base) // 2 + 1)
                return operand

            def turn_bank(b, source, chunks):
                for j in chunks:
                    for t in range(HALVES):
                        mm = nc.tensor.transpose(PS[:, b, (j % 2) * SEQ + t * P:(j % 2) * SEQ + (t + 1) * P], source(j, t), ident)
                return mm

            def turn(name, source, side):
                for b in range(dict(TURN_BANKS)[name]):
                    turn_bank(side + b, source, (2 * b, 2 * b + 1)).then_inc(turn_done, 1)

            def row_chunk(first, step=P):
                return lambda j, t: rows[:, t, first + j * step:first + j * step + P]

            def norm_turn(name):
                pe.wait_ge(scaled_act, SCALED_ACT[name] + 1)
                pe.wait_ge(scaled_dve, SCALED_DVE[name] + 1)
                for c in range(0, CH, 2):
                    turn_bank(norm_bank(name, c), row_chunk(0), (c, c + 1)).then_inc(xturn_done, 1)

            def attend(us, side):
                for s in range(len(us) + 2):
                    if s < len(us):
                        a = us[s]
                        if a.u >= 2:
                            pe.wait_ge(p_ready, a.u - 1)
                        for t, col, keys in a.parts:
                            S = PS[:, side + a.u % 2, col:col + keys]
                            mla = a.family == "mla"
                            mm = nc.tensor.matmul(S, a.q[:, t * P:(t + 1) * P], a.k[:, 0:keys], start=True, stop=not mla)
                            if mla:
                                mm = nc.tensor.matmul(S, a.qpe[:, t * P:(t + 1) * P], a.kpe[:, 0:keys], start=False, stop=True)
                        mm.then_inc(s_done, 1)
                    if 1 <= s <= len(us):
                        a = us[s - 1]
                        pe.wait_ge(p_ready, a.u + 1)
                        if a.u:
                            pe.wait_ge(pt_ready, a.u)
                        for col in range(0, a.cols, P):
                            mm = nc.tensor.transpose(PS[:, side + 2, col:col + P], logit[:, a.u % 2, col:col + P], ident)
                        mm.then_inc(pt_done, 1)
                    if s >= 2:
                        a = us[s - 2]
                        pe.wait_ge(pt_ready, a.u + 1)
                        if a.u:
                            pe.wait_ge(o_ready, a.u)
                        for t, col, keys in a.parts:
                            for n in range(keys // P):
                                mm = nc.tensor.matmul(PS[:, side + 3, t * a.dv:(t + 1) * a.dv],
                                                      prob[:, a.u % 2, col + n * P:col + (n + 1) * P], a.v[:, n, :],
                                                      start=n == 0, stop=n == keys // P - 1)
                        mm.then_inc(o_done, 1)
                    yield

            def chained(*sides):
                for side in sides:
                    yield from side

            def side_turn(name, follow):
                yield
                evacuated(pe, name)
                turn(name, row_chunk(1024), side_of(follow))
                yield
                yield

            def mixer_out(first, second, last_proj, first_family, family, o_names, sub):
                side = side_of(first)
                evacuated(pe, last_proj)
                pe.wait_ge(o_ready, UNITS[first_family] + 8)
                for c in range(0, 8, 2):
                    turn_bank(side + c // 2, row_chunk(0), (c, c + 1)).then_inc(xturn_done, 1)

                def attend_after_split():
                    split(pe, o_names[0], 4)
                    yield from attend(units(family), side)
                stream_group(first, attend_after_split(), operand_of(o_names[0]), 0, 8)
                if sub:
                    pe.wait_ge(scaled_dve, SCALED_DVE["sub"] + 1)
                else:
                    pe.wait_ge(o_ready, UNITS[family] + 8)
                for c in range(0, 8, 2):
                    turn_bank(side + c // 2, row_chunk(1024), (c, c + 1)).then_inc(xturn_done, 1)
                stream_group(first, operand=operand_of(o_names[1], 8), first=8, count=8)
                stream_group(second)

            def cross(l):
                norm_turn(f"x{l}")
                split(pe, f"x{l}", 4)
                stream_group(f"xq{l}", operand=operand_of(f"x{l}"))
                evacuated(pe, f"xq{l}")
                turn(f"xq{l}", row_chunk(1024), 4)
                turns_evacuated(pe, f"xq{l}")
                for _ in attend(units(f"x{l}", 0, 4), 0):
                    pass
                pe.wait_ge(o_ready, UNITS[f"x{l}"] + 4)
                for c in (0, 2):
                    turn_bank(c // 2, row_chunk(0), (c, c + 1)).then_inc(xturn_done, 1)
                stream_group(f"xo{l}0", operand=operand_of(f"xo{l}"))
                stream_group(f"xo{l}1")

            def mlp(l):
                m = Mlp(l)

                def hidden(i, b):
                    yield
                    pe.wait_ge(evac_act, at(i, Mlp.ACT, m.a + 2 * b + 2))
                    pe.wait_ge(evac_dve, at(i, Mlp.DVE, m.hid_dve(b) + 2))
                    for n in range(4):
                        turn_bank(bank(m.up(b)[0], 0, 0) + n, row_chunk(0), (2 * n, 2 * n + 1)).then_inc(xturn_done, 1)
                    yield

                def up(i, b, side=iter(()), operand=None):
                    g, tile = m.up(b)
                    products(i, tile, 16, g, 1, 1024, CH, x_hi, x_lo, operand, 0, side)

                def down(i, b, half, side=iter(())):
                    g, tile = m.down(b, half)
                    products(i, tile, 8, g, 1, 1024, 8, h_hi[b % 2], h_lo[b % 2], None, 0, side)

                def sums_free(i, b, half):
                    pe.wait_ge(evac_dve, at(i, Mlp.DVE, m.y_dve(b, half) + 4))

                def hidden_split(i, b):
                    pe.wait_ge(split_hi, at(i, Mlp.SPLITS, m.s + 4 * b + 4))
                    pe.wait_ge(split_lo, at(i, Mlp.SPLITS, m.s + 4 * b + 4))

                norm_turn(f"f{l}")
                split(pe, f"f{l}", 4)
                up(None, 0, operand=operand_of(f"f{l}"))
                up(None, 1, hidden(None, 0))
                hidden_split(None, 0)
                down(None, 0, 0, hidden(None, 1))
                hidden_split(None, 1)
                down(None, 0, 1)
                with pe.Fori(0, (BLOCKS - 2) // 2) as i:
                    for b in (1, 2):
                        sums_free(i, b - 1, 0)
                        up(i, b + 1)
                        sums_free(i, b - 1, 1)
                        down(i, b, 0, hidden(i, b + 1))
                        hidden_split(i, b + 1)
                        down(i, b, 1)
                sums_free(None, BLOCKS - 2, 0)
                down(None, BLOCKS - 1, 0)
                sums_free(None, BLOCKS - 2, 1)
                down(None, BLOCKS - 1, 1)

            pe.wait_ge(const_loaded, 16)
            pe.wait_ge(small_loaded, 16 * SMALL_LOADS)
            nc.tensor.transpose(PS[:, 7, 0:120], gain_rows[:, :], ident[0:120, 0:120]).then_inc(turn_done, 1)
            pe.wait_ge(turned_dve, TURNED_DVE["gain"] + 1)
            norm_turn("mem")
            split(pe, "mem", 4)
            stream_group("mem", operand=operand_of("mem"))
            evacuated(pe, "mem")
            norm_turn("a0")

            split(pe, "a0", 4)
            stream_group("fg", operand=operand_of("a0"))

            def side_gate():
                side = side_of("fv")
                yield
                evacuated(pe, "fg")
                turn("mem_k", lambda j, t: qT_b[:, 2 * t:2 * t + 2, :].rearrange("p h s -> p (h s)")[:, j * P:(j + 1) * P], side)
                yield
                yield
                pe.wait_ge(gate_dve, 2)
                nc.tensor.matmul(PS[:, side + 2, 0:8], tri, gate_l[:, 0, :], start=True, stop=True)
                nc.tensor.matmul(PS[:, side + 2, 8:16], ones, gate_l[:, 0, :], start=True, stop=False)
                nc.tensor.matmul(PS[:, side + 2, 8:16], tri, gate_l[:, 1, :], start=False, stop=True).then_inc(gate_pe, 1)
                yield
                pe.wait_ge(gate_dve, 3)
                for t in range(HALVES):
                    mm = nc.tensor.transpose(PS[0:8, side + 3, t * P:(t + 1) * P], cum[:, t, :], ident)
                mm.then_inc(turn_done, 1)
                yield
                turns_evacuated(pe, "cum")
                for h in range(8):
                    mm = nc.tensor.matmul(PS[:, side + h // 2, (h % 2) * SEQ:(h % 2 + 1) * SEQ],
                                          ident[0:8, h:h + 1].to_broadcast([8, P]), cumT, start=True, stop=True)
                mm.then_inc(gate_pe, 1)
                yield
            stream_group("fv", side_gate())
            pe.wait_ge(key_cum_act, 2)
            pe.wait_ge(gate_dve, 5)
            stream_group("fq")
            evacuated(pe, "fv")
            stream_group("fk", side_turn("fq", "fk"))
            turns_evacuated(pe, "fq")
            stream_group("dq", side_turn("fk", "dq"))
            turns_evacuated(pe, "fk")
            stream_group("dk", chained(side_turn("dq", "dk"), wait_then(lambda: turns_evacuated(pe, "dq"),
                                                                          attend(units("fox", 0, FOX_FIRST), side_of("dk")))))
            pe.wait_ge(o_ready, UNITS["fox"] + FOX_FIRST)
            stream_group("dv", chained(side_turn("dk", "dv"), wait_then(lambda: turns_evacuated(pe, "dk"),
                                                                          attend(units("fox", FOX_FIRST, 8), side_of("dv")))))
            mixer_out("abo0", "abo1", "dv", "fox", "diff", ("o0a", "o0b"), True)
            cross(0)
            mlp(0)

            norm_turn("a1")
            split(pe, "a1", 4)
            stream_group("kpe", operand=operand_of("a1"))

            def side_kpe():
                yield
                yield
                pe.wait_ge(rope_ready, 1)
                for t in range(HALVES):
                    mm = nc.tensor.transpose(PS[:, side_of("cqkv"), t * P:(t + 1) * P], rows[:, t, 1088:1216], ident)
                mm.then_inc(turn_done, 1)
                yield
            stream_group("cqkv", side_kpe())
            turns_evacuated(pe, "kpe")

            def side_low_rank():
                yield
                yield
                pe.wait_ge(scaled_act, SCALED_ACT["c1"] + 1)
                pe.wait_ge(scaled_dve, SCALED_DVE["c1"] + 1)
                for c in range(0, 8, 2):
                    turn_bank(side_of("mq") + c // 2, row_chunk(0), (c, c + 1)).then_inc(xturn_done, 1)
                yield
            stream_group("mq", side_low_rank())
            split(pe, "c1", 4)
            stream_group("uq0", side_turn("mq", "uq0"), hi=c_hi, lo=c_lo)
            turns_evacuated(pe, "mq")
            stream_group("uq1", hi=c_hi, lo=c_lo)
            evacuated(pe, "uq0")
            stream_group("ukv0", hi=c_hi[:, 4:8, :], lo=c_lo[:, 4:8, :])
            evacuated(pe, "uq1")

            def side_key(name, turn_name, follow):
                yield
                evacuated(pe, name)
                turn(turn_name, row_chunk(1536), side_of(follow))
                yield
                yield
            stream_group("ukv1", side_key("ukv0", "kn0", "ukv1"), hi=c_hi[:, 4:8, :], lo=c_lo[:, 4:8, :])
            turns_evacuated(pe, "kn0")

            def side_queries():
                turns_evacuated(pe, "kn1")
                turn("qn", row_chunk(0, MLA_QK), side_of("mk"))
                yield
                yield
                turns_evacuated(pe, "qn")
                pe.wait_ge(rope_ready, 3)
                turn("qpe", lambda j, t: prob[:, t, j * P:(j + 1) * P], side_of("mk"))
                yield
                yield
            stream_group("mk", chained(side_key("ukv1", "kn1", "mk"), side_queries(),
                                       wait_then(lambda: turns_evacuated(pe, "qpe"),
                                                 attend(units("mla", 0, MLA_FIRST), side_of("mk")))))
            pe.wait_ge(o_ready, UNITS["mla"] + MLA_FIRST)
            stream_group("mv", chained(side_turn("mk", "mv"), wait_then(lambda: turns_evacuated(pe, "mk"),
                                                                          attend(units("mla", MLA_FIRST, 8), side_of("mv")))))
            mixer_out("cdo0", "cdo1", "mv", "mla", "moba", ("o1a", "o1b"), False)
            cross(1)
            mlp(1)


def shape_constants():
    c = np.zeros((P, C_END), np.float32)
    row, col = np.arange(P)[:, None], np.arange(P)[None, :]
    c[:, C_ID:C_TRI] = row == col
    c[:, C_TRI:C_ONE] = row <= col
    c[:, C_ONE:C_DIST] = 1.0
    q = np.concatenate([np.broadcast_to(row, (P, P)), np.broadcast_to(row + P, (P, 2 * P))], 1)
    k = np.concatenate([np.arange(P), np.arange(2 * P)])[None, :]
    c[:, C_DIST:C_MASK] = np.where(k <= q, k - q, MASKED)
    c[:, C_MASK:C_COS] = np.where(k <= q, 0.0, MASKED)
    inv = np.float32(10000.0) ** (-np.arange(0, MLA_ROPE, 2, dtype=np.float32) / np.float32(MLA_ROPE))
    angle = np.arange(SEQ, dtype=np.float32)[:, None] * inv[None, :]
    for at0, f in ((C_COS, np.cos), (C_SIN, np.sin)):
        c[:, at0:at0 + 64] = f(angle).astype(np.float32).reshape(HALVES, P, 32).transpose(1, 0, 2).reshape(P, 64)
    return c


_INS = ["x", "mem", "mem_norm", "mem_wkv", "norms", "xattn_wq", "xattn_wo", "ffn_w1", "ffn_w2", "ab_w_in", "ab_w_out",
        "fox_b_f", "diff_lambda", "diff_subln", "cd_w_in", "cd_w_out", "mla_q_norm", "mla_kv_norm", "mla_w_uq", "mla_w_ukv"]


def kernel(**inputs):
    import concourse.bacc as _bacc
    from concourse import mybir as _mybir
    from concourse.bass_utils import run_bass_kernel_spmd as _run

    nc = _bacc.Bacc("TRN2", target_bir_lowering=False, num_devices=1)
    arrays, args = {}, []
    for name in _INS + ["consts"]:
        a = np.ascontiguousarray(inputs[name]) if name != "consts" else shape_constants()
        arrays[f"in_{name}_dram"] = a
        args.append(nc.dram_tensor(f"in_{name}_dram", a.shape, _mybir.dt.from_np(a.dtype), kind="ExternalInput").ap())
    args.append(nc.dram_tensor("out_0_dram", (1, SEQ, D), F32, kind="ExternalOutput").ap())
    trunk(nc, *args)
    r = _run(nc, [arrays], core_ids=[0])
    return r.results[0]["out_0_dram"]
```

```python
from contextlib import ExitStack
import math

import numpy as np

import concourse.bass as bass
from concourse import mybir

F32 = mybir.dt.float32
F32R = mybir.dt.float32r
ALU = mybir.AluOpType
ACT = mybir.ActivationFunctionType
AX_X = mybir.AxisListType.X

P = 128
SEQ = 256
HALVES = SEQ // P
D = 2048
CH = D // P
FFN = 4 * D
BLOCKS = FFN // 1024
EPS = 1e-6
HD = 128
FOX_W = 1024
DIFF_HEADS = 4
MLA_ROPE = 64
MLA_QK = HD + MLA_ROPE
MEM_LEN = 256
XW = 512
SCALE = HD ** -0.5
MLA_SCALE = MLA_QK ** -0.5
LAM_INIT = 0.8 - 0.6 * math.exp(0.0)
MASKED = -1e36

RAW = 4
RING = 4
TILE = 1024
LEAD = 3

C_ID, C_TRI, C_ONE, C_DIST, C_MASK, C_COS, C_SIN, C_END = np.cumsum([0, 128, 128, 128, 384, 384, 64, 64]).tolist()

GROUPS = [
    ("mem", 16, 1, 1024),
    ("fv", 16, 1, 1024), ("fg", 16, 8, 8), ("fq", 16, 1, 1024), ("fk", 16, 1, 1024),
    ("dq", 16, 1, 1024), ("dk", 16, 1, 1024), ("dv", 16, 1, 1024),
    ("abo0", 16, 1, 1024), ("abo1", 16, 1, 1024),
    ("xq0", 16, 2, 512), ("xo00", 4, 1, 1024), ("xo01", 4, 1, 1024),
    ("ffn0", None, None, None),
    ("cqkv", 16, 1, 1024), ("kpe", 16, 8, 64), ("mq", 16, 1, 1024),
    ("uq0", 4, 1, 768), ("uq1", 4, 1, 768), ("ukv0", 4, 1, 1024), ("ukv1", 4, 1, 1024),
    ("mk", 16, 1, 1024), ("mv", 16, 1, 1024),
    ("cdo0", 16, 1, 1024), ("cdo1", 16, 1, 1024),
    ("xq1", 16, 2, 512), ("xo10", 4, 1, 1024), ("xo11", 4, 1, 1024),
    ("ffn1", None, None, None),
]
OUT_GROUPS = ("abo0", "abo1", "cdo0", "cdo1", "xo00", "xo01", "xo10", "xo11")
FFN_GROUPS = 3 * BLOCKS
FFN_TILES = BLOCKS * (16 + 2 * 8)


def col_banks(width):
    n = -(-width // 512)
    return [(c * (width // n), width // n) for c in range(n)]


def plan_groups():
    plan, index, tile, act, dve = {}, 0, 0, 0, 0
    for name, chunks, per, width in GROUPS:
        plan[name] = dict(index=index, tile=tile, chunks=chunks, per=per, width=width, act=act, dve=dve)
        if chunks is None:
            index, tile = index + FFN_GROUPS, tile + FFN_TILES
            act, dve = act + BLOCKS, dve + 5 * BLOCKS
        else:
            n = 2 if name in OUT_GROUPS else 1
            plan[name].update(tiles=chunks // per, evacs=n)
            index, tile, act, dve = index + 1, tile + chunks // per, act + n, dve + n
    return plan


def running(items):
    at, out = 0, {}
    for name, n in items:
        out[name] = at
        at += n
    return out


PLAN = plan_groups()
SPLITS = running([("mem", 8), ("a0", 8), ("o0a", 4), ("o0b", 4), ("x0", 8), ("xo0", 2), ("f0", 8), ("h0", 4 * BLOCKS),
                  ("a1", 8), ("c1", 4), ("o1a", 4), ("o1b", 4), ("x1", 8), ("xo1", 2), ("f1", 8), ("h1", 4 * BLOCKS)])
TURN_BANKS = [("gain", 1), ("mem_k", 2), ("cum", 1), ("fq", 4), ("fk", 4), ("dq", 4), ("dk", 4), ("xq0", 2),
              ("kpe", 1), ("mq", 4), ("kn0", 2), ("kn1", 2), ("qn", 4), ("qpe", 2), ("mk", 4), ("xq1", 2)]
TURNS = running(TURN_BANKS)


def turned_by(name):
    return int(dict(TURN_BANKS)[name] > 1), 1


TURNED_ACT = running([(n, turned_by(n)[0]) for n, _ in TURN_BANKS])
TURNED_DVE = running([(n, turned_by(n)[1]) for n, _ in TURN_BANKS])
UNITS = running([("fox", 8), ("diff", 8), ("x0", 4), ("mla", 8), ("moba", 8), ("x1", 4)])
NORMS = running([(n, 1) for n in ("mem", "a0", "sub", "pa0", "x0", "px0", "f0", "pf0",
                                  "a1", "c1", "pa1", "x1", "px1", "f1", "pf1")])
SQUARES = running([(n, 1) for n in ("mem", "a0", "sub", "x0", "f0", "a1", "c1", "x1", "f1")])
GAIN_COL = {"mem": 0, "a0": 16, "x0": 32, "f0": 48, "a1": 64, "x1": 80, "f1": 96, "q": 112, "kv": 116}
POST = {"pa0": (0, 1), "px0": (0, 3), "pf0": (0, 5), "pa1": (1, 1), "px1": (1, 3), "pf1": (1, 5)}
POST_AT = {n: i for i, n in enumerate(POST)}
BEFORE = {"x0": "pa0", "f0": "px0", "a1": "pf0", "x1": "pa1", "f1": "px1"}
SMALL_LOADS, GAIN_LOADS = 3, 9
FOX_FIRST, MLA_FIRST = 5, 2
NEXT_GROUP = {"mem": "mem", "x0": "xq0", "f0": "ffn0", "a1": "cqkv", "x1": "xq1", "f1": "ffn1"}
PIECES = 4
PREFILL = 3


def at(i, per, static):
    return static if i is None else i * per + static


class Mlp:
    TILES, SPLITS, ACT, DVE = 64, 8, 2, 10

    def __init__(self, l):
        g = PLAN[f"ffn{l}"]
        self.l, self.g, self.t, self.a, self.v, self.s = l, g["index"], g["tile"], g["act"], g["dve"], SPLITS[f"h{l}"]

    def up(self, b):
        return (self.g + b, self.t + 16 * b) if b < 2 else (self.g + 3 * b - 2, self.t + 32 * b - 16)

    def down(self, b, half):
        if b == 0:
            return self.g + 2 + half, self.t + 32 + 8 * half
        if b == BLOCKS - 1:
            return self.g + 3 * b + 1 + half, self.t + 32 * b + 16 + 8 * half
        return self.g + 3 * b + 2 + half, self.t + 32 * b + 32 + 8 * half

    def hid_dve(self, b):
        return self.v + (0 if b == 0 else 5 * b - 4)

    def y_dve(self, b, half):
        return self.v + (5 * b + 2 if b < BLOCKS - 1 else 5 * b + 1) + 2 * half


def trunk(nc, x, mem, mem_norm, mem_wkv, norms, xattn_wq, xattn_wo, ffn_w1, ffn_w2, ab_w_in, ab_w_out,
          fox_b_f, diff_lambda, diff_subln, cd_w_in, cd_w_out, mla_q_norm, mla_kv_norm, mla_w_uq, mla_w_ukv,
          consts, out):
    AB, CD = ab_w_in[0], cd_w_in[0]
    weights = {
        "mem": (mem_wkv, 0),
        "fq": (AB, 0), "fk": (AB, 1024), "fv": (AB, 2048), "fg": (AB, 3072),
        "dq": (AB, 3080), "dk": (AB, 4104), "dv": (AB, 5128),
        "abo0": (ab_w_out[0], 0), "abo1": (ab_w_out[0], 1024),
        "kpe": (CD, 1024), "cqkv": (CD, 0), "mq": (CD, 1088), "mk": (CD, 2112), "mv": (CD, 3136),
        "uq0": (mla_w_uq[0], 0), "uq1": (mla_w_uq[0], 768), "ukv0": (mla_w_ukv[0], 0), "ukv1": (mla_w_ukv[0], 1024),
        "cdo0": (cd_w_out[0], 0), "cdo1": (cd_w_out[0], 1024),
    }
    for l in range(2):
        weights |= {f"xq{l}": (xattn_wq[l], 0), f"xo{l}0": (xattn_wo[l], 0), f"xo{l}1": (xattn_wo[l], 1024)}

    with ExitStack() as ctx:
        def sb(name, shape, dt=F32, own=ctx):
            return own.enter_context(nc.sbuf_tensor(name, shape, dt))

        def sem(name):
            return ctx.enter_context(nc.semaphore(name))

        PS = ctx.enter_context(nc.psum_tensor("PS", [P, 8, 512], F32))
        resid = sb("resid", [P, HALVES, D])
        x_hi = sb("x_hi", [P, CH, SEQ], F32R)
        x_lo = sb("x_lo", [P, CH, SEQ], F32R)
        rows = sb("rows", [P, HALVES, D])
        raw = sb("raw", [P, RAW, 2 * TILE])
        w_hi = sb("w_hi", [P, RING, TILE], F32R)
        w_lo = sb("w_lo", [P, RING, TILE], F32R)
        const = sb("const", [P, C_END])
        mem_kT = sb("mem_kT", [P, 4, MEM_LEN])
        mem_v = sb("mem_v", [P, HALVES, XW])
        gain_rows = sb("gain_rows", [120, P])
        gain_col = sb("gain_col", [P, 120])
        small = sb("small", [P, 192])
        subln = sb("subln", [P, 2 * HD])
        with ExitStack() as mixer:
            qT_a = sb("qT_a", [P, 8, SEQ], own=mixer)
            kT_a = sb("kT_a", [P, 8, SEQ], own=mixer)
            v_a = sb("v_a", [P, HALVES, 1024], own=mixer)
            qT_b = sb("qT_b", [P, 8, SEQ], own=mixer)
            kT_b = sb("kT_b", [P, 8, SEQ], own=mixer)
            v_b = sb("v_b", [P, HALVES, 1024], own=mixer)
            logit = sb("logit", [P, 2, 512], own=mixer)
            prob = sb("prob", [P, 2, 512], own=mixer)
            qpeT = sb("qpeT", [P, 4, SEQ], own=mixer)
            kpeT = sb("kpeT", [P, SEQ], own=mixer)
        with ExitStack() as low_rank:
            sb("gap_q", [P, 4, 8 * SEQ], own=low_rank)
            c_hi = sb("c_hi", [P, 8, SEQ], F32R, own=low_rank)
            c_lo = sb("c_lo", [P, 8, SEQ], F32R, own=low_rank)
        with ExitStack() as mlp:
            gain_row = sb("gain_row", [P, D], own=mlp)
            y_acc = sb("y_acc", [P, HALVES, D], own=mlp)
            h_hi = [sb(f"h_hi{i}", [P, 8, SEQ], F32R, own=mlp) for i in range(2)]
            h_lo = [sb(f"h_lo{i}", [P, 8, SEQ], F32R, own=mlp) for i in range(2)]
        sb("mixer_region", [P, 6 * 8 * SEQ + 2 * 1024 + 5 * SEQ])

        ident = const[:, C_ID:C_TRI]
        tri = const[:, C_TRI:C_ONE]
        ones = const[:, C_ONE:C_DIST]
        dist = const[:, C_DIST:C_MASK]
        mask = const[:, C_MASK:C_COS]
        cos = const[:, C_COS:C_SIN].rearrange("p (t r) -> p t r", t=2)
        sin = const[:, C_SIN:C_END].rearrange("p (t r) -> p t r", t=2)

        b_f = small[:, 0:8]
        gate_z = small[:, 8:24].rearrange("p (t h) -> p t h", t=2)
        gate_a = small[:, 24:40].rearrange("p (t h) -> p t h", t=2)
        gate_l = small[:, 40:56].rearrange("p (t h) -> p t h", t=2)
        cum = small[:, 56:72].rearrange("p (t h) -> p t h", t=2)
        lam = small[:, 72:77]
        top = small[:, 144:148].rearrange("p (u t) -> p u t", t=2)
        shift = small[:, 82:86].rearrange("p (u t) -> p u t", t=2)
        total = small[:, 86:94].rearrange("p (u t) -> p u t", t=2)
        inverse = small[:, 148:152].rearrange("p (u t) -> p u t", t=2)
        sumsq = small[:, 96:112]
        var = small[:, 112:120]
        rstd_sub = small[:, 120:128]
        rstd_pre = small[:, 152:154]
        rstd_post = small[:, 154:156]
        rstd_c = small[:, 156:160]
        sumsq_post = small[:, 160:164]
        post_base = small[:, 164:166]
        sumsq_pre = small[:, 166:168]
        sumsq_c = small[:, 168:172]
        newton = small[:, 128:136]
        seed = small[:, 136:144]
        lam_rows = prob[:, 0, :]
        cumT = prob[0:8, 1, 0:SEQ]
        key_cum = v_b[:, :, :].rearrange("p t (h k) -> p (t h) k", k=SEQ)

        x_loaded, const_loaded, small_loaded, gain_rows_loaded = map(sem, ("x_loaded", "const_loaded", "small_loaded", "gain_rows_loaded"))
        mem_loaded = [sem(f"mem_loaded{p}") for p in range(PIECES)]
        raw_loaded = [sem(f"raw_loaded{s}") for s in range(RAW)]
        gain_loaded = sem("gain_loaded")
        hi_ready, lo_ready, tile_used = map(sem, ("hi_ready", "lo_ready", "tile_used"))
        evac_act, evac_dve = sem("evac_act"), sem("evac_dve")
        turn_done, turned_act, turned_dve = map(sem, ("turn_done", "turned_act", "turned_dve"))
        xturn_done, split_hi, split_lo = map(sem, ("xturn_done", "split_hi", "split_lo"))
        squares_act, var_ready, seed_ready, rstd_ready = map(
            sem, ("squares_act", "var_ready", "seed_ready", "rstd_ready"))
        resid_ready = sem("resid_ready")
        s_done, soft_ready, p_ready, pt_done, pt_ready, o_done, o_ready = map(
            sem, ("s_done", "soft_ready", "p_ready", "pt_done", "pt_ready", "o_done", "o_ready"))
        act_chain, dve_chain = sem("act_chain"), sem("dve_chain")
        gate_pe, gate_act, gate_dve = map(sem, ("gate_pe", "gate_act", "gate_dve"))
        key_cum_act, relu_act, relu_dve, lam_exp = map(sem, ("key_cum_act", "relu_act", "relu_dve", "lam_exp"))
        sub_scaled, rope_ready, lam_ready, out_stored = map(sem, ("sub_scaled", "rope_ready", "lam_ready", "out_stored"))
        y_zero, y_squares, y_gained = map(sem, ("y_zero", "y_squares", "y_gained"))

        def bank(index, c, t):
            return 4 * (index % 2) + 2 * t + c

        def side_of(name):
            return 4 * ((PLAN[name]["index"] + 1) % 2)

        def finished(eng, name):
            eng.wait_ge(tile_used, PLAN[name]["tile"] + PLAN[name]["tiles"])

        def evacuated(eng, name):
            g = PLAN[name]
            eng.wait_ge(evac_act, g["act"] + g["evacs"])
            eng.wait_ge(evac_dve, g["dve"] + g["evacs"])

        def turns_evacuated(eng, name):
            eng.wait_ge(turned_act, TURNED_ACT[name] + turned_by(name)[0])
            eng.wait_ge(turned_dve, TURNED_DVE[name] + turned_by(name)[1])

        def split(eng, name, banks):
            eng.wait_ge(split_hi, SPLITS[name] + banks)
            eng.wait_ge(split_lo, SPLITS[name] + banks)

        def sums(index, t, width):
            first, parts = bank(index, 0, t), col_banks(width)
            if len(parts) == 1:
                return PS[:, first, 0:width]
            return PS[:, first:first + 2, 0:parts[0][1]]

        def like(to, width):
            n = len(col_banks(width))
            return to if n == 1 else to.rearrange("p (c w) -> p c w", c=n)

        def operand_bank(name, pair):
            return 4 * ((PLAN[NEXT_GROUP[name]]["index"] + 1) % 2) + pair % 4

        def chained(*sides):
            for side in sides:
                yield from side

        def wait_then(wait, side):
            wait()
            yield from side

        class Unit:
            def __init__(self, family, n):
                self.u = UNITS[family] + n
                self.family, self.n = family, n
                self.causal = family not in ("x0", "x1")
                self.scale = MLA_SCALE if family == "mla" else SCALE
                j = n
                if family in ("fox", "mla"):
                    self.q, self.k = qT_a[:, j, :], kT_a[:, j, :]
                    self.v = v_a[:, :, j * HD:(j + 1) * HD]
                    self.o = rows[:, :, j * HD:(j + 1) * HD]
                elif family == "diff":
                    h = j // 2
                    self.q, self.k = qT_b[:, j, :], kT_b[:, j, :]
                    self.v = v_b[:, :, h * 2 * HD:(h + 1) * 2 * HD]
                    self.o = rows[:, :, FOX_W + h * 2 * HD:FOX_W + (h + 1) * 2 * HD]
                    self.slope = 2.0 ** (-8.0 * (h + 1) / DIFF_HEADS)
                elif family == "moba":
                    self.q, self.k = qT_b[:, j, :], kT_b[:, j, :]
                    self.v = v_b[:, :, j * HD:(j + 1) * HD]
                    self.o = rows[:, :, 1024 + j * HD:1024 + (j + 1) * HD]
                    self.slope = 2.0 ** (-8.0 * (j + 1) / 8)
                else:
                    self.q, self.k = kT_a[:, j, :], mem_kT[:, j, :]
                    self.v = mem_v[:, :, j * HD:(j + 1) * HD]
                    self.o = rows[:, :, j * HD:(j + 1) * HD]
                if family == "mla":
                    r = 64 * (j % 2)
                    self.qpe, self.kpe = qpeT[r:r + 64, j // 2, :], kpeT[r:r + 64, :]
                self.exp_scale = 1.0 if family == "fox" else self.scale
                self.dv = 2 * HD if family == "diff" else HD
                self.parts = [(0, 0, P), (1, P, 2 * P)] if self.causal else [(0, 0, 2 * P), (1, 2 * P, 2 * P)]
                self.cols = sum(p[2] for p in self.parts)

        def units(family, a=0, b=8):
            return [Unit(family, n) for n in range(a, b)]

        block = ctx.enter_context(nc.Block())

        @block.sync
        def _(sp):
            def piece(of, p):
                return of[:, :, p * D // PIECES:(p + 1) * D // PIECES]

            sp.dma_start(const[:, :], consts).then_inc(const_loaded, 16)
            for p in range(PIECES):
                sp.dma_start(piece(rows, p), piece(mem[0].rearrange("(t p) d -> p t d", p=P), p)).then_inc(mem_loaded[p], 16)

            def load(i, dma, source, per, width):
                slot = dma % RAW
                if i is not None or dma >= RAW:
                    sp.wait_ge(hi_ready, at(i, Mlp.TILES, 2 * dma - 2 * RAW + 2))
                    sp.wait_ge(lo_ready, at(i, Mlp.TILES, 2 * dma - 2 * RAW + 2))
                sp.dma_start(raw[:, slot, 0:2 * per * width].rearrange("p (c w) -> p c w", w=width), source)\
                    .then_inc(raw_loaded[slot], 16)

            def load_group(name):
                g = PLAN[name]
                w, col = weights[name]
                height = 2 * g["per"] * P
                for n in range(g["tiles"] // 2):
                    if name == "mem" and n == RAW:
                        sp.dma_start(resid[:, :, :], x[0].rearrange("(t p) d -> p t d", p=P)).then_inc(x_loaded, 16)
                    source = w[n * height:(n + 1) * height, col:col + g["width"]].rearrange("(c p) w -> p c w", p=P)
                    load(None, g["tile"] // 2 + n, source, g["per"], g["width"])

            def load_up(l, i, b, tile):
                for n in range(8):
                    source = ffn_w1[l][2 * n * P:2 * (n + 1) * P, bass.ds(at(i, 2048, b * 1024), 1024)]
                    load(i, tile // 2 + n, source.rearrange("(c p) w -> p c w", p=P), 1, 1024)

            def load_down(l, i, b, tile):
                for half in range(2):
                    for n in range(4):
                        source = ffn_w2[l][bass.ds(at(i, 2048, b * 1024 + 2 * n * P), 2 * P), 1024 * half:1024 * (half + 1)]
                        load(i, tile // 2 + 4 * half + n, source.rearrange("(c p) w -> p c w", p=P), 1, 1024)

            for name, chunks, _, _ in GROUPS:
                if chunks is not None:
                    load_group(name)
                    continue
                l = int(name[3])
                m = Mlp(l)
                load_up(l, None, 0, m.up(0)[1])
                load_up(l, None, 1, m.up(1)[1])
                load_down(l, None, 0, m.down(0, 0)[1])
                with sp.Fori(0, (BLOCKS - 2) // 2) as i:
                    for b in (1, 2):
                        load_up(l, i, b + 1, m.up(b + 1)[1])
                        load_down(l, i, b, m.down(b, 0)[1])
                load_down(l, None, BLOCKS - 1, m.down(BLOCKS - 1, 0)[1])
            for p in range(PIECES):
                sp.wait_ge(resid_ready, 2 * PIECES * POST_AT["pf1"] + 2 * p + 2)
                sp.dma_start(piece(out[0].rearrange("(t p) d -> p t d", p=P), p), piece(resid, p)).then_inc(out_stored, 16)
            sp.wait_ge(out_stored, 16 * PIECES)

        @block.gpsimd
        def _(pool):
            for to, source in ((b_f, fox_b_f[0:1, :].to_broadcast([P, 8])),
                               (subln[:, :], diff_subln[0:1, :].to_broadcast([P, 2 * HD])),
                               (lam_rows, diff_lambda.rearrange("a b d -> a (b d)").to_broadcast([P, 4 * HD]))):
                pool.dma_start(to, source).then_inc(small_loaded, 16)
            for name, (l, i) in POST.items():
                if name[1] == "a":
                    pool.wait_ge(o_done, UNITS["diff" if l == 0 else "moba"] + 8)
                else:
                    pool.wait_ge(resid_ready, 2 * PIECES * POST_AT[name])
                pool.dma_start(gain_row[:, :], norms[l, i:i + 1, :].to_broadcast([P, D])).then_inc(gain_loaded, 16)

        @block.scalar
        def _(act):
            chain = [0]

            def link(ins):
                chain[0] += 1
                ins.then_inc(act_chain, 1)
                act.wait_ge(act_chain, chain[0])

            def stream(i, tile, count, cols, side=iter(()), done=0):
                for k in range(tile + done, tile + count):
                    if k % 2 == 0:
                        act.wait_ge(raw_loaded[(k // 2) % RAW], at(i, 16 * Mlp.TILES // 2 // RAW, 16 * (k // 2 // RAW + 1)))
                    if i is not None or k >= RING:
                        act.wait_ge(tile_used, at(i, Mlp.TILES, k - RING + 1))
                    nc.scalar.activation(w_hi[:, k % RING, 0:cols], raw[:, (k // 2) % RAW, (k % 2) * cols:(k % 2 + 1) * cols],
                                         ACT.Copy).then_inc(hi_ready, 1)
                    if k - tile >= LEAD:
                        next(side, None)
                for _ in side:
                    pass

            def stream_group(name, side=iter(()), first=0, count=None, done=0):
                g = PLAN[name]
                stream(None, g["tile"] + first, count or g["tiles"], g["per"] * g["width"], side, done)

            def prefill(name, first=0):
                if name.startswith("ffn"):
                    stream(None, PLAN[name]["tile"], PREFILL, TILE)
                else:
                    stream_group(name, first=first, count=PREFILL)

            def evacuate(name, to, scale=None):
                g = PLAN[name]
                finished(act, name)
                nc.scalar.activation(like(to, g["width"]), sums(g["index"], 0, g["width"]), ACT.Copy,
                                     scale=rstd_pre[:, 0:1] if scale is None else scale).then_inc(evac_act, 1)

            def turned(name, to, side):
                n = dict(TURN_BANKS)[name] // 2
                act.wait_ge(turn_done, TURNS[name] + n)
                nc.scalar.activation(to[:, 0:2 * n, :].rearrange("p (b c) s -> p b (c s)", c=2), PS[:, side:side + n, :], ACT.Copy)\
                    .then_inc(turned_act, 1)

            def heads(name, pair, b, to=x_hi, gain=None):
                act.wait_ge(xturn_done, SPLITS[name] + pair + 1)
                c = 2 * pair
                if gain is None:
                    nc.scalar.activation(to[:, c:c + 2, :].rearrange("p c s -> p (c s)"), PS[:, b, :], ACT.Copy).then_inc(split_hi, 1)
                    return
                nc.scalar.activation(to[:, c, :], PS[:, b, 0:SEQ], ACT.Copy, scale=gain_col[:, gain + c:gain + c + 1])
                nc.scalar.activation(to[:, c + 1, :], PS[:, b, SEQ:2 * SEQ], ACT.Copy,
                                     scale=gain_col[:, gain + c + 1:gain + c + 2]).then_inc(split_hi, 1)

            def rstd_seed(name, width=2):
                act.wait_ge(var_ready, NORMS[name] + 1)
                link(nc.scalar.activation(newton[:, 0:width], var[:, 0:width], ACT.Ln))
                nc.scalar.activation(seed[:, 0:width], newton[:, 0:width], ACT.Exp, scale=-0.5).then_inc(seed_ready, 1)

            def row_squares(source, scratch):
                for t in range(HALVES):
                    ins = nc.scalar.activation(scratch(t), source[:, t, :], ACT.Square, accum_out=sumsq_pre[:, t:t + 1])
                ins.then_inc(squares_act, 1)

            def side_operand(name):
                for pair in range(4, 8):
                    heads(name, pair, operand_bank(name, pair), gain=GAIN_COL[name])
                    yield
                row_squares(resid, lambda t: rows[:, t, :])
                yield
                rstd_seed(name)
                yield
                act.wait_ge(rstd_ready, NORMS[name] + 1)

            def handover(name):
                for pair in range(4):
                    heads(name, pair, operand_bank(name, pair), gain=GAIN_COL[name])

            def attend(us, side):
                for s in range(len(us) + 2):
                    if 1 <= s <= len(us):
                        a = us[s - 1]
                        act.wait_ge(pt_done, a.u + 1)
                        if a.u >= 2:
                            act.wait_ge(o_done, a.u - 1)
                        nc.scalar.activation(prob[:, a.u % 2, 0:a.cols], PS[:, side + 2, 0:a.cols], ACT.Copy).then_inc(pt_ready, 1)
                    if s < len(us):
                        a = us[s]
                        act.wait_ge(soft_ready, a.u + 1)
                        if not a.causal:
                            act.wait_ge(pt_done, a.u - 1)
                        for t, col, keys in a.parts:
                            source = logit[:, a.u % 2, col:col + keys] if a.causal else PS[:, side + a.u % 2, col:col + keys]
                            ins = nc.scalar.activation(logit[:, a.u % 2, col:col + keys], source, ACT.Exp,
                                                       bias=shift[:, a.u % 2, t:t + 1], scale=a.exp_scale,
                                                       accum_out=total[:, a.u % 4, t:t + 1])
                        ins.then_inc(p_ready, 1)
                    yield

            def squares_of(name, part, t):
                g = PLAN[name]
                finished(act, name)
                if t:
                    act.wait_ge(evac_dve, g["dve"] + 1)
                if part:
                    act.wait_ge(evac_act, g["act"] - 1 + t)
                nc.scalar.activation((logit, prob)[t][:, :, :], sums(g["index"], t, 1024), ACT.Square,
                                     accum_out=sumsq_post[:, 2 * part + t:2 * part + t + 1]).then_inc(evac_act, 1)

            def out_projection(names, norm, following):
                def side():
                    yield
                    for t in range(HALVES):
                        squares_of(names[0], 0, t)
                        yield
                stream_group(names[1], side())
                prefill(following)
                for t in range(HALVES):
                    squares_of(names[1], 1, t)
                rstd_seed(norm)

            def mixer_out(names, last_proj, family, o_names, sub, norm, following):
                first = names[0]
                prefill(first)
                evacuate(last_proj, v_b[:, 0, :])
                side = side_of(first)
                for pair in range(4):
                    heads(o_names[0], pair, side + pair)
                stream_group(first, attend(units(family), side), 0, 8, PREFILL)
                prefill(first, 8)
                if sub:
                    act.wait_ge(o_ready, UNITS["diff"] + 8)
                    for h in range(DIFF_HEADS):
                        part = rows[:, 0, FOX_W + 256 * h:FOX_W + 256 * (h + 1)]
                        ins = nc.scalar.activation(x_hi[:, 8 + h, :], part, ACT.Square, accum_out=sumsq[:, h:h + 1])
                    ins.then_inc(squares_act, 1)
                    rstd_seed("sub", 8)
                for pair in range(4):
                    heads(o_names[1], pair, side + pair, x_hi[:, 8:16, :])
                stream_group(first, first=8, count=8, done=PREFILL)
                out_projection(names, norm, following)

            def cross(l):
                handover(f"x{l}")
                stream_group(f"xq{l}", side_operand(f"x{l}"), done=PREFILL)
                prefill(f"xo{l}0")
                evacuate(f"xq{l}", rows[:, 0, 1024:1536])
                turned(f"xq{l}", kT_a, 4)
                for _ in attend(units(f"x{l}", 0, 4), 0):
                    pass
                for pair in range(2):
                    heads(f"xo{l}", pair, pair)
                stream_group(f"xo{l}0", done=PREFILL)
                out_projection((f"xo{l}0", f"xo{l}1"), f"px{l}", f"ffn{l}")

            def mlp(l, following):
                m = Mlp(l)

                def hidden(i, b):
                    g, tile = m.up(b)
                    act.wait_ge(tile_used, at(i, Mlp.TILES, tile + 16))
                    if i is not None or b > 0:
                        act.wait_ge(xturn_done, at(i, Mlp.SPLITS, m.s + 4 * b))
                    part = like(rows[:, 0, 0:1024], 1024)
                    nc.scalar.activation(part, sums(g, 0, 1024), ACT.Relu, scale=rstd_pre[:, 0:1]).then_inc(relu_act, 1)
                    act.wait_ge(relu_act, at(i, Mlp.ACT, BLOCKS * l + b + 1))
                    nc.scalar.activation(part, part, ACT.Square).then_inc(evac_act, 1)
                    yield
                    yield
                    for n in range(4):
                        act.wait_ge(xturn_done, at(i, Mlp.SPLITS, m.s + 4 * b + n + 1))
                        nc.scalar.activation(h_hi[b % 2][:, 2 * n:2 * n + 2, :].rearrange("p c s -> p (c s)"),
                                             PS[:, bank(g, 0, 0) + n, :], ACT.Copy).then_inc(split_hi, 1)
                        yield

                def y_row_squares(half):
                    for t in range(HALVES):
                        act.wait_ge(evac_dve, m.y_dve(BLOCKS - 1, half) + t + 1)
                        ins = nc.scalar.activation(x_hi[:, 4 * t:4 * t + 4, :].rearrange("p c s -> p (c s)"),
                                                   y_acc[:, t, 1024 * half:1024 * (half + 1)], ACT.Square,
                                                   accum_out=sumsq_post[:, 2 * half + t:2 * half + t + 1])
                    ins.then_inc(y_squares, 1)

                def side_last():
                    yield
                    yield
                    y_row_squares(0)
                    yield

                def up(i, b, side=iter(()), done=0):
                    stream(i, m.up(b)[1], 16, 1024, side, done)

                def down(i, b, half, side=iter(())):
                    stream(i, m.down(b, half)[1], 8, 1024, side)

                handover(f"f{l}")
                up(None, 0, side_operand(f"f{l}"), PREFILL)
                up(None, 1, hidden(None, 0))
                down(None, 0, 0, hidden(None, 1))
                down(None, 0, 1)
                with act.Fori(0, (BLOCKS - 2) // 2) as i:
                    for b in (1, 2):
                        up(i, b + 1)
                        down(i, b, 0, hidden(i, b + 1))
                        down(i, b, 1)
                down(None, BLOCKS - 1, 0)
                down(None, BLOCKS - 1, 1, side_last())
                if following:
                    prefill(following)
                y_row_squares(1)
                rstd_seed(f"pf{l}")

            gain_loads = [(gain_rows[0:16, :], mem_norm)]
            for n, (l, i) in enumerate([(0, 0), (0, 2), (0, 4), (1, 0), (1, 2), (1, 4)]):
                gain_loads.append((gain_rows[16 + 16 * n:32 + 16 * n, :], norms[l, i]))
            gain_loads += [(gain_rows[112:116, :], mla_q_norm[0]), (gain_rows[116:120, :], mla_kv_norm[0])]
            assert len(gain_loads) == GAIN_LOADS
            for to, source in gain_loads:
                act.dma_start(to, source.rearrange("(c p) -> c p", p=P)).then_inc(gain_rows_loaded, 16)
            act.wait_ge(turned_dve, TURNED_DVE["gain"] + 1)
            handover("mem")
            prefill("mem")

            def side_first():
                for pair in range(4, 8):
                    heads("mem", pair, operand_bank("mem", pair), gain=GAIN_COL["mem"])
                    yield
                for p in range(PIECES):
                    act.wait_ge(mem_loaded[p], 16)
                row_squares(rows, lambda t: (qT_a, kT_a)[t][:, :, :].rearrange("p h s -> p (h s)"))
                act.wait_ge(lam_ready, 1)
                nc.scalar.activation(lam[:, 2:4], lam[:, 0:2], ACT.Exp).then_inc(lam_exp, 1)
                yield
                rstd_seed("mem")
                for pair in range(8):
                    act.wait_ge(tile_used, 2 * pair + 2)
                    heads("a0", pair, operand_bank("mem", pair), gain=GAIN_COL["a0"])
                    yield
                act.wait_ge(rstd_ready, NORMS["mem"] + 1)
            stream_group("mem", side_first(), done=PREFILL)

            def side_memory():
                g = PLAN["mem"]
                finished(act, "mem")
                nc.scalar.activation(qT_b[:, 0:2, :].rearrange("p h s -> p (h s)"), PS[:, bank(g["index"], 0, 0), :], ACT.Copy,
                                     scale=rstd_pre[:, 0:1])
                nc.scalar.activation(mem_v[:, 0, :], PS[:, bank(g["index"], 1, 0), :], ACT.Copy, scale=rstd_pre[:, 0:1])\
                    .then_inc(evac_act, 1)
                yield
                yield
                turned("mem_k", mem_kT, side_of("fv"))
                yield
                row_squares(resid, lambda t: rows[:, t, :])
                yield
                rstd_seed("a0")
                yield
                act.wait_ge(rstd_ready, NORMS["a0"] + 1)
            stream_group("fv", side_memory())

            def side_value(name, to):
                evacuate(name, to[:, 0, :])
                yield
            stream_group("fg", side_value("fv", v_a))

            def side_gate():
                side = side_of("fq")
                evacuate("fg", gate_z[:, 0, :])
                yield
                act.wait_ge(gate_dve, 1)
                link(nc.scalar.activation(gate_a[:, :, :], gate_a[:, :, :], ACT.Exp))
                nc.scalar.activation(gate_a[:, :, :], gate_a[:, :, :], ACT.Ln, bias=1.0).then_inc(gate_act, 1)
                yield
                yield
                yield
                yield
                act.wait_ge(gate_pe, 2)
                nc.scalar.activation(key_cum[:, 0:4, :].rearrange("p (b h) k -> p b (h k)", h=2), PS[:, side:side + 2, :], ACT.Copy)\
                    .then_inc(key_cum_act, 1)
                yield
            stream_group("fq", side_gate())

            def side_turn(name, to, follow):
                evacuate(name, rows[:, 0, 1024:2048])
                yield
                yield
                turned(name, to, side_of(follow))
                yield

            stream_group("fk", side_turn("fq", qT_a, "fk"))
            stream_group("dq", side_turn("fk", kT_a, "dq"))
            stream_group("dk", chained(side_turn("dq", qT_b, "dk"), attend(units("fox", 0, FOX_FIRST), side_of("dk"))))
            stream_group("dv", chained(side_turn("dk", kT_b, "dv"), attend(units("fox", FOX_FIRST, 8), side_of("dv"))))
            mixer_out(("abo0", "abo1"), "dv", "diff", ("o0a", "o0b"), True, "pa0", "xq0")
            cross(0)
            mlp(0, "cqkv")

            handover("a1")
            stream_group("cqkv", side_operand("a1"), done=PREFILL)

            def side_latent():
                evacuate("cqkv", rows[:, 0, 0:1024])
                yield
            stream_group("kpe", side_latent())

            def side_low_rank():
                evacuate("kpe", rows[:, 0, 1024:1088])
                yield
                evacuated(act, "kpe")
                for c in range(2):
                    ins = nc.scalar.activation(v_b[:, c, 0:512], rows[:, 0, 512 * c:512 * c + 512], ACT.Square,
                                               accum_out=sumsq_c[:, c:c + 1])
                ins.then_inc(squares_act, 1)
                yield
                rstd_seed("c1", 4)
                yield
                yield
                yield
                for pair in range(4):
                    heads("c1", pair, side_of("mq") + pair, c_hi, GAIN_COL["q"])
                    yield
                act.wait_ge(rstd_ready, NORMS["c1"] + 1)
            stream_group("mq", side_low_rank())
            stream_group("uq0", side_turn("mq", qT_b, "uq0"))

            def side_query(name, first):
                evacuate(name, rows[:, 0, first:first + 768], rstd_c[:, 0:1])
                yield
            stream_group("uq1", side_query("uq0", 0))
            stream_group("ukv0", side_query("uq1", 768))

            def side_key_value(name, turn, n, follow):
                g = PLAN[name]
                finished(act, name)
                if n:
                    act.wait_ge(turn_done, TURNS["kn0"] + 2)
                for w, to in ((0, rows[:, 0, 1536:2048]), (1, v_a[:, 0, 512 * n:512 * n + 512])):
                    ins = nc.scalar.activation(to.rearrange("p (c h d) -> p c h d", c=2, h=2),
                                               sums(g["index"], 0, 1024).rearrange("p c (h w d) -> p c h w d", h=2, w=2)[:, :, :, w, :],
                                               ACT.Copy, scale=rstd_c[:, 1:2])
                ins.then_inc(evac_act, 1)
                yield
                yield
                turned(turn, kT_a[:, 4 * n:4 * n + 4, :], side_of(follow))
                yield
            stream_group("ukv1", side_key_value("ukv0", "kn0", 0, "ukv1"))

            def side_queries():
                yield
                turned("qn", qT_a, side_of("mk"))
                yield
                yield
                turned("qpe", qpeT, side_of("mk"))
                yield
            stream_group("mk", chained(side_key_value("ukv1", "kn1", 1, "mk"), side_queries(),
                                       attend(units("mla", 0, MLA_FIRST), side_of("mk"))))
            stream_group("mv", chained(side_turn("mk", kT_b, "mv"), attend(units("mla", MLA_FIRST, 8), side_of("mv"))))
            mixer_out(("cdo0", "cdo1"), "mv", "moba", ("o1a", "o1b"), False, "pa1", "xq1")
            cross(1)
            mlp(1, None)

        @block.vector
        def _(dve):
            chain = [0]

            def link(ins):
                chain[0] += 1
                ins.then_inc(dve_chain, 1)
                dve.wait_ge(dve_chain, chain[0])

            def stream(i, tile, count, cols, side=iter(()), done=0):
                for k in range(tile + done, tile + count):
                    dve.wait_ge(hi_ready, at(i, Mlp.TILES, k + 1))
                    nc.vector.tensor_tensor(w_lo[:, k % RING, 0:cols], raw[:, (k // 2) % RAW, (k % 2) * cols:(k % 2 + 1) * cols],
                                            w_hi[:, k % RING, 0:cols].bitcast(F32), ALU.subtract).then_inc(lo_ready, 1)
                    if k - tile >= LEAD:
                        next(side, None)
                for _ in side:
                    pass

            def stream_group(name, side=iter(()), first=0, count=None, done=0):
                g = PLAN[name]
                stream(None, g["tile"] + first, count or g["tiles"], g["per"] * g["width"], side, done)

            def prefill(name, first=0):
                if name.startswith("ffn"):
                    stream(None, PLAN[name]["tile"], PREFILL, TILE)
                else:
                    stream_group(name, first=first, count=PREFILL)

            def evacuate(name, to, scale=None):
                g = PLAN[name]
                finished(dve, name)
                nc.vector.tensor_scalar(like(to, g["width"]), sums(g["index"], 1, g["width"]),
                                        rstd_pre[:, 1:2] if scale is None else scale, None, ALU.mult).then_inc(evac_dve, 1)

            def turned(name, to, side):
                banks = dict(TURN_BANKS)[name]
                n = banks // 2
                dve.wait_ge(turn_done, TURNS[name] + banks)
                nc.vector.tensor_copy(to[:, 2 * n:2 * banks, :].rearrange("p (b c) s -> p b (c s)", c=2), PS[:, side + n:side + banks, :])\
                    .then_inc(turned_dve, 1)

            def rests(name, pair, b, hi=x_hi, lo=x_lo, gain=None):
                dve.wait_ge(split_hi, SPLITS[name] + pair + 1)
                c = 2 * pair
                if gain is None:
                    nc.vector.tensor_tensor(lo[:, c:c + 2, :].rearrange("p c s -> p (c s)"), PS[:, b, :],
                                            hi[:, c:c + 2, :].rearrange("p c s -> p (c s)").bitcast(F32), ALU.subtract)\
                        .then_inc(split_lo, 1)
                    return
                nc.vector.scalar_tensor_tensor(out=lo[:, c, :], in0=PS[:, b, 0:SEQ], scalar=gain_col[:, gain + c:gain + c + 1],
                                               in1=hi[:, c, :].bitcast(F32), op0=ALU.mult, op1=ALU.subtract)
                nc.vector.scalar_tensor_tensor(out=lo[:, c + 1, :], in0=PS[:, b, SEQ:2 * SEQ],
                                               scalar=gain_col[:, gain + c + 1:gain + c + 2],
                                               in1=hi[:, c + 1, :].bitcast(F32), op0=ALU.mult, op1=ALU.subtract)\
                    .then_inc(split_lo, 1)

            def squares(scratch, source, to):
                return nc.vector.tensor_tensor_reduce(scratch, source, source, 1.0, 0.0, ALU.mult, ALU.add, to)

            def refine(name, width, to):
                dve.wait_ge(seed_ready, NORMS[name] + 1)
                v, y, w = var[:, 0:width], seed[:, 0:width], newton[:, 0:width]
                link(nc.vector.tensor_tensor(w, y, y, ALU.mult))
                link(nc.vector.tensor_tensor(w, w, v, ALU.mult))
                link(nc.vector.tensor_scalar(w, w, -0.5, 1.5, ALU.mult, ALU.add))
                nc.vector.tensor_tensor(to, w, y, ALU.mult).then_inc(rstd_ready, 1)
                dve.wait_ge(rstd_ready, NORMS[name] + 1)

            def row_rstd(name, width, length, source, to):
                dve.wait_ge(squares_act, SQUARES[name] + 1)
                nc.vector.tensor_scalar(var[:, 0:width], source, 1.0 / length, EPS, ALU.mult, ALU.add).then_inc(var_ready, 1)
                refine(name, width, to)

            def post_rstd(name):
                nc.vector.scalar_tensor_tensor(out=var[:, 0:2], in0=sumsq_post[:, 2:4], scalar=1.0 / D, in1=post_base[:, :],
                                               op0=ALU.mult, op1=ALU.add).then_inc(var_ready, 1)
                refine(name, 2, rstd_post[:, :])

            def post_first():
                link(nc.vector.tensor_scalar(post_base[:, :], sumsq_post[:, 0:2], 1.0 / D, EPS, ALU.mult, ALU.add))

            def update(pieces):
                w = D // PIECES
                for p in pieces:
                    for t in range(HALVES):
                        h = resid[:, t, p * w:(p + 1) * w]
                        nc.vector.scalar_tensor_tensor(out=h, in0=rows[:, t, p * w:(p + 1) * w], scalar=rstd_post[:, t:t + 1], in1=h,
                                                       op0=ALU.mult, op1=ALU.add).then_inc(resid_ready, 1)

            def side_operand(name):
                for pair in range(4, 8):
                    rests(name, pair, operand_bank(name, pair), gain=GAIN_COL[name])
                    yield
                yield
                row_rstd(name, 2, D, sumsq_pre[:, :], rstd_pre[:, :])
                yield

            def handover(name):
                update((0, 1))
                for pair in range(4):
                    rests(name, pair, operand_bank(name, pair), gain=GAIN_COL[name])
                update((2, 3))

            def attend(us, side):
                for s in range(len(us) + 2):
                    if s < len(us):
                        a = us[s]
                        S, L = PS[:, side + a.u % 2, 0:a.cols], logit[:, a.u % 2, 0:a.cols]
                        dve.wait_ge(s_done, a.u + 1)
                        if a.u >= 2 and a.causal:
                            dve.wait_ge(pt_done, a.u - 1)
                        if a.family == "fox":
                            for t, col, keys in a.parts:
                                ins = nc.vector.scalar_tensor_tensor(
                                    out=logit[:, a.u % 2, col:col + keys], in0=key_cum[:, a.n, 0:keys], scalar=cum[:, t, a.n:a.n + 1],
                                    in1=mask[:, col:col + keys], op0=ALU.subtract, op1=ALU.subtract)
                            link(ins)
                            link(nc.vector.scalar_tensor_tensor(out=L, in0=S, scalar=SCALE, in1=L, op0=ALU.mult, op1=ALU.subtract))
                        elif a.family == "mla":
                            link(nc.vector.tensor_tensor(L, S, mask, ALU.add))
                        elif a.causal:
                            link(nc.vector.scalar_tensor_tensor(out=L, in0=dist, scalar=a.slope / SCALE, in1=S, op0=ALU.mult, op1=ALU.add))
                        source = L if a.causal else S
                        for t, col, keys in a.parts:
                            ins = nc.vector.tensor_reduce(top[:, a.u % 2, t:t + 1], source[:, col:col + keys], AX_X, ALU.max)
                        link(ins)
                        nc.vector.tensor_scalar(shift[:, a.u % 2, :], top[:, a.u % 2, :], -a.exp_scale, None, ALU.mult).then_inc(soft_ready, 1)
                    if s >= 2:
                        a = us[s - 2]
                        dve.wait_ge(o_done, a.u + 1)
                        link(nc.vector.reciprocal(inverse[:, a.u % 2, :], total[:, a.u % 4, :]))
                        minus = a.family == "diff" and a.n % 2
                        if minus:
                            link(nc.vector.tensor_scalar(inverse[:, a.u % 2, :], inverse[:, a.u % 2, :], lam[:, 4:5], None, ALU.mult))
                            dve.wait_ge(o_ready, a.u)
                        for t in range(HALVES):
                            O = PS[:, side + 3, t * a.dv:(t + 1) * a.dv]
                            if minus:
                                ins = nc.vector.scalar_tensor_tensor(out=a.o[:, t, :], in0=O, scalar=inverse[:, a.u % 2, t:t + 1],
                                                                     in1=a.o[:, t, :], op0=ALU.mult, op1=ALU.add)
                            else:
                                ins = nc.vector.tensor_scalar(a.o[:, t, :], O, inverse[:, a.u % 2, t:t + 1], None, ALU.mult)
                        ins.then_inc(o_ready, 1)
                    yield

            def gained(name, part, norm):
                g = PLAN[name]
                finished(dve, name)
                dve.wait_ge(gain_loaded, 16 * (POST_AT[norm] + 1))
                cols = slice(1024 * part, 1024 * (part + 1))
                for t in (1, 0):
                    if t == 0:
                        dve.wait_ge(evac_act, g["act"] + 1)
                    nc.vector.tensor_tensor(like(rows[:, t, cols], 1024), sums(g["index"], t, 1024), like(gain_row[:, cols], 1024),
                                            ALU.mult).then_inc(evac_dve, 1)

            def out_projection(names, norm, following):
                def side():
                    yield
                    gained(names[0], 0, norm)
                    yield
                    yield
                    dve.wait_ge(evac_act, PLAN[names[0]]["act"] + 2)
                    post_first()
                stream_group(names[1], side())
                prefill(following)
                gained(names[1], 1, norm)
                dve.wait_ge(evac_act, PLAN[names[1]]["act"] + 2)
                post_rstd(norm)

            def mixer_out(names, last_proj, family, o_names, sub, norm, following):
                first = names[0]
                prefill(first)
                evacuate(last_proj, v_b[:, 1, :])
                side = side_of(first)
                for pair in range(4):
                    rests(o_names[0], pair, side + pair)
                stream_group(first, attend(units(family), side), 0, 8, PREFILL)
                prefill(first, 8)
                if sub:
                    dve.wait_ge(o_ready, UNITS["diff"] + 8)
                    for h in range(DIFF_HEADS):
                        ins = squares(x_lo[:, 8 + h, :], rows[:, 1, FOX_W + 256 * h:FOX_W + 256 * (h + 1)], sumsq[:, 4 + h:5 + h])
                    link(ins)
                    row_rstd("sub", 8, 2 * HD, sumsq[:, 0:8], rstd_sub)
                    for t in range(HALVES):
                        for h in range(DIFF_HEADS):
                            part = rows[:, t, FOX_W + 256 * h:FOX_W + 256 * (h + 1)]
                            ins = nc.vector.scalar_tensor_tensor(out=part, in0=part, scalar=rstd_sub[:, 4 * t + h:4 * t + h + 1],
                                                                 in1=subln[:, :], op0=ALU.mult, op1=ALU.mult)
                    ins.then_inc(sub_scaled, 1)
                for pair in range(4):
                    rests(o_names[1], pair, side + pair, x_hi[:, 8:16, :], x_lo[:, 8:16, :])
                stream_group(first, first=8, count=8, done=PREFILL)
                out_projection(names, norm, following)

            def cross(l):
                handover(f"x{l}")
                stream_group(f"xq{l}", side_operand(f"x{l}"), done=PREFILL)
                prefill(f"xo{l}0")
                evacuate(f"xq{l}", rows[:, 1, 1024:1536])
                turned(f"xq{l}", kT_a, 4)
                for _ in attend(units(f"x{l}", 0, 4), 0):
                    pass
                for pair in range(2):
                    rests(f"xo{l}", pair, pair)
                stream_group(f"xo{l}0", done=PREFILL)
                out_projection((f"xo{l}0", f"xo{l}1"), f"px{l}", f"ffn{l}")

            def mlp(l, following):
                m = Mlp(l)

                def hidden(i, b):
                    g, tile = m.up(b)
                    dve.wait_ge(tile_used, at(i, Mlp.TILES, tile + 16))
                    if i is not None or b > 0:
                        dve.wait_ge(xturn_done, at(i, Mlp.SPLITS, m.s + 4 * b))
                    part = like(rows[:, 1, 0:1024], 1024)
                    nc.vector.tensor_scalar(part, sums(g, 1, 1024), rstd_pre[:, 1:2], 0.0, ALU.mult, ALU.max).then_inc(relu_dve, 1)
                    dve.wait_ge(relu_dve, at(i, Mlp.ACT, BLOCKS * l + b + 1))
                    nc.vector.tensor_tensor(part, part, part, ALU.mult).then_inc(evac_dve, 1)
                    yield
                    yield
                    for n in range(4):
                        dve.wait_ge(split_hi, at(i, Mlp.SPLITS, m.s + 4 * b + n + 1))
                        nc.vector.tensor_tensor(h_lo[b % 2][:, 2 * n:2 * n + 2, :].rearrange("p c s -> p (c s)"),
                                                PS[:, bank(g, 0, 0) + n, :],
                                                h_hi[b % 2][:, 2 * n:2 * n + 2, :].rearrange("p c s -> p (c s)").bitcast(F32),
                                                ALU.subtract).then_inc(split_lo, 1)
                        yield

                def accumulate(i, b, half):
                    g, tile = m.down(b, half)
                    dve.wait_ge(tile_used, at(i, Mlp.TILES, tile + 8))
                    if b:
                        dve.wait_ge(evac_dve, at(i, Mlp.DVE, m.y_dve(b, half)))
                    for t in range(HALVES):
                        y = like(y_acc[:, t, 1024 * half:1024 * (half + 1)], 1024)
                        nc.vector.tensor_tensor(y, y, sums(g, t, 1024), ALU.add).then_inc(evac_dve, 1)
                        yield

                def gained_sums(half):
                    dve.wait_ge(evac_dve, m.y_dve(BLOCKS - 1, half) + 2)
                    cols = slice(1024 * half, 1024 * (half + 1))
                    for t in range(HALVES):
                        nc.vector.tensor_tensor(rows[:, t, cols], y_acc[:, t, cols], gain_row[:, cols], ALU.mult).then_inc(y_gained, 1)

                def side_last():
                    yield from accumulate(None, BLOCKS - 1, 0)
                    dve.wait_ge(gain_loaded, 16 * (POST_AT[f"pf{l}"] + 1))
                    gained_sums(0)
                    yield
                    dve.wait_ge(y_squares, 2 * l + 1)
                    post_first()
                    yield

                def up(i, b, side=iter(()), done=0):
                    stream(i, m.up(b)[1], 16, 1024, side, done)

                def down(i, b, half, side=iter(())):
                    stream(i, m.down(b, half)[1], 8, 1024, side)

                def zero_sums():
                    for t in range(HALVES):
                        nc.vector.memset(y_acc[:, t, :], 0.0).then_inc(y_zero, 1)
                        yield
                    dve.wait_ge(y_zero, HALVES * (l + 1))

                handover(f"f{l}")
                up(None, 0, chained(side_operand(f"f{l}"), zero_sums()), PREFILL)
                up(None, 1, hidden(None, 0))
                down(None, 0, 0, hidden(None, 1))
                down(None, 0, 1, accumulate(None, 0, 0))
                with dve.Fori(0, (BLOCKS - 2) // 2) as i:
                    for b in (1, 2):
                        up(i, b + 1, accumulate(i, b - 1, 1))
                        down(i, b, 0, hidden(i, b + 1))
                        down(i, b, 1, accumulate(i, b, 0))
                down(None, BLOCKS - 1, 0, accumulate(None, BLOCKS - 2, 1))
                down(None, BLOCKS - 1, 1, side_last())
                if following:
                    prefill(following)
                for _ in accumulate(None, BLOCKS - 1, 1):
                    pass
                gained_sums(1)
                dve.wait_ge(y_squares, 2 * l + 2)
                dve.wait_ge(y_gained, 4 * l + 4)
                post_rstd(f"pf{l}")

            dve.wait_ge(turn_done, TURNS["gain"] + 1)
            nc.vector.tensor_copy(gain_col[:, :], PS[:, 0, 0:120]).then_inc(turned_dve, 1)
            dve.wait_ge(turned_dve, TURNED_DVE["gain"] + 1)
            for pair in range(4):
                rests("mem", pair, operand_bank("mem", pair), gain=GAIN_COL["mem"])
            prefill("mem")

            def side_first():
                for pair in range(4, 8):
                    rests("mem", pair, operand_bank("mem", pair), gain=GAIN_COL["mem"])
                    if pair == 6:
                        dve.wait_ge(small_loaded, 16 * SMALL_LOADS)
                        for n in range(2):
                            ins = nc.vector.tensor_tensor_reduce(logit[:, 0, n * HD:(n + 1) * HD], lam_rows[:, 2 * n * HD:(2 * n + 1) * HD],
                                                                 lam_rows[:, (2 * n + 1) * HD:(2 * n + 2) * HD], 1.0, 0.0, ALU.mult,
                                                                 ALU.add, lam[:, n:n + 1])
                        ins.then_inc(lam_ready, 1)
                        nc.vector.tensor_scalar(subln[:, :], subln[:, :], 1.0 - LAM_INIT, None, ALU.mult)
                    yield
                yield
                row_rstd("mem", 2, D, sumsq_pre[:, :], rstd_pre[:, :])
                dve.wait_ge(lam_exp, 1)
                link(nc.vector.tensor_tensor(lam[:, 4:5], lam[:, 3:4], lam[:, 2:3], ALU.subtract))
                link(nc.vector.tensor_scalar(lam[:, 4:5], lam[:, 4:5], -LAM_INIT, None, ALU.add))
                for pair in range(8):
                    rests("a0", pair, operand_bank("mem", pair), gain=GAIN_COL["a0"])
                    yield
            stream_group("mem", side_first(), done=PREFILL)

            def side_memory():
                g = PLAN["mem"]
                finished(dve, "mem")
                nc.vector.tensor_scalar(qT_b[:, 2:4, :].rearrange("p h s -> p (h s)"), PS[:, bank(g["index"], 0, 1), :],
                                        rstd_pre[:, 1:2], None, ALU.mult)
                nc.vector.tensor_scalar(mem_v[:, 1, :], PS[:, bank(g["index"], 1, 1), :], rstd_pre[:, 1:2], None, ALU.mult)\
                    .then_inc(evac_dve, 1)
                yield
                yield
                turned("mem_k", mem_kT, side_of("fv"))
                yield
                yield
                row_rstd("a0", 2, D, sumsq_pre[:, :], rstd_pre[:, :])
                yield
            stream_group("fv", side_memory())

            def side_value(name, to):
                evacuate(name, to[:, 1, :])
                yield
            stream_group("fg", side_value("fv", v_a))

            def side_gate():
                side = side_of("fq")
                evacuate("fg", gate_z[:, 1, :])
                yield
                evacuated(dve, "fg")
                for t in range(HALVES):
                    ins = nc.vector.tensor_tensor(gate_z[:, t, :], gate_z[:, t, :], b_f, ALU.add)
                link(ins)
                nc.vector.scalar_tensor_tensor(out=gate_a[:, :, :], in0=gate_z[:, :, :], scalar=-1.0, in1=gate_z[:, :, :],
                                               op0=ALU.mult, op1=ALU.min).then_inc(gate_dve, 1)
                dve.wait_ge(gate_act, 1)
                nc.vector.scalar_tensor_tensor(out=gate_l[:, :, :], in0=gate_z[:, :, :], scalar=0.0, in1=gate_a[:, :, :],
                                               op0=ALU.min, op1=ALU.subtract).then_inc(gate_dve, 1)
                yield
                dve.wait_ge(gate_pe, 1)
                nc.vector.tensor_copy(cum[:, :, :].rearrange("p t h -> p (t h)"), PS[:, side + 2, 0:16]).then_inc(gate_dve, 1)
                yield
                dve.wait_ge(turn_done, TURNS["cum"] + 1)
                nc.vector.tensor_copy(cumT, PS[0:8, side + 3, 0:SEQ]).then_inc(turned_dve, 1)
                yield
                yield
                dve.wait_ge(gate_pe, 2)
                nc.vector.tensor_copy(key_cum[:, 4:8, :].rearrange("p (b h) k -> p b (h k)", h=2), PS[:, side + 2:side + 4, :])\
                    .then_inc(gate_dve, 1)
                yield
                dve.wait_ge(key_cum_act, 1)
            stream_group("fq", side_gate())

            def side_turn(name, to, follow):
                evacuate(name, rows[:, 1, 1024:2048])
                yield
                yield
                turned(name, to, side_of(follow))
                yield

            stream_group("fk", side_turn("fq", qT_a, "fk"))
            stream_group("dq", side_turn("fk", kT_a, "dq"))
            stream_group("dk", chained(side_turn("dq", qT_b, "dk"), attend(units("fox", 0, FOX_FIRST), side_of("dk"))))
            stream_group("dv", chained(side_turn("dk", kT_b, "dv"), attend(units("fox", FOX_FIRST, 8), side_of("dv"))))
            mixer_out(("abo0", "abo1"), "dv", "diff", ("o0a", "o0b"), True, "pa0", "xq0")
            cross(0)
            mlp(0, "cqkv")

            handover("a1")
            stream_group("cqkv", side_operand("a1"), done=PREFILL)

            def side_latent():
                evacuate("cqkv", rows[:, 1, 0:1024])
                yield
            stream_group("kpe", side_latent())

            def rotate(source, to, t, heads, done):
                c = cos[:, t:t + 1, :].to_broadcast([P, heads, 32])
                s = sin[:, t:t + 1, :].to_broadcast([P, heads, 32])
                t1, t2 = source[:, :, 0:32], source[:, :, 32:64]
                a = logit[:, 0, 0:32 * heads].rearrange("p (h r) -> p h r", h=heads)
                b = logit[:, 1, 0:32 * heads].rearrange("p (h r) -> p h r", h=heads)
                nc.vector.tensor_tensor(a, t1, c, ALU.mult)
                link(nc.vector.tensor_tensor(b, t2, s, ALU.mult))
                link(nc.vector.tensor_tensor(to[:, :, 0:32], a, b, ALU.subtract))
                nc.vector.tensor_tensor(a, t2, c, ALU.mult)
                link(nc.vector.tensor_tensor(b, t1, s, ALU.mult))
                done(nc.vector.tensor_tensor(to[:, :, 32:64], a, b, ALU.add))

            def side_low_rank():
                evacuate("kpe", rows[:, 1, 1024:1088])
                yield
                evacuated(dve, "kpe")
                for t in range(HALVES):
                    source = rows[:, t, 1024:1088].rearrange("p (h r) -> p h r", h=1)
                    to = rows[:, t, 1088:1152].rearrange("p (h r) -> p h r", h=1)
                    rotate(source, to, t, 1, link)
                    ins = nc.vector.tensor_copy(rows[:, t, 1152:1216], rows[:, t, 1088:1152])
                ins.then_inc(rope_ready, 1)
                yield
                for c in range(2):
                    ins = squares(v_b[:, c, 512:1024], rows[:, 1, 512 * c:512 * c + 512], sumsq_c[:, 2 + c:3 + c])
                link(ins)
                row_rstd("c1", 4, 512, sumsq_c[:, :], rstd_c[:, :])
                yield
                dve.wait_ge(turn_done, TURNS["kpe"] + 1)
                nc.vector.tensor_copy(kpeT[:, :], PS[:, side_of("mq"), 0:SEQ]).then_inc(turned_dve, 1)
                yield
                yield
                for pair in range(4):
                    rests("c1", pair, side_of("mq") + pair, c_hi, c_lo, GAIN_COL["q"])
                    yield
            stream_group("mq", side_low_rank())
            stream_group("uq0", side_turn("mq", qT_b, "uq0"))

            def side_query(name, first):
                evacuate(name, rows[:, 1, first:first + 768], rstd_c[:, 2:3])
                yield
            stream_group("uq1", side_query("uq0", 0))
            stream_group("ukv0", side_query("uq1", 768))

            def side_key_value(name, turn, n, follow):
                g = PLAN[name]
                finished(dve, name)
                if n:
                    dve.wait_ge(turn_done, TURNS["kn0"] + 2)
                for w, to in ((0, rows[:, 1, 1536:2048]), (1, v_a[:, 1, 512 * n:512 * n + 512])):
                    ins = nc.vector.tensor_scalar(to.rearrange("p (c h d) -> p c h d", c=2, h=2),
                                                  sums(g["index"], 1, 1024).rearrange("p c (h w d) -> p c h w d", h=2, w=2)[:, :, :, w, :],
                                                  rstd_c[:, 3:4], None, ALU.mult)
                ins.then_inc(evac_dve, 1)
                yield
                yield
                turned(turn, kT_a[:, 4 * n:4 * n + 4, :], side_of(follow))
                yield
            stream_group("ukv1", side_key_value("ukv0", "kn0", 0, "ukv1"))

            def side_queries():
                evacuated(dve, "uq1")
                for t in range(HALVES):
                    source = rows[:, t, 0:8 * MLA_QK].rearrange("p (h w) -> p h w", w=MLA_QK)[:, :, HD:MLA_QK]
                    to = prob[:, t, :].rearrange("p (h r) -> p h r", h=8)
                    rotate(source, to, t, 8, lambda ins: ins.then_inc(rope_ready, 1))
                    dve.wait_ge(rope_ready, 2 + t)
                yield
                turned("qn", qT_a, side_of("mk"))
                yield
                yield
                turned("qpe", qpeT, side_of("mk"))
                yield
            stream_group("mk", chained(side_key_value("ukv1", "kn1", 1, "mk"), side_queries(),
                                       attend(units("mla", 0, MLA_FIRST), side_of("mk"))))
            stream_group("mv", chained(side_turn("mk", kT_b, "mv"), attend(units("mla", MLA_FIRST, 8), side_of("mv"))))
            mixer_out(("cdo0", "cdo1"), "mv", "moba", ("o1a", "o1b"), False, "pa1", "xq1")
            cross(1)
            mlp(1, None)
            update(range(PIECES))

        @block.tensor
        def _(pe):
            def products(i, tile, count, group, per, width, chunks, hi, lo, operand=None, first=0, side=iter(())):
                for k in range(count):
                    pe.wait_ge(hi_ready, at(i, Mlp.TILES, tile + k + 1))
                    pe.wait_ge(lo_ready, at(i, Mlp.TILES, tile + k + 1))
                    slot = (tile + k) % RING
                    for j in range(per):
                        ch = first + k * per + j
                        if operand is not None:
                            operand(ch)
                        start, stop = ch == 0, ch == chunks - 1
                        for t in range(HALVES):
                            xh, xl = hi[:, ch, t * P:(t + 1) * P], lo[:, ch, t * P:(t + 1) * P]
                            for x_part, w_part, a, z in ((xh, w_hi, start, False), (xh, w_lo, False, False), (xl, w_hi, False, stop)):
                                for c, (col, w) in enumerate(col_banks(width)):
                                    mm = nc.tensor.matmul(PS[:, bank(group, c, t), 0:w], x_part,
                                                          w_part[:, slot, j * width + col:j * width + col + w], start=a, stop=z)
                    mm.then_inc(tile_used, 1)
                    next(side, None)
                for _ in side:
                    pass

            def stream_group(name, side=iter(()), operand=None, first=0, count=None, hi=x_hi, lo=x_lo):
                g = PLAN[name]
                products(None, g["tile"] + first, count or g["tiles"], g["index"], g["per"], g["width"], g["chunks"],
                         hi, lo, operand, first * g["per"], side)

            def operand_of(name, base=0):
                def operand(ch):
                    if ch % 2 == 0 and ch >= base:
                        split(pe, name, (ch - base) // 2 + 1)
                return operand

            def turn_bank(b, source, chunks):
                for j in chunks:
                    for t in range(HALVES):
                        mm = nc.tensor.transpose(PS[:, b, (j % 2) * SEQ + t * P:(j % 2) * SEQ + (t + 1) * P], source(j, t), ident)
                return mm

            def turn(name, source, side):
                for b in range(dict(TURN_BANKS)[name]):
                    turn_bank(side + b, source, (2 * b, 2 * b + 1)).then_inc(turn_done, 1)

            def row_chunk(first, step=P):
                return lambda j, t: rows[:, t, first + j * step:first + j * step + P]

            def turn_pair(name, pair, source):
                turn_bank(operand_bank(name, pair), source, (2 * pair, 2 * pair + 1)).then_inc(xturn_done, 1)

            def resid_chunk(j, t):
                return resid[:, t, j * P:(j + 1) * P]

            def updated(name, pair):
                pe.wait_ge(resid_ready, 2 * PIECES * POST_AT[BEFORE[name]] + 2 * (pair // 2) + 2)

            def handover(name):
                for pair in range(4):
                    updated(name, pair)
                    turn_pair(name, pair, resid_chunk)

            def side_operand(name):
                for pair in range(4, 8):
                    updated(name, pair)
                    split(pe, name, pair - 3)
                    turn_pair(name, pair, resid_chunk)
                    yield

            def attend(us, side):
                for s in range(len(us) + 2):
                    if s < len(us):
                        a = us[s]
                        if a.u >= 2:
                            pe.wait_ge(p_ready, a.u - 1)
                        for t, col, keys in a.parts:
                            S = PS[:, side + a.u % 2, col:col + keys]
                            mla = a.family == "mla"
                            mm = nc.tensor.matmul(S, a.q[:, t * P:(t + 1) * P], a.k[:, 0:keys], start=True, stop=not mla)
                            if mla:
                                mm = nc.tensor.matmul(S, a.qpe[:, t * P:(t + 1) * P], a.kpe[:, 0:keys], start=False, stop=True)
                        mm.then_inc(s_done, 1)
                    if 1 <= s <= len(us):
                        a = us[s - 1]
                        pe.wait_ge(p_ready, a.u + 1)
                        if a.u:
                            pe.wait_ge(pt_ready, a.u)
                        for col in range(0, a.cols, P):
                            mm = nc.tensor.transpose(PS[:, side + 2, col:col + P], logit[:, a.u % 2, col:col + P], ident)
                        mm.then_inc(pt_done, 1)
                    if s >= 2:
                        a = us[s - 2]
                        pe.wait_ge(pt_ready, a.u + 1)
                        if a.u:
                            pe.wait_ge(o_ready, a.u)
                        for t, col, keys in a.parts:
                            for n in range(keys // P):
                                mm = nc.tensor.matmul(PS[:, side + 3, t * a.dv:(t + 1) * a.dv],
                                                      prob[:, a.u % 2, col + n * P:col + (n + 1) * P], a.v[:, n, :],
                                                      start=n == 0, stop=n == keys // P - 1)
                        mm.then_inc(o_done, 1)
                    yield

            def side_turn(name, follow):
                yield
                evacuated(pe, name)
                turn(name, row_chunk(1024), side_of(follow))
                yield
                yield

            def mixer_out(names, last_proj, first_family, family, o_names, sub):
                first, second = names
                side = side_of(first)
                evacuated(pe, last_proj)
                pe.wait_ge(o_ready, UNITS[first_family] + 8)
                for c in range(0, 8, 2):
                    turn_bank(side + c // 2, row_chunk(0), (c, c + 1)).then_inc(xturn_done, 1)

                def attend_after_split():
                    split(pe, o_names[0], 4)
                    yield from attend(units(family), side)
                stream_group(first, attend_after_split(), operand_of(o_names[0]), 0, 8)
                if sub:
                    pe.wait_ge(sub_scaled, 1)
                else:
                    pe.wait_ge(o_ready, UNITS[family] + 8)
                for c in range(0, 8, 2):
                    turn_bank(side + c // 2, row_chunk(1024), (c, c + 1)).then_inc(xturn_done, 1)
                stream_group(first, operand=operand_of(o_names[1], 8), first=8, count=8)
                stream_group(second)

            def cross(l):
                handover(f"x{l}")
                evacuated(pe, "abo0" if l == 0 else "cdo0")
                stream_group(f"xq{l}", side_operand(f"x{l}"), operand_of(f"x{l}"))
                evacuated(pe, f"xq{l}")
                turn(f"xq{l}", row_chunk(1024), 4)
                turns_evacuated(pe, f"xq{l}")
                for _ in attend(units(f"x{l}", 0, 4), 0):
                    pass
                pe.wait_ge(o_ready, UNITS[f"x{l}"] + 4)
                for c in (0, 2):
                    turn_bank(c // 2, row_chunk(0), (c, c + 1)).then_inc(xturn_done, 1)
                stream_group(f"xo{l}0", operand=operand_of(f"xo{l}"))
                stream_group(f"xo{l}1")

            def mlp(l):
                m = Mlp(l)

                def hidden(i, b):
                    yield
                    pe.wait_ge(evac_act, at(i, Mlp.ACT, m.a + b + 1))
                    pe.wait_ge(evac_dve, at(i, Mlp.DVE, m.hid_dve(b) + 1))
                    for n in range(4):
                        turn_bank(bank(m.up(b)[0], 0, 0) + n, row_chunk(0), (2 * n, 2 * n + 1)).then_inc(xturn_done, 1)
                    yield

                def up(i, b, side=iter(()), operand=None):
                    g, tile = m.up(b)
                    products(i, tile, 16, g, 1, 1024, CH, x_hi, x_lo, operand, 0, side)

                def down(i, b, half, side=iter(())):
                    g, tile = m.down(b, half)
                    products(i, tile, 8, g, 1, 1024, 8, h_hi[b % 2], h_lo[b % 2], None, 0, side)

                def sums_free(i, b, half):
                    pe.wait_ge(evac_dve, at(i, Mlp.DVE, m.y_dve(b, half) + 2))

                def hidden_split(i, b):
                    pe.wait_ge(split_hi, at(i, Mlp.SPLITS, m.s + 4 * b + 4))
                    pe.wait_ge(split_lo, at(i, Mlp.SPLITS, m.s + 4 * b + 4))

                handover(f"f{l}")
                evacuated(pe, f"xo{l}0")
                up(None, 0, side_operand(f"f{l}"), operand_of(f"f{l}"))
                up(None, 1, hidden(None, 0))
                hidden_split(None, 0)
                down(None, 0, 0, hidden(None, 1))
                hidden_split(None, 1)
                down(None, 0, 1)
                with pe.Fori(0, (BLOCKS - 2) // 2) as i:
                    for b in (1, 2):
                        sums_free(i, b - 1, 0)
                        up(i, b + 1)
                        sums_free(i, b - 1, 1)
                        down(i, b, 0, hidden(i, b + 1))
                        hidden_split(i, b + 1)
                        down(i, b, 1)
                sums_free(None, BLOCKS - 2, 0)
                down(None, BLOCKS - 1, 0)
                sums_free(None, BLOCKS - 2, 1)
                down(None, BLOCKS - 1, 1)

            pe.wait_ge(const_loaded, 16)
            pe.wait_ge(gain_rows_loaded, 16 * GAIN_LOADS)
            nc.tensor.transpose(PS[:, 0, 0:120], gain_rows[:, :], ident[0:120, 0:120]).then_inc(turn_done, 1)

            def mem_pair(pair):
                pe.wait_ge(mem_loaded[pair // 2], 16)
                turn_pair("mem", pair, row_chunk(0))

            for pair in range(4):
                mem_pair(pair)

            def side_first():
                for pair in range(4, 8):
                    split(pe, "mem", pair - 3)
                    mem_pair(pair)
                    yield
                yield
                pe.wait_ge(x_loaded, 16)
                for pair in range(8):
                    if pair < 4:
                        split(pe, "mem", pair + 5)
                    else:
                        split(pe, "a0", pair - 3)
                    turn_pair("mem", pair, resid_chunk)
                    yield
            pe.wait_ge(turned_dve, TURNED_DVE["gain"] + 1)
            stream_group("mem", side_first(), operand_of("mem"))

            split(pe, "a0", 8)

            def side_memory():
                yield
                evacuated(pe, "mem")
                turn("mem_k", lambda j, t: qT_b[:, 2 * t:2 * t + 2, :].rearrange("p h s -> p (h s)")[:, j * P:(j + 1) * P], side_of("fv"))
                yield
                yield
            stream_group("fv", side_memory())
            turns_evacuated(pe, "mem_k")
            stream_group("fg")
            evacuated(pe, "fv")

            def side_gate():
                side = side_of("fq")
                evacuated(pe, "fg")
                yield
                yield
                pe.wait_ge(gate_dve, 2)
                nc.tensor.matmul(PS[:, side + 2, 0:8], tri, gate_l[:, 0, :], start=True, stop=True)
                nc.tensor.matmul(PS[:, side + 2, 8:16], ones, gate_l[:, 0, :], start=True, stop=False)
                nc.tensor.matmul(PS[:, side + 2, 8:16], tri, gate_l[:, 1, :], start=False, stop=True).then_inc(gate_pe, 1)
                yield
                pe.wait_ge(gate_dve, 3)
                for t in range(HALVES):
                    mm = nc.tensor.transpose(PS[0:8, side + 3, t * P:(t + 1) * P], cum[:, t, :], ident)
                mm.then_inc(turn_done, 1)
                yield
                turns_evacuated(pe, "cum")
                for h in range(8):
                    mm = nc.tensor.matmul(PS[:, side + h // 2, (h % 2) * SEQ:(h % 2 + 1) * SEQ],
                                          ident[0:8, h:h + 1].to_broadcast([8, P]), cumT, start=True, stop=True)
                mm.then_inc(gate_pe, 1)
                yield
            stream_group("fq", side_gate())
            pe.wait_ge(key_cum_act, 1)
            pe.wait_ge(gate_dve, 4)
            stream_group("fk", side_turn("fq", "fk"))
            turns_evacuated(pe, "fq")
            stream_group("dq", side_turn("fk", "dq"))
            turns_evacuated(pe, "fk")
            stream_group("dk", chained(side_turn("dq", "dk"), wait_then(lambda: turns_evacuated(pe, "dq"),
                                                                          attend(units("fox", 0, FOX_FIRST), side_of("dk")))))
            pe.wait_ge(o_ready, UNITS["fox"] + FOX_FIRST)
            stream_group("dv", chained(side_turn("dk", "dv"), wait_then(lambda: turns_evacuated(pe, "dk"),
                                                                          attend(units("fox", FOX_FIRST, 8), side_of("dv")))))
            mixer_out(("abo0", "abo1"), "dv", "fox", "diff", ("o0a", "o0b"), True)
            cross(0)
            mlp(0)

            handover("a1")
            pe.wait_ge(evac_dve, Mlp(0).y_dve(BLOCKS - 1, 0) + 2)
            stream_group("cqkv", side_operand("a1"), operand_of("a1"))
            pe.wait_ge(evac_dve, Mlp(0).y_dve(BLOCKS - 1, 1) + 2)
            stream_group("kpe")
            evacuated(pe, "cqkv")

            def side_low_rank():
                yield
                yield
                pe.wait_ge(rope_ready, 1)
                for t in range(HALVES):
                    mm = nc.tensor.transpose(PS[:, side_of("mq"), t * P:(t + 1) * P], rows[:, t, 1088:1216], ident)
                mm.then_inc(turn_done, 1)
                yield
                yield
                turns_evacuated(pe, "kpe")
                for c in range(0, 8, 2):
                    turn_bank(side_of("mq") + c // 2, row_chunk(0), (c, c + 1)).then_inc(xturn_done, 1)
                yield
            stream_group("mq", side_low_rank())
            split(pe, "c1", 4)
            stream_group("uq0", side_turn("mq", "uq0"), hi=c_hi, lo=c_lo)
            turns_evacuated(pe, "mq")
            stream_group("uq1", hi=c_hi, lo=c_lo)
            evacuated(pe, "uq0")
            stream_group("ukv0", hi=c_hi[:, 4:8, :], lo=c_lo[:, 4:8, :])
            evacuated(pe, "uq1")

            def side_key(name, turn_name, follow):
                yield
                evacuated(pe, name)
                turn(turn_name, row_chunk(1536), side_of(follow))
                yield
                yield
            stream_group("ukv1", side_key("ukv0", "kn0", "ukv1"), hi=c_hi[:, 4:8, :], lo=c_lo[:, 4:8, :])
            turns_evacuated(pe, "kn0")

            def side_queries():
                turns_evacuated(pe, "kn1")
                turn("qn", row_chunk(0, MLA_QK), side_of("mk"))
                yield
                yield
                turns_evacuated(pe, "qn")
                pe.wait_ge(rope_ready, 3)
                turn("qpe", lambda j, t: prob[:, t, j * P:(j + 1) * P], side_of("mk"))
                yield
                yield
            stream_group("mk", chained(side_key("ukv1", "kn1", "mk"), side_queries(),
                                       wait_then(lambda: turns_evacuated(pe, "qpe"),
                                                 attend(units("mla", 0, MLA_FIRST), side_of("mk")))))
            pe.wait_ge(o_ready, UNITS["mla"] + MLA_FIRST)
            stream_group("mv", chained(side_turn("mk", "mv"), wait_then(lambda: turns_evacuated(pe, "mk"),
                                                                          attend(units("mla", MLA_FIRST, 8), side_of("mv")))))
            mixer_out(("cdo0", "cdo1"), "mv", "mla", "moba", ("o1a", "o1b"), False)
            cross(1)
            mlp(1)


def shape_constants():
    c = np.zeros((P, C_END), np.float32)
    row, col = np.arange(P)[:, None], np.arange(P)[None, :]
    c[:, C_ID:C_TRI] = row == col
    c[:, C_TRI:C_ONE] = row <= col
    c[:, C_ONE:C_DIST] = 1.0
    q = np.concatenate([np.broadcast_to(row, (P, P)), np.broadcast_to(row + P, (P, 2 * P))], 1)
    k = np.concatenate([np.arange(P), np.arange(2 * P)])[None, :]
    c[:, C_DIST:C_MASK] = np.where(k <= q, k - q, MASKED)
    c[:, C_MASK:C_COS] = np.where(k <= q, 0.0, MASKED)
    inv = np.float32(10000.0) ** (-np.arange(0, MLA_ROPE, 2, dtype=np.float32) / np.float32(MLA_ROPE))
    angle = np.arange(SEQ, dtype=np.float32)[:, None] * inv[None, :]
    for at0, f in ((C_COS, np.cos), (C_SIN, np.sin)):
        c[:, at0:at0 + 64] = f(angle).astype(np.float32).reshape(HALVES, P, 32).transpose(1, 0, 2).reshape(P, 64)
    return c


_INS = ["x", "mem", "mem_norm", "mem_wkv", "norms", "xattn_wq", "xattn_wo", "ffn_w1", "ffn_w2", "ab_w_in", "ab_w_out",
        "fox_b_f", "diff_lambda", "diff_subln", "cd_w_in", "cd_w_out", "mla_q_norm", "mla_kv_norm", "mla_w_uq", "mla_w_ukv"]


def kernel(**inputs):
    import concourse.bacc as _bacc
    from concourse import mybir as _mybir
    from concourse.bass_utils import run_bass_kernel_spmd as _run

    nc = _bacc.Bacc("TRN2", target_bir_lowering=False, num_devices=1)
    arrays, args = {}, []
    for name in _INS + ["consts"]:
        a = np.ascontiguousarray(inputs[name]) if name != "consts" else shape_constants()
        arrays[f"in_{name}_dram"] = a
        args.append(nc.dram_tensor(f"in_{name}_dram", a.shape, _mybir.dt.from_np(a.dtype), kind="ExternalInput").ap())
    args.append(nc.dram_tensor("out_0_dram", (1, SEQ, D), F32, kind="ExternalOutput").ap())
    trunk(nc, *args)
    r = _run(nc, [arrays], core_ids=[0])
    return r.results[0]["out_0_dram"]
```

```python
from contextlib import ExitStack
import math

import numpy as np

import concourse.bass as bass
from concourse import mybir

F32 = mybir.dt.float32
F32R = mybir.dt.float32r
ALU = mybir.AluOpType
ACT = mybir.ActivationFunctionType
AX_X = mybir.AxisListType.X

P = 128
SEQ = 256
HALVES = SEQ // P
D = 2048
CH = D // P
FFN = 4 * D
BLOCKS = FFN // 1024
EPS = 1e-6
HD = 128
FOX_W = 1024
DIFF_HEADS = 4
MLA_ROPE = 64
MLA_QK = HD + MLA_ROPE
MEM_LEN = 256
XW = 512
SCALE = HD ** -0.5
MLA_SCALE = MLA_QK ** -0.5
LAM_INIT = 0.8 - 0.6 * math.exp(0.0)
MASKED = -1e36

RAW = 4
RING = 4
TILE = 1024
LEAD = 3

C_ID, C_TRI, C_ONE, C_DIST, C_MASK, C_COS, C_SIN, C_END = np.cumsum([0, 128, 128, 128, 384, 384, 64, 64]).tolist()

GROUPS = [
    ("mem", 16, 1, 1024),
    ("fv", 16, 1, 1024), ("fg", 16, 8, 8), ("fq", 16, 1, 1024), ("fk", 16, 1, 1024),
    ("dq", 16, 1, 1024), ("dk", 16, 1, 1024), ("dv0", 16, 2, 512), ("dv1", 16, 2, 512),
    ("abo0", 16, 1, 1024), ("abo1", 16, 1, 1024),
    ("xq0", 16, 2, 512), ("xo00", 4, 1, 1024), ("xo01", 4, 1, 1024),
    ("ffn0", None, None, None),
    ("cqkv", 16, 1, 1024), ("kpe", 16, 8, 64), ("mq", 16, 1, 1024),
    ("uq0", 4, 1, 768), ("uq1", 4, 1, 768), ("ukv0", 4, 1, 1024), ("ukv1", 4, 1, 1024),
    ("mk", 16, 1, 1024), ("mv", 16, 1, 1024),
    ("cdo0", 16, 1, 1024), ("cdo1", 16, 1, 1024),
    ("xq1", 16, 2, 512), ("xo10", 4, 1, 1024), ("xo11", 4, 1, 1024),
    ("ffn1", None, None, None),
]
OUT_GROUPS = ("abo0", "abo1", "cdo0", "cdo1", "xo00", "xo01", "xo10", "xo11")
NARROW_GROUPS = ("fg", "kpe")
FFN_GROUPS = 3 * BLOCKS
FFN_TILES = BLOCKS * (16 + 2 * 8)


def col_banks(width):
    n = -(-width // 512)
    return [(c * (width // n), width // n) for c in range(n)]


def plan_groups():
    plan, index, tile, act, dve = {}, 0, 0, 0, 0
    for name, chunks, per, width in GROUPS:
        plan[name] = dict(index=index, tile=tile, chunks=chunks, per=per, width=width, act=act, dve=dve)
        if chunks is None:
            index, tile = index + FFN_GROUPS, tile + FFN_TILES
            act, dve = act + BLOCKS, dve + 5 * BLOCKS
        else:
            n = 2 if name in OUT_GROUPS else 1
            n_act = 0 if name in NARROW_GROUPS else n
            plan[name].update(tiles=chunks // per, evacs_act=n_act, evacs_dve=n)
            index, tile, act, dve = index + 1, tile + chunks // per, act + n_act, dve + n
    return plan


def running(items):
    at, out = 0, {}
    for name, n in items:
        out[name] = at
        at += n
    return out


PLAN = plan_groups()
SPLITS = running([("mem", 8), ("a0", 8), ("o0a", 4), ("o0b", 4), ("x0", 8), ("xo0", 2), ("f0", 8), ("h0", 4 * BLOCKS),
                  ("a1", 8), ("c1", 4), ("o1a", 4), ("o1b", 4), ("x1", 8), ("xo1", 2), ("f1", 8), ("h1", 4 * BLOCKS)])
TURN_BANKS = [("gain", 1), ("mem_k", 2), ("fg", 1), ("cum", 1), ("fq", 4), ("fk", 4), ("dq", 4), ("dk", 4), ("xq0", 2),
              ("kpe_rows", 1), ("kpe", 1), ("mq", 4), ("kn0", 2), ("kn1", 2), ("qn", 4), ("qpe", 2), ("mk", 4), ("xq1", 2)]
TURNS = running(TURN_BANKS)


def turned_by(name):
    return int(dict(TURN_BANKS)[name] > 1), 1


TURNED_ACT = running([(n, turned_by(n)[0]) for n, _ in TURN_BANKS])
TURNED_DVE = running([(n, turned_by(n)[1]) for n, _ in TURN_BANKS])
UNITS = running([("fox", 8), ("diff", 8), ("x0", 4), ("mla", 8), ("moba", 8), ("x1", 4)])
NORMS = running([(n, 1) for n in ("mem", "a0", "sub", "pa0", "x0", "px0", "f0", "pf0",
                                  "a1", "c1", "pa1", "x1", "px1", "f1", "pf1")])
SQUARES = running([(n, 1) for n in ("mem", "a0", "sub", "x0", "f0", "a1", "c1", "x1", "f1")])
GAIN_COL = {"mem": 0, "a0": 16, "x0": 32, "f0": 48, "a1": 64, "x1": 80, "f1": 96, "q": 112, "kv": 116}
POST = {"pa0": (0, 1), "px0": (0, 3), "pf0": (0, 5), "pa1": (1, 1), "px1": (1, 3), "pf1": (1, 5)}
POST_AT = {n: i for i, n in enumerate(POST)}
BEFORE = {"x0": "pa0", "f0": "px0", "a1": "pf0", "x1": "pa1", "f1": "px1"}
SMALL_LOADS, GAIN_LOADS = 3, 4
FOX_FIRST, MLA_FIRST = 7, 2
DIFF_FIRST = 4
NEXT_GROUP = {"mem": "mem", "x0": "xq0", "f0": "ffn0", "a1": "cqkv", "x1": "xq1", "f1": "ffn1"}
WARM = {"pa": 5, "px": 6, "pf": 8, "sub": 5}
PIECES = 4
UPDATES = [(0, 256), (256, 512), (512, 1024), (1024, 1536), (1536, 2048)]
PREFILL = 3


def updates_with(col, post):
    return 2 * len(UPDATES) * POST_AT[post] + 2 * sum(a < col for a, _ in UPDATES)


def at(i, per, static):
    return static if i is None else i * per + static


class Mlp:
    TILES, SPLITS, ACT, DVE = 64, 8, 2, 10

    def __init__(self, l):
        g = PLAN[f"ffn{l}"]
        self.l, self.g, self.t, self.a, self.v, self.s = l, g["index"], g["tile"], g["act"], g["dve"], SPLITS[f"h{l}"]

    def up(self, b):
        return (self.g + b, self.t + 16 * b) if b < 2 else (self.g + 3 * b - 2, self.t + 32 * b - 16)

    def down(self, b, half):
        if b == 0:
            return self.g + 2 + half, self.t + 32 + 8 * half
        if b == BLOCKS - 1:
            return self.g + 3 * b + 1 + half, self.t + 32 * b + 16 + 8 * half
        return self.g + 3 * b + 2 + half, self.t + 32 * b + 32 + 8 * half

    def hid_dve(self, b):
        return self.v + (0 if b == 0 else 5 * b - 4)

    def y_dve(self, b, half):
        return self.v + (5 * b + 2 if b < BLOCKS - 1 else 5 * b + 1) + 2 * half


def trunk(nc, x, mem, mem_norm, mem_wkv, norms, xattn_wq, xattn_wo, ffn_w1, ffn_w2, ab_w_in, ab_w_out,
          fox_b_f, diff_lambda, diff_subln, cd_w_in, cd_w_out, mla_q_norm, mla_kv_norm, mla_w_uq, mla_w_ukv,
          consts, out):
    AB, CD = ab_w_in[0], cd_w_in[0]
    weights = {
        "mem": (mem_wkv, 0),
        "fq": (AB, 0), "fk": (AB, 1024), "fv": (AB, 2048), "fg": (AB, 3072),
        "dq": (AB, 3080), "dk": (AB, 4104), "dv0": (AB, 5128), "dv1": (AB, 5640),
        "abo0": (ab_w_out[0], 0), "abo1": (ab_w_out[0], 1024),
        "kpe": (CD, 1024), "cqkv": (CD, 0), "mq": (CD, 1088), "mk": (CD, 2112), "mv": (CD, 3136),
        "uq0": (mla_w_uq[0], 0), "uq1": (mla_w_uq[0], 768), "ukv0": (mla_w_ukv[0], 0), "ukv1": (mla_w_ukv[0], 1024),
        "cdo0": (cd_w_out[0], 0), "cdo1": (cd_w_out[0], 1024),
    }
    for l in range(2):
        weights |= {f"xq{l}": (xattn_wq[l], 0), f"xo{l}0": (xattn_wo[l], 0), f"xo{l}1": (xattn_wo[l], 1024)}

    with ExitStack() as ctx:
        def sb(name, shape, dt=F32, own=ctx):
            return own.enter_context(nc.sbuf_tensor(name, shape, dt))

        def sem(name):
            return ctx.enter_context(nc.semaphore(name))

        PS = ctx.enter_context(nc.psum_tensor("PS", [P, 8, 512], F32))
        resid = sb("resid", [P, HALVES, D])
        x_hi = sb("x_hi", [P, CH, SEQ], F32R)
        x_lo = sb("x_lo", [P, CH, SEQ], F32R)
        rows = sb("rows", [P, HALVES, D])
        raw = sb("raw", [P, RAW, 2 * TILE])
        w_hi = sb("w_hi", [P, RING, TILE], F32R)
        w_lo = sb("w_lo", [P, RING, TILE], F32R)
        const = sb("const", [P, C_END])
        mem_kT = sb("mem_kT", [P, 4, MEM_LEN])
        mem_v = sb("mem_v", [P, HALVES, XW])
        gain_rows = sb("gain_rows", [120, P])
        gain_col = sb("gain_col", [P, 120])
        small = sb("small", [P, 192])
        subln = sb("subln", [P, 2 * HD])
        with ExitStack() as mixer:
            qT_a = sb("qT_a", [P, 8, SEQ], own=mixer)
            kT_a = sb("kT_a", [P, 8, SEQ], own=mixer)
            v_a = sb("v_a", [P, HALVES, 1024], own=mixer)
            qT_b = sb("qT_b", [P, 8, SEQ], own=mixer)
            kT_b = sb("kT_b", [P, 8, SEQ], own=mixer)
            v_b = sb("v_b", [P, HALVES, 1024], own=mixer)
            logit = sb("logit", [P, 2, 512], own=mixer)
            prob = sb("prob", [P, 2, 512], own=mixer)
            qpeT = sb("qpeT", [P, 4, SEQ], own=mixer)
            kpeT = sb("kpeT", [P, SEQ], own=mixer)
        with ExitStack() as low_rank:
            sb("gap_q", [P, 4, 8 * SEQ], own=low_rank)
            c_hi = sb("c_hi", [P, 8, SEQ], F32R, own=low_rank)
            c_lo = sb("c_lo", [P, 8, SEQ], F32R, own=low_rank)
        with ExitStack() as mlp:
            gain_row = sb("gain_row", [P, D], own=mlp)
            y_acc = sb("y_acc", [P, HALVES, D], own=mlp)
            h_hi = [sb(f"h_hi{i}", [P, 8, SEQ], F32R, own=mlp) for i in range(2)]
            h_lo = [sb(f"h_lo{i}", [P, 8, SEQ], F32R, own=mlp) for i in range(2)]
        sb("mixer_region", [P, 6 * 8 * SEQ + 2 * 1024 + 5 * SEQ])

        ident = const[:, C_ID:C_TRI]
        tri = const[:, C_TRI:C_ONE]
        ones = const[:, C_ONE:C_DIST]
        dist = const[:, C_DIST:C_MASK]
        mask = const[:, C_MASK:C_COS]
        cos = const[:, C_COS:C_SIN].rearrange("p (t r) -> p t r", t=2)
        sin = const[:, C_SIN:C_END].rearrange("p (t r) -> p t r", t=2)

        b_f = small[:, 0:8]
        gate_z = small[:, 8:24].rearrange("p (t h) -> p t h", t=2)
        gate_a = small[:, 24:40].rearrange("p (t h) -> p t h", t=2)
        gate_l = small[:, 40:56].rearrange("p (t h) -> p t h", t=2)
        cum = small[:, 56:72].rearrange("p (t h) -> p t h", t=2)
        lam = small[:, 72:77]
        top = small[:, 144:148].rearrange("p (u t) -> p u t", t=2)
        shift = small[:, 82:86].rearrange("p (u t) -> p u t", t=2)
        total = small[:, 86:94].rearrange("p (u t) -> p u t", t=2)
        inverse = small[:, 148:152].rearrange("p (u t) -> p u t", t=2)
        sumsq = small[:, 96:112]
        var = small[:, 112:120]
        rstd_sub = small[:, 120:128]
        rstd_pre = small[:, 152:154]
        rstd_post = small[:, 154:156]
        rstd_c = small[:, 156:160]
        sumsq_post = small[:, 160:164]
        post_base = small[:, 164:166]
        sumsq_pre = small[:, 166:168]
        sumsq_c = small[:, 168:172]
        newton = small[:, 128:136]
        seed = small[:, 136:144]
        lam_rows = prob[:, 0, :]
        cumT = prob[0:8, 1, 0:SEQ]
        narrow = logit[0:MLA_ROPE, 0, 0:SEQ]
        key_cum = v_b[:, :, :].rearrange("p t (h k) -> p (t h) k", k=SEQ)

        ident_loaded, const_loaded, small_loaded, gain_rows_loaded = map(sem, ("ident_loaded", "const_loaded", "small_loaded", "gain_rows_loaded"))
        x_loaded = [sem(f"x_loaded{p}") for p in range(PIECES)]
        mem_loaded = [sem(f"mem_loaded{p}") for p in range(PIECES)]
        raw_loaded = [sem(f"raw_loaded{s}") for s in range(RAW)]
        gain_loaded = sem("gain_loaded")
        hi_ready, lo_ready, tile_used = map(sem, ("hi_ready", "lo_ready", "tile_used"))
        evac_act, evac_dve = sem("evac_act"), sem("evac_dve")
        turn_done, turned_act, turned_dve = map(sem, ("turn_done", "turned_act", "turned_dve"))
        xturn_done, split_hi, split_lo = map(sem, ("xturn_done", "split_hi", "split_lo"))
        squares_act, var_ready, seed_ready, rstd_ready = map(
            sem, ("squares_act", "var_ready", "seed_ready", "rstd_ready"))
        resid_ready = sem("resid_ready")
        s_done, soft_ready, p_ready, pt_done, pt_ready, o_done, o_ready = map(
            sem, ("s_done", "soft_ready", "p_ready", "pt_done", "pt_ready", "o_done", "o_ready"))
        act_chain, dve_chain = sem("act_chain"), sem("dve_chain")
        gate_pe, gate_act, gate_dve = map(sem, ("gate_pe", "gate_act", "gate_dve"))
        key_cum_act, relu_act, relu_dve, lam_exp = map(sem, ("key_cum_act", "relu_act", "relu_dve", "lam_exp"))
        sub_scaled, rope_ready, lam_ready, out_stored = map(sem, ("sub_scaled", "rope_ready", "lam_ready", "out_stored"))
        y_zero, y_squares, y_gained = map(sem, ("y_zero", "y_squares", "y_gained"))

        def bank(index, c, t):
            return 4 * (index % 2) + 2 * t + c

        def side_of(name):
            return 4 * ((PLAN[name]["index"] + 1) % 2)

        def finished(eng, name):
            eng.wait_ge(tile_used, PLAN[name]["tile"] + PLAN[name]["tiles"])

        def evacuated(eng, name):
            g = PLAN[name]
            eng.wait_ge(evac_act, g["act"] + g["evacs_act"])
            eng.wait_ge(evac_dve, g["dve"] + g["evacs_dve"])

        def turns_evacuated(eng, name):
            eng.wait_ge(turned_act, TURNED_ACT[name] + turned_by(name)[0])
            eng.wait_ge(turned_dve, TURNED_DVE[name] + turned_by(name)[1])

        def split(eng, name, banks):
            eng.wait_ge(split_hi, SPLITS[name] + banks)
            eng.wait_ge(split_lo, SPLITS[name] + banks)

        def sums(index, t, width):
            first, parts = bank(index, 0, t), col_banks(width)
            if len(parts) == 1:
                return PS[:, first, 0:width]
            return PS[:, first:first + 2, 0:parts[0][1]]

        def like(to, width):
            n = len(col_banks(width))
            return to if n == 1 else to.rearrange("p (c w) -> p c w", c=n)

        def operand_bank(name, pair):
            return 4 * ((PLAN[NEXT_GROUP[name]]["index"] + 1) % 2) + pair % 4

        def chained(*sides):
            for side in sides:
                yield from side

        def wait_then(wait, side):
            wait()
            yield from side

        class Unit:
            def __init__(self, family, n):
                self.u = UNITS[family] + n
                self.family, self.n = family, n
                self.causal = family not in ("x0", "x1")
                self.scale = MLA_SCALE if family == "mla" else SCALE
                j = n
                if family in ("fox", "mla"):
                    self.q, self.k = qT_a[:, j, :], kT_a[:, j, :]
                    self.v = v_a[:, :, j * HD:(j + 1) * HD]
                    self.o = rows[:, :, j * HD:(j + 1) * HD]
                elif family == "diff":
                    h = j // 2
                    self.q, self.k = qT_b[:, j, :], kT_b[:, j, :]
                    self.v = v_b[:, :, h * 2 * HD:(h + 1) * 2 * HD]
                    self.o = rows[:, :, FOX_W + h * 2 * HD:FOX_W + (h + 1) * 2 * HD]
                    self.slope = 2.0 ** (-8.0 * (h + 1) / DIFF_HEADS)
                elif family == "moba":
                    self.q, self.k = qT_b[:, j, :], kT_b[:, j, :]
                    self.v = v_b[:, :, j * HD:(j + 1) * HD]
                    self.o = rows[:, :, 1024 + j * HD:1024 + (j + 1) * HD]
                    self.slope = 2.0 ** (-8.0 * (j + 1) / 8)
                else:
                    self.q, self.k = kT_a[:, j, :], mem_kT[:, j, :]
                    self.v = mem_v[:, :, j * HD:(j + 1) * HD]
                    self.o = rows[:, :, j * HD:(j + 1) * HD]
                if family == "mla":
                    r = 64 * (j % 2)
                    self.qpe, self.kpe = qpeT[r:r + 64, j // 2, :], kpeT[r:r + 64, :]
                self.dv = 2 * HD if family == "diff" else HD
                self.parts = [(0, 0, P), (1, P, 2 * P)] if self.causal else [(0, 0, 2 * P), (1, 2 * P, 2 * P)]
                self.cols = sum(p[2] for p in self.parts)

        def units(family, a=0, b=8):
            return [Unit(family, n) for n in range(a, b)]

        block = ctx.enter_context(nc.Block())

        @block.sync
        def _(sp):
            def piece(of, p):
                return of[:, :, p * D // PIECES:(p + 1) * D // PIECES]

            def load_mem(p):
                sp.dma_start(piece(rows, p), piece(mem[0].rearrange("(t p) d -> p t d", p=P), p)).then_inc(mem_loaded[p], 16)

            sp.dma_start(ident, consts[:, C_ID:C_TRI]).then_inc(ident_loaded, 16)
            prenorms = norms.rearrange("l (i two) (c p) -> (l i) two c p", two=2, p=P)[:, 0]
            gain_loads = [(gain_rows[0:16, :], mem_norm.rearrange("(c p) -> c p", p=P)),
                          (gain_rows[16:112, :], prenorms),
                          (gain_rows[112:116, :], mla_q_norm[0].rearrange("(c p) -> c p", p=P)),
                          (gain_rows[116:120, :], mla_kv_norm[0].rearrange("(c p) -> c p", p=P))]
            for to, source in gain_loads:
                sp.dma_start(to, source).then_inc(gain_rows_loaded, 16)
            load_mem(0)

            def load(i, dma, source, per, width):
                slot = dma % RAW
                if i is not None or dma >= RAW:
                    sp.wait_ge(hi_ready, at(i, Mlp.TILES, 2 * dma - 2 * RAW + 2))
                    sp.wait_ge(lo_ready, at(i, Mlp.TILES, 2 * dma - 2 * RAW + 2))
                sp.dma_start(raw[:, slot, 0:2 * per * width].rearrange("p (c w) -> p c w", w=width), source)\
                    .then_inc(raw_loaded[slot], 16)

            def load_group(name):
                g = PLAN[name]
                w, col = weights[name]
                height = 2 * g["per"] * P
                for n in range(g["tiles"] // 2):
                    if name == "mem" and 1 <= n < PIECES:
                        load_mem(n)
                    if name == "mem" and n >= RAW:
                        p = n - RAW
                        sp.dma_start(piece(resid, p), piece(x[0].rearrange("(t p) d -> p t d", p=P), p)).then_inc(x_loaded[p], 16)
                    source = w[n * height:(n + 1) * height, col:col + g["width"]].rearrange("(c p) w -> p c w", p=P)
                    load(None, g["tile"] // 2 + n, source, g["per"], g["width"])
                if name == "mem":
                    sp.dma_start(const[:, C_TRI:C_END], consts[:, C_TRI:C_END]).then_inc(const_loaded, 16)

            def load_up(l, i, b, tile):
                for n in range(8):
                    source = ffn_w1[l][2 * n * P:2 * (n + 1) * P, bass.ds(at(i, 2048, b * 1024), 1024)]
                    load(i, tile // 2 + n, source.rearrange("(c p) w -> p c w", p=P), 1, 1024)

            def load_down(l, i, b, tile):
                for half in range(2):
                    for n in range(4):
                        source = ffn_w2[l][bass.ds(at(i, 2048, b * 1024 + 2 * n * P), 2 * P), 1024 * half:1024 * (half + 1)]
                        load(i, tile // 2 + 4 * half + n, source.rearrange("(c p) w -> p c w", p=P), 1, 1024)

            for name, chunks, _, _ in GROUPS:
                if chunks is not None:
                    load_group(name)
                    continue
                l = int(name[3])
                m = Mlp(l)
                load_up(l, None, 0, m.up(0)[1])
                load_up(l, None, 1, m.up(1)[1])
                load_down(l, None, 0, m.down(0, 0)[1])
                with sp.Fori(0, (BLOCKS - 2) // 2) as i:
                    for b in (1, 2):
                        load_up(l, i, b + 1, m.up(b + 1)[1])
                        load_down(l, i, b, m.down(b, 0)[1])
                load_down(l, None, BLOCKS - 1, m.down(BLOCKS - 1, 0)[1])
            for p in range(PIECES):
                sp.wait_ge(resid_ready, updates_with((p + 1) * D // PIECES, "pf1"))
                sp.dma_start(piece(out[0].rearrange("(t p) d -> p t d", p=P), p), piece(resid, p)).then_inc(out_stored, 16)
            sp.wait_ge(out_stored, 16 * PIECES)

        @block.gpsimd
        def _(pool):
            pool.wait_ge(mem_loaded[0], 16)
            for to, source in ((b_f, fox_b_f[0:1, :].to_broadcast([P, 8])),
                               (subln[:, :], diff_subln[0:1, :].to_broadcast([P, 2 * HD])),
                               (lam_rows, diff_lambda.rearrange("a b d -> a (b d)").to_broadcast([P, 4 * HD]))):
                pool.dma_start(to, source).then_inc(small_loaded, 16)
            for name, (l, i) in POST.items():
                if name[1] == "a":
                    pool.wait_ge(o_done, UNITS["diff" if l == 0 else "moba"] + 8)
                else:
                    pool.wait_ge(resid_ready, updates_with(0, name))
                pool.dma_start(gain_row[:, :], norms[l, i:i + 1, :].to_broadcast([P, D])).then_inc(gain_loaded, 16)

        @block.scalar
        def _(act):
            chain = [0]

            def link(ins):
                chain[0] += 1
                ins.then_inc(act_chain, 1)
                act.wait_ge(act_chain, chain[0])

            def stream(i, tile, count, cols, side=iter(()), done=0):
                for k in range(tile + done, tile + count):
                    if k % 2 == 0:
                        act.wait_ge(raw_loaded[(k // 2) % RAW], at(i, 16 * Mlp.TILES // 2 // RAW, 16 * (k // 2 // RAW + 1)))
                    if i is not None or k >= RING:
                        act.wait_ge(tile_used, at(i, Mlp.TILES, k - RING + 1))
                    nc.scalar.activation(w_hi[:, k % RING, 0:cols], raw[:, (k // 2) % RAW, (k % 2) * cols:(k % 2 + 1) * cols],
                                         ACT.Copy).then_inc(hi_ready, 1)
                    if k - tile >= LEAD:
                        next(side, None)
                for _ in side:
                    pass

            def stream_group(name, side=iter(()), first=0, count=None, done=0):
                g = PLAN[name]
                stream(None, g["tile"] + first, count or g["tiles"], g["per"] * g["width"], side, done)

            def prefill(name, first=0):
                if name.startswith("ffn"):
                    stream(None, PLAN[name]["tile"], PREFILL, TILE)
                else:
                    stream_group(name, first=first, count=PREFILL)

            def evacuate(name, to, scale=None):
                g = PLAN[name]
                finished(act, name)
                nc.scalar.activation(like(to, g["width"]), sums(g["index"], 0, g["width"]), ACT.Copy,
                                     scale=rstd_pre[:, 0:1] if scale is None else scale).then_inc(evac_act, 1)

            def turned(name, to, side):
                n = dict(TURN_BANKS)[name] // 2
                act.wait_ge(turn_done, TURNS[name] + n)
                nc.scalar.activation(to[:, 0:2 * n, :].rearrange("p (b c) s -> p b (c s)", c=2), PS[:, side:side + n, :], ACT.Copy)\
                    .then_inc(turned_act, 1)

            def heads(name, pair, b, to=x_hi, gain=None):
                act.wait_ge(xturn_done, SPLITS[name] + pair + 1)
                c = 2 * pair
                if gain is None:
                    nc.scalar.activation(to[:, c:c + 2, :].rearrange("p c s -> p (c s)"), PS[:, b, :], ACT.Copy).then_inc(split_hi, 1)
                    return
                nc.scalar.activation(to[:, c, :], PS[:, b, 0:SEQ], ACT.Copy, scale=gain_col[:, gain + c:gain + c + 1])
                nc.scalar.activation(to[:, c + 1, :], PS[:, b, SEQ:2 * SEQ], ACT.Copy,
                                     scale=gain_col[:, gain + c + 1:gain + c + 2]).then_inc(split_hi, 1)

            def rstd_seed(name, width=2):
                act.wait_ge(var_ready, NORMS[name] + 1)
                nc.scalar.activation(seed[:, 0:width], var[:, 0:width], ACT.Sqrt).then_inc(seed_ready, 1)

            def row_squares(source, scratch):
                for t in range(HALVES):
                    ins = nc.scalar.activation(scratch(t), source[:, t, :], ACT.Square, accum_out=sumsq_pre[:, t:t + 1])
                ins.then_inc(squares_act, 1)

            def side_operand(name):
                for pair in range(2, 8):
                    heads(name, pair, operand_bank(name, pair), gain=GAIN_COL[name])
                    if pair % 2:
                        yield
                row_squares(resid, lambda t: rows[:, t, :])
                yield
                rstd_seed(name)
                yield
                act.wait_ge(rstd_ready, NORMS[name] + 1)

            def handover(name):
                for pair in range(2):
                    heads(name, pair, operand_bank(name, pair), gain=GAIN_COL[name])

            def attend(us, side):
                for s in range(len(us) + 2):
                    if 1 <= s <= len(us):
                        a = us[s - 1]
                        act.wait_ge(pt_done, a.u + 1)
                        if a.u >= 2:
                            act.wait_ge(o_done, a.u - 1)
                        nc.scalar.activation(prob[:, a.u % 2, 0:a.cols], PS[:, side + 2, 0:a.cols], ACT.Copy).then_inc(pt_ready, 1)
                    if s < len(us):
                        a = us[s]
                        act.wait_ge(soft_ready, a.u + 1)
                        if not a.causal:
                            act.wait_ge(pt_done, a.u - 1)
                        for t, col, keys in a.parts:
                            source = logit[:, a.u % 2, col:col + keys] if a.causal else PS[:, side + a.u % 2, col:col + keys]
                            ins = nc.scalar.activation(logit[:, a.u % 2, col:col + keys], source, ACT.Exp,
                                                       bias=shift[:, a.u % 2, t:t + 1], scale=a.scale,
                                                       accum_out=total[:, a.u % 4, t:t + 1])
                        ins.then_inc(p_ready, 1)
                    yield

            def squares_of(name, part, t):
                g = PLAN[name]
                finished(act, name)
                if t:
                    act.wait_ge(evac_dve, g["dve"] + 1)
                if part:
                    act.wait_ge(evac_act, g["act"] - 1 + t)
                nc.scalar.activation((logit, prob)[t][:, :, :], sums(g["index"], t, 1024), ACT.Square,
                                     accum_out=sumsq_post[:, 2 * part + t:2 * part + t + 1]).then_inc(evac_act, 1)

            def out_projection(names, norm, following):
                def side():
                    yield
                    for t in range(HALVES):
                        squares_of(names[0], 0, t)
                        yield
                stream_group(names[1], side())
                prefill(following)
                for t in range(HALVES):
                    squares_of(names[1], 1, t)
                rstd_seed(norm)

            def mixer_out(names, last_proj, family, attended, o_names, sub, norm, following):
                first = names[0]
                prefill(first)
                evacuate(last_proj, v_b[:, 0, attended * HD:])
                side = side_of(first)
                for pair in range(4):
                    heads(o_names[0], pair, side + pair)
                stream_group(first, attend(units(family, attended), side), 0, 8, PREFILL)
                prefill(first, 8)
                if sub:
                    act.wait_ge(o_ready, UNITS["diff"] + 8)
                    for h in range(DIFF_HEADS):
                        part = rows[:, 0, FOX_W + 256 * h:FOX_W + 256 * (h + 1)]
                        ins = nc.scalar.activation(x_hi[:, 8 + h, :], part, ACT.Square, accum_out=sumsq[:, h:h + 1])
                    ins.then_inc(squares_act, 1)
                    rstd_seed("sub", 8)
                for pair in range(4):
                    heads(o_names[1], pair, side + pair, x_hi[:, 8:16, :])
                stream_group(first, first=8, count=8, done=PREFILL)
                out_projection(names, norm, following)

            def cross(l):
                handover(f"x{l}")
                stream_group(f"xq{l}", side_operand(f"x{l}"), done=PREFILL)
                prefill(f"xo{l}0")
                evacuate(f"xq{l}", rows[:, 0, 1024:1536])
                side = side_of(f"xo{l}0")
                turned(f"xq{l}", kT_a, side_of(f"xq{l}"))
                attention = attend(units(f"x{l}", 0, 4), side)
                for _ in range(5):
                    next(attention)
                heads(f"xo{l}", 0, side_of(f"xq{l}"))
                for _ in attention:
                    pass
                heads(f"xo{l}", 1, side)
                stream_group(f"xo{l}0", done=PREFILL)
                out_projection((f"xo{l}0", f"xo{l}1"), f"px{l}", f"ffn{l}")

            def mlp(l, following):
                m = Mlp(l)

                def hidden(i, b):
                    g, tile = m.up(b)
                    act.wait_ge(tile_used, at(i, Mlp.TILES, tile + 16))
                    if i is not None or b > 0:
                        act.wait_ge(xturn_done, at(i, Mlp.SPLITS, m.s + 4 * b))
                    part = like(rows[:, 0, 0:1024], 1024)
                    nc.scalar.activation(part, sums(g, 0, 1024), ACT.Relu, scale=rstd_pre[:, 0:1]).then_inc(relu_act, 1)
                    act.wait_ge(relu_act, at(i, Mlp.ACT, BLOCKS * l + b + 1))
                    nc.scalar.activation(part, part, ACT.Square).then_inc(evac_act, 1)
                    yield
                    yield
                    for n in range(4):
                        act.wait_ge(xturn_done, at(i, Mlp.SPLITS, m.s + 4 * b + n + 1))
                        nc.scalar.activation(h_hi[b % 2][:, 2 * n:2 * n + 2, :].rearrange("p c s -> p (c s)"),
                                             PS[:, bank(g, 0, 0) + n, :], ACT.Copy).then_inc(split_hi, 1)
                        yield

                def y_row_squares(half):
                    for t in range(HALVES):
                        act.wait_ge(evac_dve, m.y_dve(BLOCKS - 1, half) + t + 1)
                        ins = nc.scalar.activation(x_hi[:, 4 * t:4 * t + 4, :].rearrange("p c s -> p (c s)"),
                                                   y_acc[:, t, 1024 * half:1024 * (half + 1)], ACT.Square,
                                                   accum_out=sumsq_post[:, 2 * half + t:2 * half + t + 1])
                    ins.then_inc(y_squares, 1)

                def side_last():
                    yield
                    yield
                    y_row_squares(0)
                    yield

                def up(i, b, side=iter(()), done=0):
                    stream(i, m.up(b)[1], 16, 1024, side, done)

                def down(i, b, half, side=iter(())):
                    stream(i, m.down(b, half)[1], 8, 1024, side)

                handover(f"f{l}")
                up(None, 0, side_operand(f"f{l}"), PREFILL)
                up(None, 1, hidden(None, 0))
                down(None, 0, 0, hidden(None, 1))
                down(None, 0, 1)
                with act.Fori(0, (BLOCKS - 2) // 2) as i:
                    for b in (1, 2):
                        up(i, b + 1)
                        down(i, b, 0, hidden(i, b + 1))
                        down(i, b, 1)
                down(None, BLOCKS - 1, 0)
                down(None, BLOCKS - 1, 1, side_last())
                if following:
                    prefill(following)
                y_row_squares(1)
                rstd_seed(f"pf{l}")

            act.wait_ge(turned_dve, TURNED_DVE["gain"] + 1)
            for pair in range(2):
                heads("mem", pair, operand_bank("mem", pair), gain=GAIN_COL["mem"])
            prefill("mem")

            def heads_behind(pair):
                act.wait_ge(tile_used, 2 * pair + 2)
                heads("a0", pair, operand_bank("mem", pair), gain=GAIN_COL["a0"])

            def side_first():
                for pair in range(2, 8):
                    heads("mem", pair, operand_bank("mem", pair), gain=GAIN_COL["mem"])
                    if pair % 2:
                        yield
                for p in range(PIECES):
                    act.wait_ge(mem_loaded[p], 16)
                row_squares(rows, lambda t: (qT_a, kT_a)[t][:, :, :].rearrange("p h s -> p (h s)"))
                act.wait_ge(lam_ready, 1)
                nc.scalar.activation(lam[:, 2:4], lam[:, 0:2], ACT.Exp).then_inc(lam_exp, 1)
                yield
                rstd_seed("mem")
                yield
                for pair in range(7):
                    heads_behind(pair)
                    yield
                act.wait_ge(rstd_ready, NORMS["mem"] + 1)
            stream_group("mem", side_first(), done=PREFILL)
            prefill("fv")
            heads_behind(7)

            def side_memory():
                g = PLAN["mem"]
                finished(act, "mem")
                nc.scalar.activation(qT_b[:, 0:2, :].rearrange("p h s -> p (h s)"), PS[:, bank(g["index"], 0, 0), :], ACT.Copy,
                                     scale=rstd_pre[:, 0:1])
                nc.scalar.activation(mem_v[:, 0, :], PS[:, bank(g["index"], 1, 0), :], ACT.Copy, scale=rstd_pre[:, 0:1])\
                    .then_inc(evac_act, 1)
                yield
                yield
                turned("mem_k", mem_kT, side_of("fv"))
                yield
                row_squares(resid, lambda t: rows[:, t, :])
                yield
                rstd_seed("a0")
                yield
                act.wait_ge(rstd_ready, NORMS["a0"] + 1)
            stream_group("fv", side_memory(), done=PREFILL)

            def side_value(name, to):
                evacuate(name, to[:, 0, :])
                yield
            stream_group("fg", side_value("fv", v_a))

            def side_gate():
                side = side_of("fq")
                yield
                act.wait_ge(gate_dve, 1)
                link(nc.scalar.activation(gate_a[:, :, :], gate_a[:, :, :], ACT.Exp))
                nc.scalar.activation(gate_a[:, :, :], gate_a[:, :, :], ACT.Ln, bias=1.0).then_inc(gate_act, 1)
                yield
                yield
                yield
                yield
                act.wait_ge(gate_pe, 2)
                nc.scalar.activation(key_cum[:, 0:4, :].rearrange("p (b h) k -> p b (h k)", h=2), PS[:, side:side + 2, :], ACT.Copy)\
                    .then_inc(key_cum_act, 1)
                yield
            stream_group("fq", side_gate())

            def side_turn(name, to, follow):
                evacuate(name, rows[:, 0, 1024:2048])
                yield
                yield
                turned(name, to, side_of(follow))
                yield

            stream_group("fk", side_turn("fq", qT_a, "fk"))
            stream_group("dq", side_turn("fk", kT_a, "dq"))
            stream_group("dk", chained(side_turn("dq", qT_b, "dk"), attend(units("fox", 0, FOX_FIRST), side_of("dk"))))
            stream_group("dv0", chained(side_turn("dk", kT_b, "dv0"), attend(units("fox", FOX_FIRST, 8), side_of("dv0"))))
            stream_group("dv1", chained(side_value("dv0", v_b[:, :, 0:512]), attend(units("diff", 0, DIFF_FIRST), side_of("dv1"))))
            mixer_out(("abo0", "abo1"), "dv1", "diff", DIFF_FIRST, ("o0a", "o0b"), True, "pa0", "xq0")
            cross(0)
            mlp(0, "cqkv")

            handover("a1")
            stream_group("cqkv", side_operand("a1"), done=PREFILL)

            def side_latent():
                evacuate("cqkv", rows[:, 0, 0:1024])
                yield
            stream_group("kpe", side_latent())

            def side_low_rank():
                yield
                evacuated(act, "cqkv")
                for c in range(2):
                    ins = nc.scalar.activation(v_b[:, c, 0:512], rows[:, 0, 512 * c:512 * c + 512], ACT.Square,
                                               accum_out=sumsq_c[:, c:c + 1])
                ins.then_inc(squares_act, 1)
                yield
                rstd_seed("c1", 4)
                yield
                yield
                yield
                for pair in range(4):
                    heads("c1", pair, side_of("mq") + pair, c_hi, GAIN_COL["q"])
                    yield
                act.wait_ge(rstd_ready, NORMS["c1"] + 1)
            stream_group("mq", side_low_rank())
            stream_group("uq0", side_turn("mq", qT_b, "uq0"))

            def side_query(name, first):
                evacuate(name, rows[:, 0, first:first + 768], rstd_c[:, 0:1])
                yield
            stream_group("uq1", side_query("uq0", 0))
            stream_group("ukv0", side_query("uq1", 768))

            def side_key_value(name, turn, n, follow):
                g = PLAN[name]
                finished(act, name)
                if n:
                    act.wait_ge(turn_done, TURNS["kn0"] + 2)
                for w, to in ((0, rows[:, 0, 1536:2048]), (1, v_a[:, 0, 512 * n:512 * n + 512])):
                    ins = nc.scalar.activation(to.rearrange("p (c h d) -> p c h d", c=2, h=2),
                                               sums(g["index"], 0, 1024).rearrange("p c (h w d) -> p c h w d", h=2, w=2)[:, :, :, w, :],
                                               ACT.Copy, scale=rstd_c[:, 1:2])
                ins.then_inc(evac_act, 1)
                yield
                yield
                turned(turn, kT_a[:, 4 * n:4 * n + 4, :], side_of(follow))
                yield
            stream_group("ukv1", side_key_value("ukv0", "kn0", 0, "ukv1"))

            def side_queries():
                yield
                turned("qn", qT_a, side_of("mk"))
                yield
                yield
                turned("qpe", qpeT, side_of("mk"))
                yield
            stream_group("mk", chained(side_key_value("ukv1", "kn1", 1, "mk"), side_queries(),
                                       attend(units("mla", 0, MLA_FIRST), side_of("mk"))))
            stream_group("mv", chained(side_turn("mk", kT_b, "mv"), attend(units("mla", MLA_FIRST, 8), side_of("mv"))))
            mixer_out(("cdo0", "cdo1"), "mv", "moba", 0, ("o1a", "o1b"), False, "pa1", "xq1")
            cross(1)
            mlp(1, None)

        @block.vector
        def _(dve):
            chain = [0]

            def link(ins):
                chain[0] += 1
                ins.then_inc(dve_chain, 1)
                dve.wait_ge(dve_chain, chain[0])

            def stream(i, tile, count, cols, side=iter(()), done=0):
                for k in range(tile + done, tile + count):
                    dve.wait_ge(hi_ready, at(i, Mlp.TILES, k + 1))
                    nc.vector.tensor_tensor(w_lo[:, k % RING, 0:cols], raw[:, (k // 2) % RAW, (k % 2) * cols:(k % 2 + 1) * cols],
                                            w_hi[:, k % RING, 0:cols].bitcast(F32), ALU.subtract).then_inc(lo_ready, 1)
                    if k - tile >= LEAD:
                        next(side, None)
                for _ in side:
                    pass

            def stream_group(name, side=iter(()), first=0, count=None, done=0):
                g = PLAN[name]
                stream(None, g["tile"] + first, count or g["tiles"], g["per"] * g["width"], side, done)

            def prefill(name, first=0):
                if name.startswith("ffn"):
                    stream(None, PLAN[name]["tile"], PREFILL, TILE)
                else:
                    stream_group(name, first=first, count=PREFILL)

            def evacuate(name, to, scale=None):
                g = PLAN[name]
                finished(dve, name)
                nc.vector.tensor_scalar(like(to, g["width"]), sums(g["index"], 1, g["width"]),
                                        rstd_pre[:, 1:2] if scale is None else scale, None, ALU.mult).then_inc(evac_dve, 1)

            def evacuate_narrow(name, width):
                g = PLAN[name]
                finished(dve, name)
                nc.vector.tensor_copy(narrow[0:width, :], PS[0:width, bank(g["index"], 0, 0), 0:SEQ]).then_inc(evac_dve, 1)

            def turned(name, to, side):
                banks = dict(TURN_BANKS)[name]
                n = banks // 2
                dve.wait_ge(turn_done, TURNS[name] + banks)
                nc.vector.tensor_copy(to[:, 2 * n:2 * banks, :].rearrange("p (b c) s -> p b (c s)", c=2), PS[:, side + n:side + banks, :])\
                    .then_inc(turned_dve, 1)

            def rests(name, pair, b, hi=x_hi, lo=x_lo, gain=None):
                dve.wait_ge(split_hi, SPLITS[name] + pair + 1)
                c = 2 * pair
                if gain is None:
                    nc.vector.tensor_tensor(lo[:, c:c + 2, :].rearrange("p c s -> p (c s)"), PS[:, b, :],
                                            hi[:, c:c + 2, :].rearrange("p c s -> p (c s)").bitcast(F32), ALU.subtract)\
                        .then_inc(split_lo, 1)
                    return
                nc.vector.scalar_tensor_tensor(out=lo[:, c, :], in0=PS[:, b, 0:SEQ], scalar=gain_col[:, gain + c:gain + c + 1],
                                               in1=hi[:, c, :].bitcast(F32), op0=ALU.mult, op1=ALU.subtract)
                nc.vector.scalar_tensor_tensor(out=lo[:, c + 1, :], in0=PS[:, b, SEQ:2 * SEQ],
                                               scalar=gain_col[:, gain + c + 1:gain + c + 2],
                                               in1=hi[:, c + 1, :].bitcast(F32), op0=ALU.mult, op1=ALU.subtract)\
                    .then_inc(split_lo, 1)

            def squares(scratch, source, to):
                return nc.vector.tensor_tensor_reduce(scratch, source, source, 1.0, 0.0, ALU.mult, ALU.add, to)

            def refine(name, width, to):
                dve.wait_ge(seed_ready, NORMS[name] + 1)
                v, y, w = var[:, 0:width], seed[:, 0:width], newton[:, 0:width]
                link(nc.vector.reciprocal(y, y))
                link(nc.vector.tensor_tensor(w, y, y, ALU.mult))
                link(nc.vector.scalar_tensor_tensor(out=w, in0=w, scalar=-0.5, in1=v, op0=ALU.mult, op1=ALU.mult))
                nc.vector.scalar_tensor_tensor(out=to, in0=w, scalar=1.5, in1=y, op0=ALU.add, op1=ALU.mult).then_inc(rstd_ready, 1)
                dve.wait_ge(rstd_ready, NORMS[name] + 1)

            def row_rstd(name, width, length, source, to):
                dve.wait_ge(squares_act, SQUARES[name] + 1)
                nc.vector.tensor_scalar(var[:, 0:width], source, 1.0 / length, EPS, ALU.mult, ALU.add).then_inc(var_ready, 1)
                refine(name, width, to)

            def post_rstd(name):
                nc.vector.scalar_tensor_tensor(out=var[:, 0:2], in0=sumsq_post[:, 2:4], scalar=1.0 / D, in1=post_base[:, :],
                                               op0=ALU.mult, op1=ALU.add).then_inc(var_ready, 1)
                refine(name, 2, rstd_post[:, :])

            def post_first():
                link(nc.vector.tensor_scalar(post_base[:, :], sumsq_post[:, 0:2], 1.0 / D, EPS, ALU.mult, ALU.add))

            def update(pieces):
                for a, z in pieces:
                    for t in range(HALVES):
                        h = resid[:, t, a:z]
                        nc.vector.scalar_tensor_tensor(out=h, in0=rows[:, t, a:z], scalar=rstd_post[:, t:t + 1], in1=h,
                                                       op0=ALU.mult, op1=ALU.add).then_inc(resid_ready, 1)

            def side_operand(name):
                for pair in range(2, 8):
                    rests(name, pair, operand_bank(name, pair), gain=GAIN_COL[name])
                    if pair % 2:
                        yield
                yield
                row_rstd(name, 2, D, sumsq_pre[:, :], rstd_pre[:, :])
                yield

            def handover(name):
                update(UPDATES[0:2])
                rests(name, 0, operand_bank(name, 0), gain=GAIN_COL[name])
                update(UPDATES[2:3])
                rests(name, 1, operand_bank(name, 1), gain=GAIN_COL[name])
                update(UPDATES[3:])

            def attend(us, side):
                for s in range(len(us) + 2):
                    if s < len(us):
                        a = us[s]
                        S, L = PS[:, side + a.u % 2, 0:a.cols], logit[:, a.u % 2, 0:a.cols]
                        dve.wait_ge(s_done, a.u + 1)
                        if a.u >= 2 and a.causal:
                            dve.wait_ge(pt_done, a.u - 1)
                        if a.family == "fox":
                            for t, col, keys in a.parts:
                                ins = nc.vector.scalar_tensor_tensor(
                                    out=logit[:, a.u % 2, col:col + keys], in0=key_cum[:, a.n, 0:keys], scalar=cum[:, t, a.n:a.n + 1],
                                    in1=mask[:, col:col + keys], op0=ALU.subtract, op1=ALU.subtract)
                            link(ins)
                        elif a.causal and a.family != "mla":
                            link(nc.vector.tensor_scalar(L, dist, a.slope / SCALE, None, ALU.mult))
                        for t, col, keys in a.parts:
                            part, highest = slice(col, col + keys), top[:, a.u % 2, t:t + 1]
                            if a.causal:
                                ins = nc.vector.tensor_tensor_reduce(L[:, part], S[:, part], (mask if a.family == "mla" else L)[:, part],
                                                                     1.0, -3e38, ALU.subtract if a.family == "fox" else ALU.add, ALU.max, highest)
                            else:
                                ins = nc.vector.tensor_reduce(highest, S[:, part], AX_X, ALU.max)
                        link(ins)
                        nc.vector.tensor_scalar(shift[:, a.u % 2, :], top[:, a.u % 2, :], -a.scale, None, ALU.mult).then_inc(soft_ready, 1)
                    if s >= 2:
                        a = us[s - 2]
                        dve.wait_ge(o_done, a.u + 1)
                        link(nc.vector.reciprocal(inverse[:, a.u % 2, :], total[:, a.u % 4, :]))
                        minus = a.family == "diff" and a.n % 2
                        if minus:
                            link(nc.vector.tensor_scalar(inverse[:, a.u % 2, :], inverse[:, a.u % 2, :], lam[:, 4:5], None, ALU.mult))
                            dve.wait_ge(o_ready, a.u)
                        for t in range(HALVES):
                            O = PS[:, side + 3, t * a.dv:(t + 1) * a.dv]
                            if minus:
                                ins = nc.vector.scalar_tensor_tensor(out=a.o[:, t, :], in0=O, scalar=inverse[:, a.u % 2, t:t + 1],
                                                                     in1=a.o[:, t, :], op0=ALU.mult, op1=ALU.add)
                            else:
                                ins = nc.vector.tensor_scalar(a.o[:, t, :], O, inverse[:, a.u % 2, t:t + 1], None, ALU.mult)
                        ins.then_inc(o_ready, 1)
                    yield

            def gained(name, part, norm):
                g = PLAN[name]
                finished(dve, name)
                dve.wait_ge(gain_loaded, 16 * (POST_AT[norm] + 1))
                cols = slice(1024 * part, 1024 * (part + 1))
                for t in (1, 0):
                    if t == 0:
                        dve.wait_ge(evac_act, g["act"] + 1)
                    nc.vector.tensor_tensor(like(rows[:, t, cols], 1024), sums(g["index"], t, 1024), like(gain_row[:, cols], 1024),
                                            ALU.mult).then_inc(evac_dve, 1)

            def out_projection(names, norm, following):
                def side():
                    yield
                    gained(names[0], 0, norm)
                    yield
                    yield
                    dve.wait_ge(evac_act, PLAN[names[0]]["act"] + 2)
                    post_first()
                stream_group(names[1], side())
                prefill(following)
                gained(names[1], 1, norm)
                dve.wait_ge(evac_act, PLAN[names[1]]["act"] + 2)
                post_rstd(norm)

            def mixer_out(names, last_proj, family, attended, o_names, sub, norm, following):
                first = names[0]
                prefill(first)
                evacuate(last_proj, v_b[:, 1, attended * HD:])
                side = side_of(first)
                for pair in range(4):
                    rests(o_names[0], pair, side + pair)
                stream_group(first, attend(units(family, attended), side), 0, 8, PREFILL)
                prefill(first, 8)
                if sub:
                    dve.wait_ge(o_ready, UNITS["diff"] + 8)
                    for h in range(DIFF_HEADS):
                        ins = squares(x_lo[:, 8 + h, :], rows[:, 1, FOX_W + 256 * h:FOX_W + 256 * (h + 1)], sumsq[:, 4 + h:5 + h])
                    link(ins)
                    row_rstd("sub", 8, 2 * HD, sumsq[:, 0:8], rstd_sub)
                    for h in range(DIFF_HEADS):
                        for t in range(HALVES):
                            part = rows[:, t, FOX_W + 256 * h:FOX_W + 256 * (h + 1)]
                            ins = nc.vector.scalar_tensor_tensor(out=part, in0=part, scalar=rstd_sub[:, 4 * t + h:4 * t + h + 1],
                                                                 in1=subln[:, :], op0=ALU.mult, op1=ALU.mult)
                        ins.then_inc(sub_scaled, 1)
                for pair in range(4):
                    rests(o_names[1], pair, side + pair, x_hi[:, 8:16, :], x_lo[:, 8:16, :])
                stream_group(first, first=8, count=8, done=PREFILL)
                out_projection(names, norm, following)

            def cross(l):
                handover(f"x{l}")
                stream_group(f"xq{l}", side_operand(f"x{l}"), done=PREFILL)
                prefill(f"xo{l}0")
                evacuate(f"xq{l}", rows[:, 1, 1024:1536])
                side = side_of(f"xo{l}0")
                turned(f"xq{l}", kT_a, side_of(f"xq{l}"))
                attention = attend(units(f"x{l}", 0, 4), side)
                for _ in range(5):
                    next(attention)
                rests(f"xo{l}", 0, side_of(f"xq{l}"))
                for _ in attention:
                    pass
                rests(f"xo{l}", 1, side)
                stream_group(f"xo{l}0", done=PREFILL)
                out_projection((f"xo{l}0", f"xo{l}1"), f"px{l}", f"ffn{l}")

            def mlp(l, following):
                m = Mlp(l)

                def hidden(i, b):
                    g, tile = m.up(b)
                    dve.wait_ge(tile_used, at(i, Mlp.TILES, tile + 16))
                    if i is not None or b > 0:
                        dve.wait_ge(xturn_done, at(i, Mlp.SPLITS, m.s + 4 * b))
                    part = like(rows[:, 1, 0:1024], 1024)
                    nc.vector.tensor_scalar(part, sums(g, 1, 1024), rstd_pre[:, 1:2], 0.0, ALU.mult, ALU.max).then_inc(relu_dve, 1)
                    dve.wait_ge(relu_dve, at(i, Mlp.ACT, BLOCKS * l + b + 1))
                    nc.vector.tensor_tensor(part, part, part, ALU.mult).then_inc(evac_dve, 1)
                    yield
                    yield
                    for n in range(4):
                        dve.wait_ge(split_hi, at(i, Mlp.SPLITS, m.s + 4 * b + n + 1))
                        nc.vector.tensor_tensor(h_lo[b % 2][:, 2 * n:2 * n + 2, :].rearrange("p c s -> p (c s)"),
                                                PS[:, bank(g, 0, 0) + n, :],
                                                h_hi[b % 2][:, 2 * n:2 * n + 2, :].rearrange("p c s -> p (c s)").bitcast(F32),
                                                ALU.subtract).then_inc(split_lo, 1)
                        yield

                def accumulate(i, b, half):
                    g, tile = m.down(b, half)
                    dve.wait_ge(tile_used, at(i, Mlp.TILES, tile + 8))
                    if b:
                        dve.wait_ge(evac_dve, at(i, Mlp.DVE, m.y_dve(b, half)))
                    for t in range(HALVES):
                        y = like(y_acc[:, t, 1024 * half:1024 * (half + 1)], 1024)
                        nc.vector.tensor_tensor(y, y, sums(g, t, 1024), ALU.add).then_inc(evac_dve, 1)
                        yield

                def gained_sums(half):
                    dve.wait_ge(evac_dve, m.y_dve(BLOCKS - 1, half) + 2)
                    cols = slice(1024 * half, 1024 * (half + 1))
                    for t in range(HALVES):
                        nc.vector.tensor_tensor(rows[:, t, cols], y_acc[:, t, cols], gain_row[:, cols], ALU.mult).then_inc(y_gained, 1)

                def side_last():
                    yield from accumulate(None, BLOCKS - 1, 0)
                    dve.wait_ge(gain_loaded, 16 * (POST_AT[f"pf{l}"] + 1))
                    gained_sums(0)
                    yield
                    dve.wait_ge(y_squares, 2 * l + 1)
                    post_first()
                    yield

                def up(i, b, side=iter(()), done=0):
                    stream(i, m.up(b)[1], 16, 1024, side, done)

                def down(i, b, half, side=iter(())):
                    stream(i, m.down(b, half)[1], 8, 1024, side)

                def zero_sums():
                    for t in range(HALVES):
                        nc.vector.memset(y_acc[:, t, :], 0.0).then_inc(y_zero, 1)
                        yield
                    dve.wait_ge(y_zero, HALVES * (l + 1))

                handover(f"f{l}")
                up(None, 0, chained(side_operand(f"f{l}"), zero_sums()), PREFILL)
                up(None, 1, hidden(None, 0))
                down(None, 0, 0, hidden(None, 1))
                down(None, 0, 1, accumulate(None, 0, 0))
                with dve.Fori(0, (BLOCKS - 2) // 2) as i:
                    for b in (1, 2):
                        up(i, b + 1, accumulate(i, b - 1, 1))
                        down(i, b, 0, hidden(i, b + 1))
                        down(i, b, 1, accumulate(i, b, 0))
                down(None, BLOCKS - 1, 0, accumulate(None, BLOCKS - 2, 1))
                down(None, BLOCKS - 1, 1, side_last())
                if following:
                    prefill(following)
                for _ in accumulate(None, BLOCKS - 1, 1):
                    pass
                gained_sums(1)
                dve.wait_ge(y_squares, 2 * l + 2)
                dve.wait_ge(y_gained, 4 * l + 4)
                post_rstd(f"pf{l}")

            dve.wait_ge(turn_done, TURNS["gain"] + 1)
            nc.vector.tensor_copy(gain_col[:, :], PS[:, 0, 0:120]).then_inc(turned_dve, 1)
            dve.wait_ge(turned_dve, TURNED_DVE["gain"] + 1)
            for pair in range(2):
                rests("mem", pair, operand_bank("mem", pair), gain=GAIN_COL["mem"])
            prefill("mem")

            def side_first():
                for pair in range(2, 8):
                    rests("mem", pair, operand_bank("mem", pair), gain=GAIN_COL["mem"])
                    if pair == 6:
                        dve.wait_ge(small_loaded, 16 * SMALL_LOADS)
                        for n in range(2):
                            ins = nc.vector.tensor_tensor_reduce(logit[:, 0, n * HD:(n + 1) * HD], lam_rows[:, 2 * n * HD:(2 * n + 1) * HD],
                                                                 lam_rows[:, (2 * n + 1) * HD:(2 * n + 2) * HD], 1.0, 0.0, ALU.mult,
                                                                 ALU.add, lam[:, n:n + 1])
                        ins.then_inc(lam_ready, 1)
                        nc.vector.tensor_scalar(subln[:, :], subln[:, :], 1.0 - LAM_INIT, None, ALU.mult)
                    if pair % 2:
                        yield
                yield
                row_rstd("mem", 2, D, sumsq_pre[:, :], rstd_pre[:, :])
                dve.wait_ge(lam_exp, 1)
                link(nc.vector.tensor_tensor(lam[:, 4:5], lam[:, 3:4], lam[:, 2:3], ALU.subtract))
                link(nc.vector.tensor_scalar(lam[:, 4:5], lam[:, 4:5], -LAM_INIT, None, ALU.add))
                yield
                for pair in range(7):
                    rests("a0", pair, operand_bank("mem", pair), gain=GAIN_COL["a0"])
                    yield
            stream_group("mem", side_first(), done=PREFILL)
            prefill("fv")
            rests("a0", 7, operand_bank("mem", 7), gain=GAIN_COL["a0"])

            def side_memory():
                g = PLAN["mem"]
                finished(dve, "mem")
                nc.vector.tensor_scalar(qT_b[:, 2:4, :].rearrange("p h s -> p (h s)"), PS[:, bank(g["index"], 0, 1), :],
                                        rstd_pre[:, 1:2], None, ALU.mult)
                nc.vector.tensor_scalar(mem_v[:, 1, :], PS[:, bank(g["index"], 1, 1), :], rstd_pre[:, 1:2], None, ALU.mult)\
                    .then_inc(evac_dve, 1)
                yield
                yield
                turned("mem_k", mem_kT, side_of("fv"))
                yield
                yield
                row_rstd("a0", 2, D, sumsq_pre[:, :], rstd_pre[:, :])
                yield
            stream_group("fv", side_memory(), done=PREFILL)

            def side_value(name, to):
                evacuate(name, to[:, 1, :])
                yield
            stream_group("fg", side_value("fv", v_a))

            def side_gate():
                side = side_of("fq")
                evacuate_narrow("fg", 8)
                yield
                dve.wait_ge(turn_done, TURNS["fg"] + 1)
                for t in range(HALVES):
                    ins = nc.vector.scalar_tensor_tensor(out=gate_z[:, t, :], in0=PS[:, side + 1, t * 8:(t + 1) * 8],
                                                         scalar=rstd_pre[:, t:t + 1], in1=b_f, op0=ALU.mult, op1=ALU.add)
                ins.then_inc(turned_dve, 1)
                dve.wait_ge(turned_dve, TURNED_DVE["fg"] + 1)
                nc.vector.scalar_tensor_tensor(out=gate_a[:, :, :], in0=gate_z[:, :, :], scalar=-1.0, in1=gate_z[:, :, :],
                                               op0=ALU.mult, op1=ALU.min).then_inc(gate_dve, 1)
                dve.wait_ge(gate_act, 1)
                nc.vector.scalar_tensor_tensor(out=gate_l[:, :, :], in0=gate_z[:, :, :], scalar=0.0, in1=gate_a[:, :, :],
                                               op0=ALU.min, op1=ALU.subtract).then_inc(gate_dve, 1)
                yield
                dve.wait_ge(gate_pe, 1)
                nc.vector.tensor_scalar(cum[:, :, :].rearrange("p t h -> p (t h)"), PS[:, side + 2, 0:16], 1.0 / SCALE, None, ALU.mult)\
                    .then_inc(gate_dve, 1)
                yield
                dve.wait_ge(turn_done, TURNS["cum"] + 1)
                nc.vector.tensor_copy(cumT, PS[0:8, side + 3, 0:SEQ]).then_inc(turned_dve, 1)
                yield
                yield
                dve.wait_ge(gate_pe, 2)
                nc.vector.tensor_copy(key_cum[:, 4:8, :].rearrange("p (b h) k -> p b (h k)", h=2), PS[:, side + 2:side + 4, :])\
                    .then_inc(gate_dve, 1)
                yield
                dve.wait_ge(key_cum_act, 1)
            stream_group("fq", side_gate())

            def side_turn(name, to, follow):
                evacuate(name, rows[:, 1, 1024:2048])
                yield
                yield
                turned(name, to, side_of(follow))
                yield

            stream_group("fk", side_turn("fq", qT_a, "fk"))
            stream_group("dq", side_turn("fk", kT_a, "dq"))
            stream_group("dk", chained(side_turn("dq", qT_b, "dk"), attend(units("fox", 0, FOX_FIRST), side_of("dk"))))
            stream_group("dv0", chained(side_turn("dk", kT_b, "dv0"), attend(units("fox", FOX_FIRST, 8), side_of("dv0"))))
            stream_group("dv1", chained(side_value("dv0", v_b[:, :, 0:512]), attend(units("diff", 0, DIFF_FIRST), side_of("dv1"))))
            mixer_out(("abo0", "abo1"), "dv1", "diff", DIFF_FIRST, ("o0a", "o0b"), True, "pa0", "xq0")
            cross(0)
            mlp(0, "cqkv")

            handover("a1")
            stream_group("cqkv", side_operand("a1"), done=PREFILL)

            def side_latent():
                evacuate("cqkv", rows[:, 1, 0:1024])
                yield
            stream_group("kpe", side_latent())

            def rotate(source, to, t, heads, done):
                c = cos[:, t:t + 1, :].to_broadcast([P, heads, 32])
                s = sin[:, t:t + 1, :].to_broadcast([P, heads, 32])
                t1, t2 = source[:, :, 0:32], source[:, :, 32:64]
                a = logit[:, 0, 0:32 * heads].rearrange("p (h r) -> p h r", h=heads)
                b = logit[:, 1, 0:32 * heads].rearrange("p (h r) -> p h r", h=heads)
                nc.vector.tensor_tensor(a, t1, c, ALU.mult)
                link(nc.vector.tensor_tensor(b, t2, s, ALU.mult))
                link(nc.vector.tensor_tensor(to[:, :, 0:32], a, b, ALU.subtract))
                nc.vector.tensor_tensor(a, t2, c, ALU.mult)
                link(nc.vector.tensor_tensor(b, t1, s, ALU.mult))
                done(nc.vector.tensor_tensor(to[:, :, 32:64], a, b, ALU.add))

            def side_low_rank():
                evacuate_narrow("kpe", MLA_ROPE)
                yield
                dve.wait_ge(turn_done, TURNS["kpe_rows"] + 1)
                for t in range(HALVES):
                    ins = nc.vector.tensor_scalar(rows[:, t, 1024:1088], PS[:, side_of("mq") + 1, t * MLA_ROPE:(t + 1) * MLA_ROPE],
                                                  rstd_pre[:, t:t + 1], None, ALU.mult)
                ins.then_inc(turned_dve, 1)
                dve.wait_ge(turned_dve, TURNED_DVE["kpe_rows"] + 1)
                for t in range(HALVES):
                    source = rows[:, t, 1024:1088].rearrange("p (h r) -> p h r", h=1)
                    to = rows[:, t, 1088:1152].rearrange("p (h r) -> p h r", h=1)
                    rotate(source, to, t, 1, link)
                    ins = nc.vector.tensor_copy(rows[:, t, 1152:1216], rows[:, t, 1088:1152])
                ins.then_inc(rope_ready, 1)
                yield
                for c in range(2):
                    ins = squares(v_b[:, c, 512:1024], rows[:, 1, 512 * c:512 * c + 512], sumsq_c[:, 2 + c:3 + c])
                link(ins)
                row_rstd("c1", 4, 512, sumsq_c[:, :], rstd_c[:, :])
                yield
                dve.wait_ge(turn_done, TURNS["kpe"] + 1)
                nc.vector.tensor_copy(kpeT[:, :], PS[:, side_of("mq"), 0:SEQ]).then_inc(turned_dve, 1)
                yield
                yield
                for pair in range(4):
                    rests("c1", pair, side_of("mq") + pair, c_hi, c_lo, GAIN_COL["q"])
                    yield
            stream_group("mq", side_low_rank())
            stream_group("uq0", side_turn("mq", qT_b, "uq0"))

            def side_query(name, first):
                evacuate(name, rows[:, 1, first:first + 768], rstd_c[:, 2:3])
                yield
            stream_group("uq1", side_query("uq0", 0))
            stream_group("ukv0", side_query("uq1", 768))

            def side_key_value(name, turn, n, follow):
                g = PLAN[name]
                finished(dve, name)
                if n:
                    dve.wait_ge(turn_done, TURNS["kn0"] + 2)
                for w, to in ((0, rows[:, 1, 1536:2048]), (1, v_a[:, 1, 512 * n:512 * n + 512])):
                    ins = nc.vector.tensor_scalar(to.rearrange("p (c h d) -> p c h d", c=2, h=2),
                                                  sums(g["index"], 1, 1024).rearrange("p c (h w d) -> p c h w d", h=2, w=2)[:, :, :, w, :],
                                                  rstd_c[:, 3:4], None, ALU.mult)
                ins.then_inc(evac_dve, 1)
                yield
                yield
                turned(turn, kT_a[:, 4 * n:4 * n + 4, :], side_of(follow))
                yield
            stream_group("ukv1", side_key_value("ukv0", "kn0", 0, "ukv1"))

            def side_queries():
                evacuated(dve, "uq1")
                for t in range(HALVES):
                    source = rows[:, t, 0:8 * MLA_QK].rearrange("p (h w) -> p h w", w=MLA_QK)[:, :, HD:MLA_QK]
                    to = prob[:, t, :].rearrange("p (h r) -> p h r", h=8)
                    rotate(source, to, t, 8, lambda ins: ins.then_inc(rope_ready, 1))
                    dve.wait_ge(rope_ready, 2 + t)
                yield
                turned("qn", qT_a, side_of("mk"))
                yield
                yield
                turned("qpe", qpeT, side_of("mk"))
                yield
            stream_group("mk", chained(side_key_value("ukv1", "kn1", 1, "mk"), side_queries(),
                                       attend(units("mla", 0, MLA_FIRST), side_of("mk"))))
            stream_group("mv", chained(side_turn("mk", kT_b, "mv"), attend(units("mla", MLA_FIRST, 8), side_of("mv"))))
            mixer_out(("cdo0", "cdo1"), "mv", "moba", 0, ("o1a", "o1b"), False, "pa1", "xq1")
            cross(1)
            mlp(1, None)
            update(UPDATES)

        @block.tensor
        def _(pe):
            def products(i, tile, count, group, per, width, chunks, hi, lo, operand=None, first=0, side=iter(())):
                for k in range(count):
                    pe.wait_ge(hi_ready, at(i, Mlp.TILES, tile + k + 1))
                    pe.wait_ge(lo_ready, at(i, Mlp.TILES, tile + k + 1))
                    slot = (tile + k) % RING
                    for j in range(per):
                        ch = first + k * per + j
                        if operand is not None:
                            operand(ch)
                        start, stop = ch == 0, ch == chunks - 1
                        if width < P:
                            wh, wl = (part[:, slot, j * width:(j + 1) * width] for part in (w_hi, w_lo))
                            xh, xl = hi[:, ch, :], lo[:, ch, :]
                            for w_part, x_part, a, z in ((wh, xh, start, False), (wl, xh, False, False), (wh, xl, False, stop)):
                                mm = nc.tensor.matmul(PS[0:width, bank(group, 0, 0), 0:SEQ], w_part, x_part, start=a, stop=z)
                            continue
                        for t in range(HALVES):
                            xh, xl = hi[:, ch, t * P:(t + 1) * P], lo[:, ch, t * P:(t + 1) * P]
                            for x_part, w_part, a, z in ((xh, w_hi, start, False), (xh, w_lo, False, False), (xl, w_hi, False, stop)):
                                for c, (col, w) in enumerate(col_banks(width)):
                                    mm = nc.tensor.matmul(PS[:, bank(group, c, t), 0:w], x_part,
                                                          w_part[:, slot, j * width + col:j * width + col + w], start=a, stop=z)
                    mm.then_inc(tile_used, 1)
                    next(side, None)
                for _ in side:
                    pass

            def stream_group(name, side=iter(()), operand=None, first=0, count=None, hi=x_hi, lo=x_lo):
                g = PLAN[name]
                products(None, g["tile"] + first, count or g["tiles"], g["index"], g["per"], g["width"], g["chunks"],
                         hi, lo, operand, first * g["per"], side)

            def operand_of(name, base=0):
                def operand(ch):
                    if ch % 2 == 0 and ch >= base:
                        split(pe, name, (ch - base) // 2 + 1)
                return operand

            def turn_bank(b, source, chunks):
                for j in chunks:
                    for t in range(HALVES):
                        mm = nc.tensor.transpose(PS[:, b, (j % 2) * SEQ + t * P:(j % 2) * SEQ + (t + 1) * P], source(j, t), ident)
                return mm

            def turn_narrow(width, b):
                for t in range(HALVES):
                    mm = nc.tensor.transpose(PS[:, b, t * width:(t + 1) * width], narrow[0:width, t * P:(t + 1) * P], ident[0:width, 0:width])
                mm.then_inc(turn_done, 1)

            def turn(name, source, side):
                for b in range(dict(TURN_BANKS)[name]):
                    turn_bank(side + b, source, (2 * b, 2 * b + 1)).then_inc(turn_done, 1)

            def row_chunk(first, step=P):
                return lambda j, t: rows[:, t, first + j * step:first + j * step + P]

            def turn_pair(name, pair, source):
                turn_bank(operand_bank(name, pair), source, (2 * pair, 2 * pair + 1)).then_inc(xturn_done, 1)

            def resid_chunk(j, t):
                return resid[:, t, j * P:(j + 1) * P]

            def updated(name, pair):
                pe.wait_ge(resid_ready, updates_with(2 * P * (pair + 1), BEFORE[name]))

            def keep_warm(b, count, width=512):
                for _ in range(count):
                    nc.tensor.matmul(PS[:, b, 0:width], ident, const[:, 0:width], start=True, stop=True)

            def handover(name):
                keep_warm(4 - operand_bank(name, 0), WARM[BEFORE[name][:2]])
                for pair in range(2):
                    updated(name, pair)
                    turn_pair(name, pair, resid_chunk)
                keep_warm(4 - operand_bank(name, 0), 5, P)

            def side_operand(name):
                for pair in range(2, 8):
                    updated(name, pair)
                    if pair >= 4:
                        split(pe, name, pair - 3)
                    turn_pair(name, pair, resid_chunk)
                    if pair % 2:
                        yield

            def attend(us, side):
                for s in range(len(us) + 2):
                    if s < len(us):
                        a = us[s]
                        if a.u >= 2:
                            pe.wait_ge(p_ready, a.u - 1)
                        for t, col, keys in a.parts:
                            S = PS[:, side + a.u % 2, col:col + keys]
                            mla = a.family == "mla"
                            mm = nc.tensor.matmul(S, a.q[:, t * P:(t + 1) * P], a.k[:, 0:keys], start=True, stop=not mla)
                            if mla:
                                mm = nc.tensor.matmul(S, a.qpe[:, t * P:(t + 1) * P], a.kpe[:, 0:keys], start=False, stop=True)
                        mm.then_inc(s_done, 1)
                    if 1 <= s <= len(us):
                        a = us[s - 1]
                        pe.wait_ge(p_ready, a.u + 1)
                        if a.u:
                            pe.wait_ge(pt_ready, a.u)
                        for col in range(0, a.cols, P):
                            mm = nc.tensor.transpose(PS[:, side + 2, col:col + P], logit[:, a.u % 2, col:col + P], ident)
                        mm.then_inc(pt_done, 1)
                    if s >= 2:
                        a = us[s - 2]
                        pe.wait_ge(pt_ready, a.u + 1)
                        if a.u:
                            pe.wait_ge(o_ready, a.u)
                        for t, col, keys in a.parts:
                            for n in range(keys // P):
                                mm = nc.tensor.matmul(PS[:, side + 3, t * a.dv:(t + 1) * a.dv],
                                                      prob[:, a.u % 2, col + n * P:col + (n + 1) * P], a.v[:, n, :],
                                                      start=n == 0, stop=n == keys // P - 1)
                        mm.then_inc(o_done, 1)
                    yield

            def side_turn(name, follow):
                yield
                evacuated(pe, name)
                turn(name, row_chunk(1024), side_of(follow))
                yield
                yield

            def mixer_out(names, last_proj, family, attended, o_names, sub):
                first, second = names
                side = side_of(first)
                evacuated(pe, last_proj)
                pe.wait_ge(o_ready, UNITS[family] + attended)
                for c in range(0, 8, 2):
                    turn_bank(side + c // 2, row_chunk(0), (c, c + 1)).then_inc(xturn_done, 1)

                def attend_after_split():
                    split(pe, o_names[0], 4)
                    yield from attend(units(family, attended), side)
                stream_group(first, attend_after_split(), operand_of(o_names[0]), 0, 8)
                if sub:
                    keep_warm(side, WARM["sub"])
                else:
                    pe.wait_ge(o_ready, UNITS[family] + 8)
                for c in range(0, 8, 2):
                    if sub:
                        pe.wait_ge(sub_scaled, c // 2 + 1)
                    turn_bank(side + c // 2, row_chunk(1024), (c, c + 1)).then_inc(xturn_done, 1)
                stream_group(first, operand=operand_of(o_names[1], 8), first=8, count=8)
                stream_group(second)

            def cross(l):
                evacuated(pe, "abo0" if l == 0 else "cdo0")
                handover(f"x{l}")
                stream_group(f"xq{l}", side_operand(f"x{l}"), operand_of(f"x{l}"))
                side = side_of(f"xo{l}0")
                keep_warm(side + 3, 4)
                evacuated(pe, f"xq{l}")
                turn(f"xq{l}", row_chunk(1024), side_of(f"xq{l}"))
                turns_evacuated(pe, f"xq{l}")
                attention = attend(units(f"x{l}", 0, 4), side)
                for _ in range(5):
                    next(attention)
                pe.wait_ge(o_ready, UNITS[f"x{l}"] + 2)
                turn_bank(side_of(f"xq{l}"), row_chunk(0), (0, 1)).then_inc(xturn_done, 1)
                for _ in attention:
                    pass

                def last_heads():
                    pe.wait_ge(o_ready, UNITS[f"x{l}"] + 4)
                    turn_bank(side, row_chunk(0), (2, 3)).then_inc(xturn_done, 1)
                    yield
                stream_group(f"xo{l}0", last_heads(), operand_of(f"xo{l}"))
                stream_group(f"xo{l}1")

            def mlp(l):
                m = Mlp(l)

                def hidden(i, b):
                    yield
                    pe.wait_ge(evac_act, at(i, Mlp.ACT, m.a + b + 1))
                    pe.wait_ge(evac_dve, at(i, Mlp.DVE, m.hid_dve(b) + 1))
                    for n in range(4):
                        turn_bank(bank(m.up(b)[0], 0, 0) + n, row_chunk(0), (2 * n, 2 * n + 1)).then_inc(xturn_done, 1)
                    yield

                def up(i, b, side=iter(()), operand=None):
                    g, tile = m.up(b)
                    products(i, tile, 16, g, 1, 1024, CH, x_hi, x_lo, operand, 0, side)

                def down(i, b, half, side=iter(())):
                    g, tile = m.down(b, half)
                    products(i, tile, 8, g, 1, 1024, 8, h_hi[b % 2], h_lo[b % 2], None, 0, side)

                def sums_free(i, b, half):
                    pe.wait_ge(evac_dve, at(i, Mlp.DVE, m.y_dve(b, half) + 2))

                def hidden_split(i, b):
                    pe.wait_ge(split_hi, at(i, Mlp.SPLITS, m.s + 4 * b + 4))
                    pe.wait_ge(split_lo, at(i, Mlp.SPLITS, m.s + 4 * b + 4))

                evacuated(pe, f"xo{l}0")
                handover(f"f{l}")
                up(None, 0, side_operand(f"f{l}"), operand_of(f"f{l}"))
                up(None, 1, hidden(None, 0))
                hidden_split(None, 0)
                down(None, 0, 0, hidden(None, 1))
                hidden_split(None, 1)
                down(None, 0, 1)
                with pe.Fori(0, (BLOCKS - 2) // 2) as i:
                    for b in (1, 2):
                        sums_free(i, b - 1, 0)
                        up(i, b + 1)
                        sums_free(i, b - 1, 1)
                        down(i, b, 0, hidden(i, b + 1))
                        hidden_split(i, b + 1)
                        down(i, b, 1)
                sums_free(None, BLOCKS - 2, 0)
                down(None, BLOCKS - 1, 0)
                sums_free(None, BLOCKS - 2, 1)
                down(None, BLOCKS - 1, 1)

            pe.wait_ge(ident_loaded, 16)
            pe.wait_ge(gain_rows_loaded, 16 * GAIN_LOADS)
            nc.tensor.transpose(PS[:, 0, 0:120], gain_rows[:, :], ident[0:120, 0:120]).then_inc(turn_done, 1)

            def mem_pair(pair):
                pe.wait_ge(mem_loaded[pair // 2], 16)
                turn_pair("mem", pair, row_chunk(0))

            for pair in range(2):
                mem_pair(pair)

            def side_first():
                for pair in range(2, 8):
                    if pair >= 4:
                        split(pe, "mem", pair - 3)
                    mem_pair(pair)
                    if pair % 2:
                        yield
                yield
                yield
                for pair in range(8):
                    if pair % 2 == 0:
                        pe.wait_ge(x_loaded[pair // 2], 16)
                    if pair < 4:
                        split(pe, "mem", pair + 5)
                    else:
                        split(pe, "a0", pair - 3)
                    turn_pair("mem", pair, resid_chunk)
                    yield
            pe.wait_ge(turned_dve, TURNED_DVE["gain"] + 1)
            keep_warm(0, 10, P)
            stream_group("mem", side_first(), operand_of("mem"))

            split(pe, "a0", 7)
            keep_warm(operand_bank("mem", 4), 8, P)
            split(pe, "a0", 8)
            pe.wait_ge(const_loaded, 16)

            def side_memory():
                yield
                evacuated(pe, "mem")
                turn("mem_k", lambda j, t: qT_b[:, 2 * t:2 * t + 2, :].rearrange("p h s -> p (h s)")[:, j * P:(j + 1) * P], side_of("fv"))
                yield
                yield
            stream_group("fv", side_memory())
            turns_evacuated(pe, "mem_k")
            stream_group("fg")
            evacuated(pe, "fv")

            def side_gate():
                side = side_of("fq")
                evacuated(pe, "fg")
                turn_narrow(8, side + 1)
                yield
                yield
                pe.wait_ge(gate_dve, 2)
                nc.tensor.matmul(PS[:, side + 2, 0:8], tri, gate_l[:, 0, :], start=True, stop=True)
                nc.tensor.matmul(PS[:, side + 2, 8:16], ones, gate_l[:, 0, :], start=True, stop=False)
                nc.tensor.matmul(PS[:, side + 2, 8:16], tri, gate_l[:, 1, :], start=False, stop=True).then_inc(gate_pe, 1)
                yield
                pe.wait_ge(gate_dve, 3)
                for t in range(HALVES):
                    mm = nc.tensor.transpose(PS[0:8, side + 3, t * P:(t + 1) * P], cum[:, t, :], ident)
                mm.then_inc(turn_done, 1)
                yield
                turns_evacuated(pe, "cum")
                for h in range(8):
                    mm = nc.tensor.matmul(PS[:, side + h // 2, (h % 2) * SEQ:(h % 2 + 1) * SEQ],
                                          ident[0:8, h:h + 1].to_broadcast([8, P]), cumT, start=True, stop=True)
                mm.then_inc(gate_pe, 1)
                yield
            stream_group("fq", side_gate())
            pe.wait_ge(key_cum_act, 1)
            pe.wait_ge(gate_dve, 4)
            stream_group("fk", side_turn("fq", "fk"))
            turns_evacuated(pe, "fq")
            stream_group("dq", side_turn("fk", "dq"))
            turns_evacuated(pe, "fk")
            stream_group("dk", chained(side_turn("dq", "dk"), wait_then(lambda: turns_evacuated(pe, "dq"),
                                                                          attend(units("fox", 0, FOX_FIRST), side_of("dk")))))
            pe.wait_ge(o_ready, UNITS["fox"] + FOX_FIRST)
            stream_group("dv0", chained(side_turn("dk", "dv0"), wait_then(lambda: turns_evacuated(pe, "dk"),
                                                                            attend(units("fox", FOX_FIRST, 8), side_of("dv0")))))
            pe.wait_ge(o_ready, UNITS["fox"] + 8)

            def side_value():
                yield
                evacuated(pe, "dv0")
            stream_group("dv1", chained(side_value(), attend(units("diff", 0, DIFF_FIRST), side_of("dv1"))))
            mixer_out(("abo0", "abo1"), "dv1", "diff", DIFF_FIRST, ("o0a", "o0b"), True)
            cross(0)
            mlp(0)

            pe.wait_ge(evac_dve, Mlp(0).y_dve(BLOCKS - 1, 0) + 2)
            handover("a1")
            stream_group("cqkv", side_operand("a1"), operand_of("a1"))
            pe.wait_ge(evac_dve, Mlp(0).y_dve(BLOCKS - 1, 1) + 2)
            stream_group("kpe")
            evacuated(pe, "cqkv")

            def side_low_rank():
                evacuated(pe, "kpe")
                turn_narrow(MLA_ROPE, side_of("mq") + 1)
                yield
                yield
                pe.wait_ge(rope_ready, 1)
                for t in range(HALVES):
                    mm = nc.tensor.transpose(PS[:, side_of("mq"), t * P:(t + 1) * P], rows[:, t, 1088:1216], ident)
                mm.then_inc(turn_done, 1)
                yield
                yield
                turns_evacuated(pe, "kpe")
                for c in range(0, 8, 2):
                    turn_bank(side_of("mq") + c // 2, row_chunk(0), (c, c + 1)).then_inc(xturn_done, 1)
                yield
            stream_group("mq", side_low_rank())
            split(pe, "c1", 4)
            stream_group("uq0", side_turn("mq", "uq0"), hi=c_hi, lo=c_lo)
            turns_evacuated(pe, "mq")
            stream_group("uq1", hi=c_hi, lo=c_lo)
            evacuated(pe, "uq0")
            stream_group("ukv0", hi=c_hi[:, 4:8, :], lo=c_lo[:, 4:8, :])
            evacuated(pe, "uq1")

            def side_key(name, turn_name, follow):
                yield
                evacuated(pe, name)
                turn(turn_name, row_chunk(1536), side_of(follow))
                yield
                yield
            stream_group("ukv1", side_key("ukv0", "kn0", "ukv1"), hi=c_hi[:, 4:8, :], lo=c_lo[:, 4:8, :])
            turns_evacuated(pe, "kn0")

            def side_queries():
                turns_evacuated(pe, "kn1")
                turn("qn", row_chunk(0, MLA_QK), side_of("mk"))
                yield
                yield
                turns_evacuated(pe, "qn")
                pe.wait_ge(rope_ready, 3)
                turn("qpe", lambda j, t: prob[:, t, j * P:(j + 1) * P], side_of("mk"))
                yield
                yield
            stream_group("mk", chained(side_key("ukv1", "kn1", "mk"), side_queries(),
                                       wait_then(lambda: turns_evacuated(pe, "qpe"),
                                                 attend(units("mla", 0, MLA_FIRST), side_of("mk")))))
            pe.wait_ge(o_ready, UNITS["mla"] + MLA_FIRST)
            stream_group("mv", chained(side_turn("mk", "mv"), wait_then(lambda: turns_evacuated(pe, "mk"),
                                                                          attend(units("mla", MLA_FIRST, 8), side_of("mv")))))
            mixer_out(("cdo0", "cdo1"), "mv", "moba", 0, ("o1a", "o1b"), False)
            cross(1)
            mlp(1)


def shape_constants():
    c = np.zeros((P, C_END), np.float32)
    row, col = np.arange(P)[:, None], np.arange(P)[None, :]
    c[:, C_ID:C_TRI] = row == col
    c[:, C_TRI:C_ONE] = row <= col
    c[:, C_ONE:C_DIST] = 1.0
    q = np.concatenate([np.broadcast_to(row, (P, P)), np.broadcast_to(row + P, (P, 2 * P))], 1)
    k = np.concatenate([np.arange(P), np.arange(2 * P)])[None, :]
    c[:, C_DIST:C_MASK] = np.where(k <= q, k - q, MASKED)
    c[:, C_MASK:C_COS] = np.where(k <= q, 0.0, MASKED)
    inv = np.float32(10000.0) ** (-np.arange(0, MLA_ROPE, 2, dtype=np.float32) / np.float32(MLA_ROPE))
    angle = np.arange(SEQ, dtype=np.float32)[:, None] * inv[None, :]
    for at0, f in ((C_COS, np.cos), (C_SIN, np.sin)):
        c[:, at0:at0 + 64] = f(angle).astype(np.float32).reshape(HALVES, P, 32).transpose(1, 0, 2).reshape(P, 64)
    return c


_INS = ["x", "mem", "mem_norm", "mem_wkv", "norms", "xattn_wq", "xattn_wo", "ffn_w1", "ffn_w2", "ab_w_in", "ab_w_out",
        "fox_b_f", "diff_lambda", "diff_subln", "cd_w_in", "cd_w_out", "mla_q_norm", "mla_kv_norm", "mla_w_uq", "mla_w_ukv"]


def kernel(**inputs):
    import concourse.bacc as _bacc
    from concourse import mybir as _mybir
    from concourse.bass_utils import run_bass_kernel_spmd as _run

    nc = _bacc.Bacc("TRN2", target_bir_lowering=False, num_devices=1)
    arrays, args = {}, []
    for name in _INS + ["consts"]:
        a = np.ascontiguousarray(inputs[name]) if name != "consts" else shape_constants()
        arrays[f"in_{name}_dram"] = a
        args.append(nc.dram_tensor(f"in_{name}_dram", a.shape, _mybir.dt.from_np(a.dtype), kind="ExternalInput").ap())
    args.append(nc.dram_tensor("out_0_dram", (1, SEQ, D), F32, kind="ExternalOutput").ap())
    trunk(nc, *args)
    r = _run(nc, [arrays], core_ids=[0])
    return r.results[0]["out_0_dram"]
```
